# Optimizing a Trainium2 kernel written in Bass

```python
import jax, jax.numpy as jnp
from jax import lax
import numpy as np

D_MODEL = 2048
BATCH = 1
SEQ = 256
DEPTH = 1
DEC_BATCH = 1
DEC_SEQ = 64
PAST_LEN = 256

CHUNK = 64
M_HEADS = 8
M_DK = 128
M_DV = 128
F_BIAS = 3.0
A_HEADS = 8
A_KV = 2
A_DH = 128
I_HEADS = 8
I_DH = 64
TOPK_MAX = 256
Q_BLOCK = 128
N_MEM = 256
C_HEADS = 4
C_DH = 256
N_BRANCH = 3
BRANCH_W = 1024
D_FF = 5632
CONV_W = 3
ROPE_THETA = 500000.0
ROPE_FRAC = 4
EPS = 1e-6
NEG = -1e30

IN_SPLITS = (M_HEADS * M_DK, M_HEADS * M_DK, M_HEADS * M_DV, M_HEADS * M_DV, M_HEADS, M_HEADS,
             A_HEADS * A_DH, A_KV * A_DH, A_KV * A_DH, I_HEADS * I_DH, I_DH, I_HEADS,
             C_HEADS * C_DH, N_BRANCH * D_MODEL)
IN_WIDTH = sum(IN_SPLITS)

kernel_name = "hybrid_mlstm_dsa_memxattn_convffn_step"

def rmsnorm(x, g):
    x32 = x.astype(jnp.float32)
    y = x32 * lax.rsqrt(jnp.mean(x32 * x32, axis=-1, keepdims=True) + EPS)
    return (y * g.astype(jnp.float32)).astype(x.dtype)

def partial_rope(x, pos):
    d = x.shape[-1]
    r = d // ROPE_FRAC
    half = r // 2
    inv = ROPE_THETA ** (-jnp.arange(half, dtype=jnp.float32) * 2.0 / r)
    ang = pos.astype(jnp.float32)[:, None] * inv[None, :]
    cos = jnp.cos(ang)[None, :, None, :]
    sin = jnp.sin(ang)[None, :, None, :]
    x32 = x.astype(jnp.float32)
    x1 = x32[..., :half]
    x2 = x32[..., half:r]
    out = jnp.concatenate([x1 * cos - x2 * sin, x2 * cos + x1 * sin, x32[..., r:]], axis=-1)
    return out.astype(x.dtype)

def split_in(p):
    outs = []
    off = 0
    for w in IN_SPLITS:
        outs.append(p[..., off:off + w])
        off += w
    return outs

def mlstm_chunk(carry, xs):
    C, n, m = carry
    q, k, v, ig, lf = xs
    L = q.shape[1]
    b = jnp.cumsum(lf, axis=1).transpose(0, 2, 1)
    igT = ig.transpose(0, 2, 1)
    causal = jnp.tril(jnp.ones((L, L), dtype=bool))
    logD = jnp.where(causal, b[..., :, None] - b[..., None, :] + igT[..., None, :], -jnp.inf)
    m_inter = b + m[..., None]
    m_t = jnp.maximum(m_inter, jnp.max(logD, axis=-1))
    D = jnp.exp(logD - m_t[..., None])
    inter = jnp.exp(m_inter - m_t)
    S = jnp.einsum('bthd,bshd->bhts', q, k) * D
    num = (jnp.einsum('bhts,bshv->bthv', S, v)
           + jnp.einsum('bhvd,bthd->bthv', C, q) * inter.transpose(0, 2, 1)[..., None])
    den = jnp.sum(S, axis=-1) + inter * jnp.einsum('bhd,bthd->bht', n, q)
    h = num / jnp.maximum(jnp.abs(den), jnp.exp(-m_t)).transpose(0, 2, 1)[..., None]
    m_new = m_t[..., -1]
    w_s = jnp.exp(b[..., -1:] - b + igT - m_new[..., None])
    decay = jnp.exp(b[..., -1] + m - m_new)
    C_new = decay[..., None, None] * C + jnp.einsum('bhs,bshv,bshd->bhvd', w_s, v, k)
    n_new = decay[..., None] * n + jnp.einsum('bhs,bshd->bhd', w_s, k)
    return (C_new, n_new, m_new), h

def mlstm_scan(q, k, v, ig, lf, state):
    B, T = q.shape[:2]
    L = min(T, CHUNK)
    nc = T // L

    def to_chunks(a):
        return jnp.moveaxis(a.reshape((B, nc, L) + a.shape[2:]), 1, 0)

    state, h = lax.scan(mlstm_chunk, state, (to_chunks(q), to_chunks(k), to_chunks(v),
                                              to_chunks(ig), to_chunks(lf)))
    h = jnp.moveaxis(h, 0, 1).reshape(B, T, M_HEADS * M_DV)
    return h, state

def dsa_block(q, qi, wi, qpos, k_all, v_all, ki_all, topk):
    f32 = jnp.float32
    B, Q = q.shape[:2]
    S = k_all.shape[1]
    chunk_end = (qpos // CHUNK + 1) * CHUNK
    admissible = jnp.arange(S)[None, :] < chunk_end[:, None]
    logits = jnp.einsum('bqhd,bsd->bqhs', qi.astype(f32), ki_all.astype(f32)) * (I_DH ** -0.5)
    score = jnp.einsum('bqhs,bqh->bqs', jax.nn.relu(logits), wi.astype(f32)) * (I_HEADS ** -0.5)
    score = jnp.where(admissible[None], score, NEG)
    _, idx = lax.top_k(score, topk)
    valid = idx < chunk_end[None, :, None]
    gather = jax.vmap(lambda a, i: a[i])
    k_sel = gather(k_all, idx)
    v_sel = gather(v_all, idx)
    qg = q.reshape(B, Q, A_KV, A_HEADS // A_KV, A_DH)
    s = jnp.einsum('bqjgd,bqnjd->bqjgn', qg, k_sel).astype(f32) * (A_DH ** -0.5)
    s = jnp.where(valid[:, :, None, None, :], s, NEG)
    p = jax.nn.softmax(s, axis=-1).astype(v_sel.dtype)
    o = jnp.einsum('bqjgn,bqnjd->bqjgd', p, v_sel)
    return o.reshape(B, Q, A_HEADS * A_DH)

def dsa_attention(q, qi, wi, pos, k_all, v_all, ki_all, topk):
    B, T = q.shape[:2]
    qb = min(T, Q_BLOCK)
    nb = T // qb

    def blocks(a):
        return jnp.moveaxis(a.reshape((B, nb, qb) + a.shape[2:]), 1, 0)

    def one(args):
        bq, bqi, bwi, bpos = args
        return dsa_block(bq, bqi, bwi, bpos, k_all, v_all, ki_all, topk)

    out = lax.map(one, (blocks(q), blocks(qi), blocks(wi), pos.reshape(nb, qb)))
    return jnp.moveaxis(out, 0, 1).reshape(B, T, A_HEADS * A_DH)

def mem_attend(cq, mem_k, mem_v):
    B, T = cq.shape[:2]
    s = jnp.einsum('bthd,bmhd->bhtm', cq, mem_k).astype(jnp.float32) * (C_DH ** -0.5)
    p = jax.nn.softmax(s, axis=-1).astype(mem_v.dtype)
    return jnp.einsum('bhtm,bmhd->bthd', p, mem_v).reshape(B, T, C_HEADS * C_DH)

def mixer(x, pos, past, mstate, mem_k, mem_v, topk, g_mix, w_in, b_ig, b_fg, w_branch, w_out):
    f32 = jnp.float32
    B, T, _ = x.shape
    xn = rmsnorm(x, g_mix)
    (mq, mk, mv, mo, mi, mf, aq, ak, av, iq, ik, iw, cq, gt) = split_in(xn @ w_in)
    q = mq.reshape(B, T, M_HEADS, M_DK).astype(f32)
    k = mk.reshape(B, T, M_HEADS, M_DK).astype(f32) * (M_DK ** -0.5)
    v = mv.reshape(B, T, M_HEADS, M_DV).astype(f32)
    ig = mi.astype(f32) + b_ig.astype(f32)
    lf = jax.nn.log_sigmoid(mf.astype(f32) + b_fg.astype(f32))
    h, new_mstate = mlstm_scan(q, k, v, ig, lf, mstate)
    branch_a = (h * jax.nn.sigmoid(mo.astype(f32))).astype(x.dtype)
    qa = partial_rope(aq.reshape(B, T, A_HEADS, A_DH), pos)
    k_new = partial_rope(ak.reshape(B, T, A_KV, A_DH), pos)
    v_new = av.reshape(B, T, A_KV, A_DH)
    qi = partial_rope(iq.reshape(B, T, I_HEADS, I_DH), pos)
    ki_new = partial_rope(ik.reshape(B, T, 1, I_DH), pos)[:, :, 0]
    if past is None:
        k_all, v_all, ki_all = k_new, v_new, ki_new
    else:
        pk, pv, pki = past
        k_all = jnp.concatenate([pk, k_new.astype(pk.dtype)], axis=1)
        v_all = jnp.concatenate([pv, v_new.astype(pv.dtype)], axis=1)
        ki_all = jnp.concatenate([pki, ki_new.astype(pki.dtype)], axis=1)
    branch_b = dsa_attention(qa, qi, iw, pos, k_all, v_all, ki_all, topk).astype(x.dtype)
    branch_c = mem_attend(cq.reshape(B, T, C_HEADS, C_DH), mem_k, mem_v).astype(x.dtype)
    branches = jnp.stack([branch_a, branch_b, branch_c], axis=2)
    proj = jnp.einsum('btnc,ncd->btnd', branches, w_branch)
    gates = jax.nn.sigmoid(gt.reshape(B, T, N_BRANCH, D_MODEL))
    merged = jnp.sum(gates * proj, axis=2)
    return merged @ w_out, (k_new, v_new, ki_new), new_mstate

def conv_ffn(x, conv_prev, g_ffn, w_up, conv_w, conv_b, w_down):
    T = x.shape[1]
    u = rmsnorm(x, g_ffn) @ w_up
    ext = jnp.concatenate([conv_prev.astype(u.dtype), u], axis=1)
    c = conv_b + ext[:, 0:T] * conv_w[0]
    for j in range(1, CONV_W):
        c = c + ext[:, j:j + T] * conv_w[j]
    gate, val = jnp.split(c, 2, axis=-1)
    y = (jax.nn.silu(gate) * val) @ w_down
    return y, ext[:, -(CONV_W - 1):]

def setup_inputs(seed: int = 0) -> dict:
    key = jax.random.key(seed)
    ks = jax.random.split(key, 28)
    f32 = jnp.float32

    def nrm(k, shape, scale=1.0):
        return jax.random.normal(k, shape, f32) * scale

    F2 = 2 * D_FF
    return {
        "x_prompt": nrm(ks[0], (BATCH, SEQ, D_MODEL)),
        "x_sample": nrm(ks[1], (DEC_BATCH, DEC_SEQ, D_MODEL)),
        "mem_prompt": nrm(ks[2], (BATCH, N_MEM, D_MODEL)),
        "cache_dsa_k": nrm(ks[3], (DEPTH, DEC_BATCH, PAST_LEN, A_KV, A_DH)),
        "cache_dsa_v": nrm(ks[4], (DEPTH, DEC_BATCH, PAST_LEN, A_KV, A_DH)),
        "cache_dsa_kidx": nrm(ks[5], (DEPTH, DEC_BATCH, PAST_LEN, I_DH)),
        "state_mlstm_C": nrm(ks[6], (DEPTH, DEC_BATCH, M_HEADS, M_DV, M_DK), M_DK ** -0.5),
        "state_mlstm_n": nrm(ks[7], (DEPTH, DEC_BATCH, M_HEADS, M_DK), M_DK ** -0.5),
        "state_mlstm_m": nrm(ks[8], (DEPTH, DEC_BATCH, M_HEADS)),
        "state_ffn_conv": nrm(ks[9], (DEPTH, DEC_BATCH, CONV_W - 1, F2)),
        "cache_mem_k": nrm(ks[10], (DEPTH, DEC_BATCH, N_MEM, C_HEADS, C_DH)),
        "cache_mem_v": nrm(ks[11], (DEPTH, DEC_BATCH, N_MEM, C_HEADS, C_DH)),
        "g_mix": 1.0 + nrm(ks[12], (DEPTH, D_MODEL), 0.05),
        "w_in": nrm(ks[13], (DEPTH, D_MODEL, IN_WIDTH), D_MODEL ** -0.5),
        "b_igate": nrm(ks[14], (DEPTH, M_HEADS), 0.1),
        "b_fgate": F_BIAS + nrm(ks[15], (DEPTH, M_HEADS), 0.5),
        "w_branch": nrm(ks[16], (DEPTH, N_BRANCH, BRANCH_W, D_MODEL), BRANCH_W ** -0.5),
        "w_out": nrm(ks[17], (DEPTH, D_MODEL, D_MODEL), D_MODEL ** -0.5),
        "g_mem": 1.0 + nrm(ks[18], (DEPTH, D_MODEL), 0.05),
        "w_mem_kv": nrm(ks[19], (DEPTH, D_MODEL, 2 * C_HEADS * C_DH), D_MODEL ** -0.5),
        "g_ffn": 1.0 + nrm(ks[20], (DEPTH, D_MODEL), 0.05),
        "w_up": nrm(ks[21], (DEPTH, D_MODEL, F2), D_MODEL ** -0.5),
        "conv_w": nrm(ks[22], (DEPTH, CONV_W, F2), CONV_W ** -0.5),
        "conv_b": nrm(ks[23], (DEPTH, F2), 0.02),
        "w_down": nrm(ks[24], (DEPTH, D_FF, D_MODEL), D_FF ** -0.5),
        "g_final": 1.0 + nrm(ks[25], (D_MODEL,), 0.05),
    }

def reference(x_prompt, x_sample, mem_prompt, cache_dsa_k, cache_dsa_v, cache_dsa_kidx,
              state_mlstm_C, state_mlstm_n, state_mlstm_m, state_ffn_conv, cache_mem_k, cache_mem_v,
              g_mix, w_in, b_igate, b_fgate, w_branch, w_out, g_mem, w_mem_kv, g_ffn, w_up,
              conv_w, conv_b, w_down, g_final):
    f32 = jnp.float32
    B, T = x_prompt.shape[:2]
    DB, DT = x_sample.shape[:2]
    P = cache_dsa_k.shape[2]
    pos_p = jnp.arange(T, dtype=jnp.int32)
    pos_s = P + jnp.arange(DT, dtype=jnp.int32)
    topk_p = min(TOPK_MAX, T // 4)
    topk_s = min(TOPK_MAX, (P + DT) // 4)
    xp, xs = x_prompt, x_sample
    pk, pv, pki, pC, pn, pm, pconv, pmk, pmv = [], [], [], [], [], [], [], [], []
    sk, sv, ski, sC, sn, sm, sconv = [], [], [], [], [], [], []
    for l in range(DEPTH):
        lw = (g_mix[l], w_in[l], b_igate[l], b_fgate[l], w_branch[l], w_out[l])
        mkv = rmsnorm(mem_prompt, g_mem[l]) @ w_mem_kv[l]
        mk_p = mkv[..., :C_HEADS * C_DH].reshape(B, N_MEM, C_HEADS, C_DH)
        mv_p = mkv[..., C_HEADS * C_DH:].reshape(B, N_MEM, C_HEADS, C_DH)
        zero_state = (jnp.zeros((B, M_HEADS, M_DV, M_DK), f32), jnp.zeros((B, M_HEADS, M_DK), f32),
                      jnp.zeros((B, M_HEADS), f32))
        a, (k_p, v_p, ki_p), (C_p, n_p, m_p) = mixer(xp, pos_p, None, zero_state, mk_p, mv_p, topk_p, *lw)
        xp = xp + a
        zero_conv = jnp.zeros((B, CONV_W - 1, 2 * D_FF), xp.dtype)
        f, conv_p = conv_ffn(xp, zero_conv, g_ffn[l], w_up[l], conv_w[l], conv_b[l], w_down[l])
        xp = xp + f
        pk.append(k_p); pv.append(v_p); pki.append(ki_p)
        pC.append(C_p.astype(x_prompt.dtype)); pn.append(n_p.astype(x_prompt.dtype)); pm.append(m_p.astype(x_prompt.dtype))
        pconv.append(conv_p); pmk.append(mk_p); pmv.append(mv_p)
        mstate = (state_mlstm_C[l].astype(f32), state_mlstm_n[l].astype(f32), state_mlstm_m[l].astype(f32))
        past = (cache_dsa_k[l], cache_dsa_v[l], cache_dsa_kidx[l])
        a, (k_s, v_s, ki_s), (C_s, n_s, m_s) = mixer(xs, pos_s, past, mstate, cache_mem_k[l], cache_mem_v[l], topk_s, *lw)
        xs = xs + a
        f, conv_s = conv_ffn(xs, state_ffn_conv[l], g_ffn[l], w_up[l], conv_w[l], conv_b[l], w_down[l])
        xs = xs + f
        sk.append(k_s); sv.append(v_s); ski.append(ki_s)
        sC.append(C_s.astype(x_sample.dtype)); sn.append(n_s.astype(x_sample.dtype)); sm.append(m_s.astype(x_sample.dtype))
        sconv.append(conv_s)
    y_prompt = rmsnorm(xp, g_final)
    y_sample = rmsnorm(xs, g_final)
    return (y_prompt, y_sample,
            jnp.stack(pk), jnp.stack(pv), jnp.stack(pki), jnp.stack(pC), jnp.stack(pn), jnp.stack(pm),
            jnp.stack(pconv), jnp.stack(pmk), jnp.stack(pmv),
            jnp.stack(sk), jnp.stack(sv), jnp.stack(ski), jnp.stack(sC), jnp.stack(sn), jnp.stack(sm),
            jnp.stack(sconv))


_drawn_inputs = setup_inputs


def setup_inputs(seed=0):
    import zlib

    import numpy as np

    out = dict(_drawn_inputs(seed))
    spreads = {}
    factors = {'conv_b': 4.487}
    for name, (base, spread) in spreads.items():
        noise = np.random.default_rng([zlib.crc32(name.encode()), seed]).standard_normal(out[name].shape)
        drawn = base * np.exp(spread * noise) if base else spread * noise
        out[name] = __import__('jax').numpy.asarray(drawn.astype(out[name].dtype))
    for name, factor in factors.items():
        out[name] = (out[name] * factor).astype(out[name].dtype)
    return out
```

```python
from contextlib import ExitStack, contextmanager

import numpy as np

import concourse.bass as bass
from concourse import mybir

F32 = mybir.dt.float32
F32R = mybir.dt.float32r
ACT = mybir.ActivationFunctionType
ALU = mybir.AluOpType
AX = mybir.AxisListType
ds = bass.ds

P = 128
D = 2048
TP, TS = 256, 64
T = TP + TS
PAST = 256
SS = PAST + TS
CH = 64
NCH = T // CH
KT = D // P
MH, AH, IH, CHD = 8, 8, 8, 4
NMEM = 256
FF = 5632
FT = FF // P
GROUPS = 4
GT = FT // GROUPS
EPS = 1e-6
NEG = -1e30
TAKEN = -3e38
TOPK_P, TOPK_S = TP // 4, SS // 4

O_MQ, O_MK, O_MV, O_MO = 0, 1024, 2048, 3072
O_IF = 4096
O_AQ = O_IF + 16
O_AK = O_AQ + 1024
O_AV = O_AK + 256
O_IQ = O_AV + 256
O_IKW = O_IQ + 512
O_CQ = O_IKW + 72
O_G = O_CQ + 1024
WIN = O_G + 3 * D

RING = 4
UK = 8
LEAD = 2

U_C, T_C = 0, 0
U_B, T_B = U_C + CHD * 12, T_C + CHD * 6
U_A, T_A = U_B + 20, T_B + 10
U_Q, T_Q = U_A + MH * 8, T_A + MH * 4
U_G, T_G = U_Q + AH * 2, T_Q + AH
U_O, T_O = U_G + KT * 9, T_G + KT * 6
U_F, T_F = U_O + KT * 2, T_O + KT
UF_G, TF_G = GT * 4 + KT * 2, GT * 2 + KT
UNITS = U_F + GROUPS * UF_G
T_END = T_F + GROUPS * TF_G

C_ID, C_CAUS, C_CUM, C_LAST, C_ONE = 0, 128, 192, 256, 384
C_R128, C_R64, C_DUP, C_RDUP = 512, 640, 768, 896
C_COS128, C_SIN128, C_COS64, C_SIN64 = (1024 + n * T for n in range(4))
C_ADM = 1024 + 4 * T
CW = C_ADM + 2 * TP


def shape_tables():
    c = np.zeros((P, CW), np.float32)
    c[:, C_ID:C_ID + P] = np.eye(P)
    i = np.arange(CH)
    c[:CH, C_CAUS:C_CAUS + CH] = np.where(i[None, :] <= i[:, None], 0.0, NEG)
    c[:CH, C_CUM:C_CUM + CH] = i[:, None] <= i[None, :]
    c[CH - 1, C_LAST:C_LAST + P] = 1.0
    c[:, C_ONE:C_ONE + P] = 1.0

    def rotation(d):
        r = np.zeros((d, d), np.float32)
        half = d // 8
        for m in range(half):
            r[m + half, m] = -1.0
            r[m, m + half] = 1.0
        return r
    c[:, C_R128:C_R128 + P] = rotation(128)
    for o in (0, 64):
        c[o:o + 64, C_R64 + o:C_R64 + o + 64] = rotation(64)
    for o in (0, 64):
        c[:64, C_DUP + o:C_DUP + o + 64] = np.eye(64)
        c[:64, C_RDUP + o:C_RDUP + o + 64] = rotation(64)
    pos = np.arange(T).astype(np.float32)
    for d, oc, os in ((128, C_COS128, C_SIN128), (64, C_COS64, C_SIN64)):
        r, half = d // 4, d // 8
        inv = np.float32(500000.0) ** (-np.arange(half, dtype=np.float32) * np.float32(2.0) / np.float32(r))
        ang = pos[:, None] * inv.astype(np.float32)[None, :]
        for p in range(P):
            q = p % d
            c[p, oc:oc + T] = np.cos(ang[:, q % half]) if q < r else 1.0
            c[p, os:os + T] = np.sin(ang[:, q % half]) if q < r else 0.0
    for t in range(2):
        q = t * P + np.arange(P)
        end = (q // CH + 1) * CH
        c[:, C_ADM + t * TP:C_ADM + (t + 1) * TP] = np.where(np.arange(TP)[None, :] < end[:, None], 0.0, NEG)
    return c


class Steps:

    def __init__(self, eng, sem):
        self.eng, self.sem, self.n, self.base = eng, sem, 0, 0

    def did(self, ins):
        ins.then_inc(self.sem, 1)
        self.n += 1

    def settle(self):
        self.eng.wait_ge(self.sem, self.base + self.n)

    @contextmanager
    def loop(self, lo, hi, per):
        start = self.n
        with self.eng.Fori(lo, hi) as i:
            self.base, self.n = (i - lo) * per + start, 0
            yield i
            assert self.n == per, f"{self.n} steps in the body"
        self.base, self.n = 0, start + (hi - lo) * per


class Place:

    def __init__(self, unit, tile):
        self.lap, self.pair = unit, tile

    def slot(self, j):
        return j % RING

    def loads(self, j):
        return (self.lap + j // RING) * 16 + 16

    def free(self, j):
        return self.lap * RING + (j + 1)

    def through(self, j):
        return self.lap * RING + (j + 1 + RING)

    def split(self, j):
        return self.lap * RING + (j + 1)

    def bank_free(self, t):
        return self.pair + (t // 2 + 1)

    def bank_read(self, t):
        return self.pair + (t // 2 + 2)


def place(unit, tile, i=0, units=0, tiles=0):
    assert unit % RING == 0 and units % RING == 0 and tile % 2 == 0 and tiles % 2 == 0
    return Place(i * (units // RING) + unit // RING, i * (tiles // 2) + tile // 2)


def layer(nc, a, o):
    with ExitStack() as ctx:
        BASE = (nc.sbuf_base + 63) // 64 * 64
        END = nc.sbuf_usable_end - BASE
        R_RING = 0
        R_XN = R_RING + 3 * RING * UK * P * 4
        R_BC = R_XN + 2 * KT * T * 4
        R_BA = R_BC + 2 * 8 * T * 4
        R_BB = R_BA + 2 * 8 * T * 4
        R_K = R_BB + 2 * 8 * T * 4
        R_S = R_K + CW * 4
        R_W = R_S + 4224

        def at(name, off, shape, dt=F32):
            size = int(np.prod(shape)) * 4
            assert off + size <= END, name
            return nc.alloc_sbuf_tensor_at(name, [P] + shape, dt, offset=BASE + off)

        class Region:

            def __init__(self, off, end):
                self.off, self.end = off, end

            def __call__(self, name, shape, dt=F32):
                t = at(name, self.off, shape, dt)
                self.off += (int(np.prod(shape)) * 4 + 31) // 32 * 32
                assert self.off <= self.end, (name, self.off, self.end)
                return t

        raw = at("w_raw", R_RING, [RING, UK, P])
        whi = at("w_hi", R_RING + RING * UK * P * 4, [RING, UK, P], F32R)
        wlo = at("w_lo", R_RING + 2 * RING * UK * P * 4, [RING, UK, P], F32R)
        xhi = at("xn_hi", R_XN, [KT, T], F32R)
        xlo = at("xn_lo", R_XN + KT * T * 4, [KT, T], F32R)
        bhi = [at(f"branch_hi{n}", r, [8, T], F32R) for n, r in enumerate((R_BA, R_BB, R_BC))]
        blo = [at(f"branch_lo{n}", r + 8 * T * 4, [8, T], F32R) for n, r in enumerate((R_BA, R_BB, R_BC))]
        K = at("shape_consts", R_K, [CW])
        ident = K[:, C_ID:C_ID + P]
        small = Region(R_S, R_W)
        gcols = small("norm_gains", [4, KT])
        ccols = small("conv_cols", [6, 2 * FT])
        ustate = small("u_last", [4, 2 * FT])
        bias16 = small("if_bias", [1])
        nout = small("n_out", [2, MH])
        nst = small("n_state", [MH])
        mst = small("m_state", [MH])
        WE = END

        pro = Region(R_W, WE)
        xT = pro("xT", [KT, T])
        memT = pro("memT", [KT, NMEM])
        nv = pro("norm_var", [3, T])
        mtok = at("mem_tokens", R_BA, [2, D])
        xtok = at("x_tokens_prompt", R_XN, [2, D])
        xtos = at("x_tokens_sample", R_BA + 2 * KT * NMEM * 4, [D])
        assert 2 * KT * NMEM * 4 + D * 4 == R_K - R_BA
        xsq = at("x_squares", R_XN + KT * T * 4, [KT, T])
        msq = at("mem_squares", R_BC, [KT, NMEM])
        rows = Region(R_BC + KT * NMEM * 4, R_BA)
        grow = rows("gain_rows", [P])
        crow = rows("conv_rows", [6, P])
        nrow = rows("n_state_rows", [P])
        mrow = pro("m_state_row", [MH])
        mhi = at("mem_hi", R_BA, [KT, NMEM], F32R)
        mlo = at("mem_lo", R_BA + KT * NMEM * 4, [KT, NMEM], F32R)

        wc = Region(R_W, WE)
        CN = 4 * NMEM + 2 * T
        c_nxt, c_cur = wc("c_next", [CN]), wc("c_current", [CN])

        def c_parts(buf):
            return (buf[:, 0:2 * NMEM].rearrange("p (d m) -> p d m", d=2),
                    buf[:, 2 * NMEM:4 * NMEM].rearrange("p (d m) -> p d m", d=2),
                    buf[:, 4 * NMEM:CN].rearrange("p (d t) -> p d t", d=2))
        mk_n, mv_n, cq_n = c_parts(c_nxt)
        mk_c, mv_c, cq_c = c_parts(c_cur)
        ck = wc("cache_mem_k_head", [2, 256])
        cv = wc("cache_mem_v_head", [2, 256])
        mvn = wc("mem_v_tokens", [2, 256])
        mkn = wc("mem_k_tokens", [2, 256])
        ckT = wc("cache_mem_kT", [2, NMEM])
        c_p = wc("c_probs", [3, NMEM])
        c_pT = wc("c_probsT", [2, T])
        c_st = wc("c_stats", [4, 4])

        wb = Region(wc.off, WE)
        kTp = wb("kT_prompt", [2, TP])
        kTs = wb("kT_sample", [2, SS])
        vnp = wb("v_prompt", [2, 256])
        vns = wb("v_new", [256])
        cvB = wb("cache_v", [2, 256])
        iw = wb("index_weights", [3, IH])
        msk = wb("mask_bias", [2 * TP + SS])
        bcs = wb("b_cumsum", [NCH, MH])
        inter = wb("inter", [NCH, MH])
        wexp = wb("w_s", [NCH, MH])
        enm = wb("exp_neg_m", [NCH, MH])
        dec = wb("decay", [NCH, MH])
        mnew = wb("m_new", [NCH, MH])
        rb = Region(R_BB, R_K)
        Dm = rb("decay_matrix", [NCH, MH, CH])
        iqT = rb("index_qT", [4, T])
        ki2 = rb("index_kT", [T])
        kic = rb("index_kT_cache", [PAST])
        rl = rb("relu", [2, SS])
        ra = Region(R_BA, R_BB)
        vraw = ra("vT_raw", [2, T])
        kiw = ra("ikw_raw", [T])
        rin = ra("rope_in", [2, T])
        rtmp = ra("rope_tmp", [T])
        ifT = ra("if_T", [T])
        ckB = ra("cache_k", [2, 256])
        ckI = ra("cache_kidx", [2, 2, 64])
        kout = ra("k_tokens", [3, 256])
        kiout = ra("kidx_tokens", [3, 64])
        score = ra("score", [SS])
        igf = ra("if_gates", [NCH, 16])
        g1 = ra("gate_tmp", [NCH, MH])
        g2 = ra("log_f", [NCH, MH])
        acs = ra("ig_minus_b", [NCH, MH])
        mxs = ra("row_max", [NCH, MH])
        mb = ra("m_and_b", [NCH, 2, MH])
        mint = ra("m_inter", [NCH, MH])
        blast = ra("b_last", [NCH, MH])
        top8 = ra("top8", [8])
        diag = at("diag", R_W + 8 * T * 4, [MH, CH])

        wa = Region(R_W, wc.off)
        a_nxt, a_cur = wa("a_next", [4, T]), wa("a_current", [4, T])
        q_c, k_c, v_c, s_c = (a_cur[:, n, :] for n in range(4))
        kw = wa("k_weighted", [NCH, P])
        vn = wa("v_tokens", [NCH, P])
        SD = wa("scores_decayed", [NCH, CH])
        sdT = wa("scoresT", [NCH, CH])
        Cst = wa("C_states", [7, P + 1])
        hn = wa("h_tokens", [NCH, P])
        ga = wa("h_gated", [T])
        cs = wa("C_state_head", [P])
        co = wa("C_out", [2, P])
        a_st = wa("a_stats", [2, 8])

        wq = Region(R_W, wc.off)
        q_raw = wq("q_raw", [2, T])
        q_nxt, q_cur = wq("q_next", [2, T]), wq("q_current", [2, T])
        v_cur = wq("v_current", [5, P])
        sp_ = wq("probs_prompt", [2, 2 * TP])
        ss_ = wq("probs_sample", [2, SS])
        pTp = wq("probsT_prompt", [2, 2 * TP])
        pTs = wq("probsT_sample", [2, 3 * TS])
        q_tmp = wq("q_rope_tmp", [T])
        q_st = wq("q_stats", [2, 4, 4])

        wg = Region(R_W, WE)
        mghi = wg("merged_hi", [KT, T], F32R)
        mglo = wg("merged_lo", [KT, T], F32R)
        kg = Region(R_K + C_COS128 * 4, R_S)
        th = kg("gate_tanh", [3, T])
        acc = kg("merged_sum", [T])
        gtmp = wg("merged_tmp", [T])
        hT = at("hT", R_BC, [KT, T])
        h2 = at("h_square", R_K + C_COS128 * 4, [T])
        hacc = at("h_square_sum", R_K + (C_COS128 + T) * 4, [3 * P])

        wf = Region(R_W, WE)
        yhi = wf("y_hi", [GT, T], F32R)
        ylo = wf("y_lo", [GT, T], F32R)
        E2 = T + 4
        ext = wf("u_ext", [2, E2])
        cbuf = wf("conv", [2, E2])
        gth = wf("ffn_tanh", [E2])
        ybuf = wf("y", [T])
        fnv = wf("ffn_norm_var", [3, T])
        hg = at("h_scaled", R_BA, [KT, T])
        ytok = at("y_tokens", R_XN, [3, D])
        cvo = at("conv_out", R_XN + 3 * D * 4, [4, P])
        nrow2 = at("n_out_rows", R_XN + 3 * D * 4 + 4 * P * 4, [2 * P])

        scratch = nc.dram_tensor("xT_scratch", (P, KT * T), F32, kind="Internal").ap()

        psum = [ctx.enter_context(nc.psum_tensor(f"bank{n}", [P, 512], F32)) for n in range(8)]
        G, M = psum[0:2], psum[2:8]

        def sem(name):
            return ctx.enter_context(nc.semaphore(name))

        tables_in, mem_in, x_in, cache_in = sem("tables_in"), sem("mem_in"), sem("x_in"), sem("cache_in")
        raw_in = [sem(f"raw_in{n}") for n in range(RING)]
        w_hi, w_lo, w_used = sem("w_hi"), sem("w_lo"), sem("w_used")
        bank_read = [sem("bank_read0"), sem("bank_read1")]
        pe_own, act_own, dve_own = sem("pe_own"), sem("act_own"), sem("dve_own")
        sp_passed, pool_passed = sem("sp_passed"), sem("pool_passed")
        rows_T, rows_out = sem("rows_transposed"), sem("rows_out")
        xp_done, xp_act, xp_dve = sem("tokens_transposed"), sem("tokens_out_act"), sem("tokens_out_dve")
        squares, sums, variances, roots = sem("squares"), sem("sums"), sem("variances"), sem("roots")
        n_x, n_hi, n_lo = sem("norm_x"), sem("norm_hi"), sem("norm_lo")
        xT_out, hT_in = sem("xT_out"), sem("hT_in")
        c_shift, c_cache, c_xp, c_mvn, c_mkn, c_ckT = (sem("c_" + n) for n in (
            "shift", "cache", "transposed", "v_tokens", "k_tokens", "cache_kT"))
        c_sc, c_nm, c_exp, c_pn, c_pt, c_pTa, c_pTd, c_pv, c_hi, c_lo, c_out = (sem("c_" + n) for n in (
            "scores", "negmax", "exp", "probs", "transposes", "pT_act", "pT_dve", "values", "hi", "lo", "out"))
        b_vx, b_gx, b_v, b_if, b_iw, b_kix, b_ki, b_rot, b_rope, b_cx, b_cT, b_kx, b_ko, b_kio, b_vo = (
            sem("b_" + n) for n in ("v_transposed", "gates_transposed", "v_tokens", "if_gates", "index_w",
                                    "ki_rotated", "ki", "rotated", "roped", "cache_transposed", "cacheT",
                                    "k_transposed", "k_tokens", "k_out", "v_out"))
        i_lg, i_relu, i_acc, i_mask = (sem("i_" + n) for n in ("logits", "relu", "score", "mask"))
        g_e, g_l, g_lf, g_b, g_bs, g_dg, g_R, g_D, g_mb, g_last, g_arg, g_exp, g_Da, g_De, g_mo = (
            sem("g_" + n) for n in ("exp", "ln", "log_f", "cumsum", "cumsum_out", "diag", "rows", "logD",
                                    "m_and_b", "last_rows", "arguments", "exps", "D_arg", "D_exp", "m_out"))
        a_shift, a_cs, a_s0, a_vn, a_sd, a_kw, a_s1, a_sdT, a_C, a_s2, a_h, a_co, a_s3, a_ga, a_hi, a_lo, a_out, a_n = (
            sem("a_" + n) for n in ("shift", "state_in", "scores", "v_tokens", "decayed", "k_weighted",
                                    "outer", "scoresT", "states", "values", "h_tokens", "C_ready", "hT", "gated",
                                    "hi", "lo", "C_out", "n_out"))
        q_shift, q_rot, q_rope, q_sc, q_nm, q_exp, q_pn, q_pt, q_pT, q_pv, q_hi, q_lo = (
            sem("q_" + n) for n in ("shift", "rotated", "roped", "scores", "negmax", "exp", "probs",
                                    "transposes", "pT", "values", "hi", "lo"))
        m_sum, m_hi, m_lo = (sem("m_" + n) for n in ("sum", "hi", "lo"))
        f_us, f_ext, f_c0, f_conv, f_th, f_y, f_hi, f_lo, f_rms = (
            sem("f_" + n) for n in ("state", "ext", "tap2", "conv", "tanh", "y", "hi", "lo", "rms"))
        h_sq, h_sum, h_hi, h_lo, h_g = (sem("h_" + n) for n in ("square", "square_sum", "hi", "lo", "scaled"))
        y_T, y_act, y_dve, y_out, u_T, u_tok, u_out, n_T, n_tok = (
            sem(n) for n in ("y_transposed", "y_tokens_act", "y_tokens_dve", "y_out", "u_transposed", "u_tokens", "u_out",
                             "n_transposed", "n_tokens"))

        w_in = a["w_in"][0].rearrange("(k p) n -> p k n", p=P)
        w_mem = a["w_mem_kv"][0].rearrange("(k p) n -> p k n", p=P)
        w_out = a["w_out"][0].rearrange("(k p) n -> p k n", p=P)
        w_up = a["w_up"][0].rearrange("(k p) n -> p k n", p=P)
        w_down = a["w_down"][0].rearrange("(k p) n -> p k n", p=P)
        w_br = a["w_branch"][0].rearrange("b (k p) n -> b p k n", p=P)
        KD = (6, GT - 6)

        block = ctx.enter_context(nc.Block())

        @block.sync
        def _(sp):
            mem, xp, xs = a["mem_prompt"][0], a["x_prompt"][0], a["x_sample"][0]
            sp.dma_start(mtok[:, :, :], mem.rearrange("(t p) n -> p t n", p=P)).then_inc(mem_in, 16)
            sp.dma_start(K[:, :], a["tables"]).then_inc(tables_in, 16)
            for n, g in enumerate(("g_mix", "g_mem", "g_ffn")):
                sp.dma_start(grow[KT * n:KT * n + KT, :], a[g][0].rearrange("(k p) -> k p", p=P)).then_inc(tables_in, 16)
            sp.dma_start(grow[3 * KT:4 * KT, :], a["g_final"].rearrange("(k p) -> k p", p=P)).then_inc(tables_in, 16)
            sp.dma_start(crow[0:2 * FT, 0:3, :], a["conv_w"][0].rearrange("j (f p) -> f j p", p=P)).then_inc(tables_in, 16)
            sp.dma_start(crow[0:2 * FT, 3, :], a["conv_b"][0].rearrange("(f p) -> f p", p=P)).then_inc(tables_in, 16)
            sp.dma_start(crow[0:2 * FT, 4:6, :],
                         a["state_ffn_conv"][0, 0].rearrange("j (f p) -> f j p", p=P)).then_inc(tables_in, 16)
            sp.dma_start(nrow[0:MH, :], a["state_mlstm_n"][0, 0]).then_inc(tables_in, 16)
            sp.dma_start(mrow[0:1, :], a["state_mlstm_m"][0]).then_inc(tables_in, 16)
            sp.dma_start(bias16[0:MH, :], a["b_igate"].rearrange("o h -> h o")).then_inc(tables_in, 16)
            sp.dma_start(bias16[MH:2 * MH, :], a["b_fgate"].rearrange("o h -> h o")).then_inc(tables_in, 16)
            sp.dma_start(xtok[:, :, :], xp.rearrange("(t p) n -> p t n", p=P)).then_inc(x_in, 16)
            sp.dma_start(xtos[0:TS, :], xs).then_inc(x_in, 16)

            def load(pl, j, src):
                n, c = src.shape[1], src.shape[2]
                sp.wait_ge(w_lo, pl.free(j))
                sp.sem_inc(sp_passed, 1)
                sp.dma_start(raw[:, pl.slot(j), 0:n, 0:c], src).then_inc(raw_in[pl.slot(j)], 16)

            def load_tile(pl, j, w, col, cols=P, ks=(UK, UK), k0=0):
                for k in ks:
                    load(pl, j, w[:, ds(k0, k), ds(col, cols)])
                    j, k0 = j + 1, k0 + k

            def head_c(pl, h):
                for n, (w, col) in enumerate(((w_mem, h * 256), (w_mem, h * 256 + P), (w_mem, h * 256 + 1024),
                                              (w_mem, h * 256 + (1024 + P)), (w_in, h * 256 + O_CQ),
                                              (w_in, h * 256 + (O_CQ + P)))):
                    load_tile(pl, 2 * n, w, col)
            head_c(place(U_C, T_C), 0)
            with sp.Fori(1, CHD) as h:
                head_c(place(U_C, T_C, h, 12, 6), h)
            pl = place(U_B, T_B)
            for n, (col, cols) in enumerate(((O_AV, P), (O_AV + P, P), (O_IF, 16), (O_IKW, 72),
                                             (O_IQ, P), (O_IQ + P, P), (O_IQ + 2 * P, P), (O_IQ + 3 * P, P),
                                             (O_AK, P), (O_AK + P, P))):
                load_tile(pl, 2 * n, w_in, col, cols)

            def head_a(pl, h):
                for n, col in enumerate((O_MQ, O_MK, O_MV, O_MO)):
                    load_tile(pl, 2 * n, w_in, h * P + col)
            head_a(place(U_A, T_A), 0)
            with sp.Fori(1, MH) as h:
                head_a(place(U_A, T_A, h, 8, 4), h)
            with sp.Fori(0, AH // 2) as i:
                pl = place(U_Q, T_Q, i, 4, 2)
                for e in range(2):
                    load_tile(pl, 2 * e, w_in, i * (2 * P) + (O_AQ + e * P))
            with sp.Fori(0, KT // 4) as i:
                pl = place(U_G, T_G, i, 36, 24)
                for n in range(4):
                    for b in range(3):
                        load_tile(pl, 9 * n + 2 * b, w_in, i * (4 * P) + (O_G + b * D + n * P))
                    for b in range(3):
                        load(pl, 9 * n + 6 + b, w_br[b][:, :, ds(i * (4 * P) + n * P, P)])
            with sp.Fori(0, KT // 2) as i:
                pl = place(U_O, T_O, i, 4, 2)
                for e in range(2):
                    load_tile(pl, 2 * e, w_out, i * (2 * P) + e * P)
            for g in range(GROUPS):
                with sp.Fori(0, GT) as f:
                    pl = place(U_F + g * UF_G, T_F + g * TF_G, f, 4, 2)
                    load_tile(pl, 0, w_up, f * P + g * GT * P)
                    load_tile(pl, 2, w_up, f * P + (FF + g * GT * P))
                with sp.Fori(0, KT // 2) as i:
                    pl = place(U_F + g * UF_G + 4 * GT, T_F + g * TF_G + 2 * GT, i, 4, 2)
                    for e in range(2):
                        load_tile(pl, 2 * e, w_down, i * (2 * P) + e * P, ks=KD, k0=g * GT)
            y_dst = o["y_prompt"][0].rearrange("(u p) n -> u p n", p=P)
            for u in range(3):
                sp.wait_ge(y_act, 2 * u + 2)
                sp.wait_ge(y_dve, 2 * u + 2)
                sp.dma_start(y_dst[u] if u < 2 else o["y_sample"][0], ytok[0:P if u < 2 else TS, u, :]).then_inc(y_out, 16)
            sp.wait_ge(c_out, 32 * CHD)
            sp.wait_ge(b_vo, 32)
            sp.wait_ge(b_kio, 64)
            sp.wait_ge(g_mo, 32)
            sp.wait_ge(a_out, 32 * MH)
            sp.wait_ge(a_n, 32)
            sp.wait_ge(u_out, 32)
            sp.wait_ge(y_out, 48)

        @block.tensor
        def _(pe):
            pe.sem_inc(w_used, RING)
            pe.sem_inc(c_pv, 2)

            def multiply(pl, t, units, n, m=P, parts=None):
                pe.wait_ge(bank_read[t % 2], pl.bank_free(t))
                out = G[t % 2][0:m, 0:n]
                for un, (j, hi, lo, k0, nk) in enumerate(units):
                    if un and parts is not None:
                        pe.wait_ge(*parts)
                    pe.wait_ge(w_lo, pl.through(j))
                    for k in range(nk):
                        h, l = whi[:, pl.slot(j), k, 0:m], wlo[:, pl.slot(j), k, 0:m]
                        pe.matmul(out, h, hi[:, k0 + k, 0:n], start=un == 0 and k == 0, stop=False)
                        pe.matmul(out, h, lo[:, k0 + k, 0:n], start=False, stop=False)
                        last = pe.matmul(out, l, hi[:, k0 + k, 0:n], start=False,
                                         stop=un == len(units) - 1 and k == nk - 1)
                    last.then_inc(w_used, 1)

            def tile_x(pl, t, j, m=P):
                multiply(pl, t, [(j, xhi, xlo, 0, UK), (j + 1, xhi, xlo, UK, UK)], T, m)

            def tile_mem(pl, t, j):
                multiply(pl, t, [(j, mhi, mlo, 0, UK), (j + 1, mhi, mlo, UK, UK)], NMEM)

            def turn(out, in_):
                return pe.transpose(out, in_, ident[0:in_.shape[0], 0:in_.shape[0]])

            def mm(out, lhsT, rhs, first=True, last=True):
                return pe.matmul(out, lhsT, rhs, start=first, stop=last)

            pe.wait_ge(tables_in, 16 * 12)
            for j in range(3):
                turn(M[4][:, 88 * j:88 * j + 88], crow[0:88, j, :])
                turn(M[5][:, 64 + 88 * j:64 + 88 * j + 88], crow[0:88, 3 + j, :])
            turn(M[5][:, 0:64], grow[0:64, :])
            turn(M[5][:, 408:416], nrow[0:MH, :])
            mm(M[5][:, 400:408], K[0:1, C_ONE:C_ONE + P], mrow[0:1, :]).then_inc(rows_T, 1)

            def bank_of_transposes(n, parts):
                if n >= 4:
                    pe.wait_ge(xp_dve if n % 2 else xp_act, (n - 4) // 2 + 1)
                for out, in_ in parts:
                    last = turn(out, in_)
                last.then_inc(xp_done, 1)
            pe.wait_ge(mem_in, 16)
            for n in range(8):
                bank_of_transposes(n, [(M[n % 4][:, e * 256 + t * P:e * 256 + t * P + P],
                                        mtok[:, t, (2 * n + e) * P:(2 * n + e + 1) * P])
                                       for e in range(2) for t in range(2)])

            def sum_squares(sq, n, bank, done):
                pe.wait_ge(squares, done)
                for k in range(KT):
                    last = mm(bank[:, 0:n], K[:, C_ONE:C_ONE + P], sq[:, k, :], k == 0, k == KT - 1)
                last.then_inc(sums, 1)
            pe.wait_ge(rows_out, 1)
            sum_squares(msq, NMEM, M[4], 1)
            pe.wait_ge(x_in, 32)
            for n in range(8, 24):
                k = n - 8
                bank_of_transposes(n, [(M[n % 4][:, t * P:t * P + P], xtok[:, t, k * P:k * P + P]) for t in range(2)]
                                   + [(M[n % 4][:, TP:T], xtos[0:TS, k * P:k * P + P])])
            sum_squares(xsq, T, M[5], 2)

            def c_turn(h):
                pe.wait_ge(c_shift, h + 1)
                pe.wait_ge(c_cache, h * 32 + 32)
                for m in range(2):
                    for d in range(2):
                        turn(M[0][:, m * 256 + d * P:m * 256 + d * P + P], mv_c[:, d, m * P:m * P + P])
                        turn(M[1][:, d * 256 + m * P:d * 256 + m * P + P], ck[:, m, d * P:d * P + P])
                        last = turn(M[2][:, m * 256 + d * P:m * 256 + d * P + P], mk_c[:, d, m * P:m * P + P])
                last.then_inc(c_xp, 1)

            def c_scores(h):
                pe.wait_ge(c_ckT, h + 1)
                pe.wait_ge(c_lo, h * 2 + 2)
                for t in range(2):
                    for d in range(2):
                        mm(M[3][:, t * NMEM:(t + 1) * NMEM], cq_c[:, d, t * P:t * P + P], mk_c[:, d, :], d == 0, d == 1)
                for d in range(2):
                    last = mm(M[4][0:TS, 0:NMEM], cq_c[:, d, TP:T], ckT[:, d, :], d == 0, d == 1)
                last.then_inc(c_sc, 1)

            def c_probsT(h):
                pe.wait_ge(c_pn, h + 1)
                pe.wait_ge(c_mkn, h + 1)
                for m in range(2):
                    b = M[5] if m == 0 else M[2]
                    for t in range(2):
                        turn(b[:, t * P:t * P + P], c_p[:, t, m * P:m * P + P])
                    last = turn(b[:, TP:T], c_p[0:TS, 2, m * P:m * P + P])
                last.then_inc(c_pt, 1)

            def c_values(h):
                pe.wait_ge(c_pTa, h + 1)
                pe.wait_ge(c_pTd, h + 1)
                pe.wait_ge(c_mvn, h + 1)
                for d in range(2):
                    b = M[3 + d]
                    for m in range(2):
                        mm(b[:, 0:TP], mvn[:, m, d * P:d * P + P], c_pT[:, m, 0:TP], m == 0, m == 1)
                    for m in range(2):
                        last = mm(b[:, TP:T], cv[:, m, d * P:d * P + P], c_pT[:, m, TP:T], m == 0, m == 1)
                    last.then_inc(c_pv, 1)

            def c_tiles(pl, stages):
                for t in range(6):
                    if t < 4:
                        tile_mem(pl, t, 2 * t)
                    else:
                        tile_x(pl, t, 2 * t)
                    if t < len(stages):
                        stages[t]()

            pe.wait_ge(n_lo, KT)
            pl = place(U_C, T_C)
            for t in range(4):
                tile_mem(pl, t, 2 * t)
            pe.wait_ge(n_lo, 2 * KT)
            for t in range(4, 6):
                tile_x(pl, t, 2 * t)
            with pe.Fori(1, CHD) as h:
                c_tiles(place(U_C, T_C, h, 12, 6), [lambda: c_turn(h - 1), lambda: c_scores(h - 1),
                                                    lambda: c_probsT(h - 1), lambda: c_values(h - 1)])

            pl = place(U_B, T_B)

            def rotate(bank, rot, x, wait_value):
                return mm(bank[:, 0:T], rot, x)
            for t in range(10):
                tile_x(pl, t, 2 * t, (P, P, 16, 72, P, P, P, P, P, P)[t])
                if t < 4:
                    (c_turn, c_scores, c_probsT, c_values)[t](CHD - 1)
                if t == 4:
                    pe.wait_ge(bank_read[0], pl.bank_read(0))
                    pe.wait_ge(bank_read[1], pl.bank_read(1))
                    for j in range(2):
                        for u in range(2):
                            turn(M[0][:, u * 256 + j * P:u * 256 + j * P + P], vraw[:, j, u * P:u * P + P])
                        last = turn(M[1][0:TS, j * P:j * P + P], vraw[:, j, TP:T])
                    last.then_inc(b_vx, 1)
                    pe.wait_ge(bank_read[0], pl.bank_read(2))
                    for c in range(NCH):
                        turn(M[5][0:CH, c * 16:c * 16 + 16], ifT[0:16, c * CH:c * CH + CH])
                    pe.wait_ge(bank_read[1], pl.bank_read(3))
                    for u in range(3):
                        n = P if u < 2 else TS
                        last = turn(M[2][0:n, u * 72:u * 72 + 72], kiw[0:72, u * P:u * P + n])
                    last.then_inc(b_gx, 1)
                if t == 5:
                    pe.wait_ge(c_lo, 2 * CHD + 2)
                    mm(M[3][:, 0:T], K[0:64, C_DUP:C_DUP + P], kiw[0:64, :])
                    mm(M[4][:, 0:T], K[0:64, C_RDUP:C_RDUP + P], kiw[0:64, :]).then_inc(b_kix, 1)
                if t == 6:
                    pe.wait_ge(cache_in, 64)
                    pe.wait_ge(b_ki, 1)
                    for j in range(2):
                        for u in range(2):
                            turn(M[3][:, j * 256 + u * P:j * 256 + u * P + P], ckB[:, u, j * P:j * P + P])
                    for u in range(2):
                        last = turn(M[4][:, u * P:u * P + P], ckI[:, u, :, :].rearrange("p a d -> p (a d)"))
                    last.then_inc(b_cx, 1)
                if 5 <= t:
                    n = t - 5
                    pe.wait_ge(bank_read[(t - 1) % 2], pl.bank_read(t - 1))
                    if n == 0:
                        pe.wait_ge(b_v, 1)
                        pe.wait_ge(b_iw, 1)
                    if n == 4:
                        pe.wait_ge(b_rope, 1)
                    bank = M[(0, 1, 2, 5, 0)[n]]
                    mm(bank[:, 0:T], K[:, C_R64:C_R64 + P] if n < 4 else K[:, C_R128:C_R128 + P],
                       rin[:, (t - 1) % 2, :]).then_inc(b_rot, 1)

            def a_scores(h):
                pe.wait_ge(tables_in, 16 * 12)
                pe.wait_ge(a_shift, h + 1)
                pe.wait_ge(a_cs, h * 16 + 16)
                for c in range(NCH):
                    q, k, v = (x[:, c * CH:c * CH + CH] for x in (q_c, k_c, v_c))
                    mm(M[0][0:CH, c * CH:c * CH + CH], q, k)
                    turn(M[1][0:CH, c * P:c * P + P] if c < 4 else M[3][0:CH, 0:P], k)
                    turn(M[2][0:CH, c * P:c * P + P] if c < 4 else M[3][0:CH, P:2 * P], v)
                turn(M[3][:, 2 * P:3 * P], cs[:, :]).then_inc(a_s0, 1)

            def a_outer(h):
                pe.wait_ge(tables_in, 16 * 12)
                pe.wait_ge(a_sd, h + 1)
                pe.wait_ge(a_kw, h + 1)
                pe.wait_ge(a_vn, h + 1)
                for c in range(NCH):
                    turn(M[0][0:CH, c * CH:c * CH + CH], SD[0:CH, c, :])
                    mm(M[1][:, c * P:c * P + P] if c < 4 else M[3][:, 0:P], kw[0:CH, c, :], vn[0:CH, c, :])
                    last = mm(M[5][:, c:c + 1], kw[0:CH, c, :], K[0:CH, C_ONE:C_ONE + 1])
                last.then_inc(a_s1, 1)

            def a_values(h):
                pe.wait_ge(tables_in, 16 * 12)
                pe.wait_ge(a_sdT, h + 1)
                pe.wait_ge(a_C, h + 1)
                for c in range(NCH):
                    q = q_c[:, c * CH:c * CH + CH]
                    C = Cst[:, c if c < 4 else 5, :]
                    mm(M[2][0:CH, c * P:c * P + P] if c < 4 else M[5][0:CH, P:2 * P], sdT[0:CH, c, :], vn[0:CH, c, :])
                    mm(M[4][0:CH, c * P:c * P + P] if c < 4 else M[5][0:CH, 2 * P:3 * P], q, C[:, 0:P])
                    mm(M[5][0:CH, 8 + c:9 + c], q, C[:, P:P + 1])
                turn(M[1][:, 0:P], Cst[:, 4, 0:P])
                turn(M[1][:, P:2 * P], Cst[:, 6, 0:P]).then_inc(a_s2, 1)

            def a_hT(h):
                pe.wait_ge(tables_in, 16 * 12)
                pe.wait_ge(a_h, h + 1)
                for c in range(NCH):
                    last = turn(M[4][:, c * CH:c * CH + CH], hn[0:CH, c, :])
                last.then_inc(a_s3, 1)

            def logits(u, h):
                n = u * IH + h
                q = 64 * (h % 2)
                rows = P if u < 2 else TS
                if n >= 2:
                    pe.wait_ge(i_relu, n - 1)
                b = M[4] if n % 2 else M[2]
                lhs = iqT[q:q + 64, h // 2, u * P:u * P + rows]
                if u < 2:
                    last = mm(b[0:rows, 0:TP], lhs, ki2[q:q + 64, 0:TP])
                else:
                    mm(b[0:rows, 0:PAST], lhs, kic[q:q + 64, :])
                    last = mm(b[0:rows, PAST:SS], lhs, ki2[q:q + 64, TP:T])
                last.then_inc(i_lg, 1)

            pl = place(U_A, T_A)
            plb = place(U_B, T_B)
            for t in range(4):
                tile_x(pl, t, 2 * t)
                if t == 0:
                    pe.wait_ge(bank_read[1], plb.bank_read(9))
                    pe.wait_ge(b_rope, 4)
                    mm(M[1][:, 0:T], K[:, C_R128:C_R128 + P], rin[:, 1, :]).then_inc(b_rot, 1)
                    pe.wait_ge(g_lf, 1)
                    mm(M[5][0:CH, 0:NCH * MH], K[0:CH, C_CUM:C_CUM + CH],
                       g2[0:CH, :, :].rearrange("p c h -> p (c h)")).then_inc(g_b, 1)
                if t == 1:
                    pe.wait_ge(b_rope, 6)
                    for j in range(2):
                        for u in range(2):
                            turn(M[0][:, u * 256 + j * P:u * 256 + j * P + P], kTp[:, j, u * P:u * P + P])
                        turn(M[1][0:TS, j * P:j * P + P], kTs[:, j, PAST:SS])
                    for u in range(3):
                        n = P if u < 2 else TS
                        last = turn(M[1][0:n, 256 + 64 * u:320 + 64 * u], ki2[0:64, u * P:u * P + n])
                    last.then_inc(b_kx, 1)
                    pe.wait_ge(b_cT, 1)
                    for c in range(NCH):
                        pe.wait_ge(g_dg, c + 1)
                        if c >= 2:
                            pe.wait_ge(g_D, c - 1)
                        mm(M[3 if c % 2 else 5][0:CH, :], K[0:CH, C_ONE:C_ONE + CH],
                           diag[0:CH, :, :].rearrange("p h s -> p (h s)")).then_inc(g_R, 1)
                if t == 2:
                    for h in range(IH):
                        logits(0, h)
                    for c in range(NCH):
                        pe.wait_ge(g_mb, c + 1)
                        mm(M[3][:, 16 * c:16 * c + 16], K[0:CH, C_LAST:C_LAST + P],
                           mb[0:CH, c, :, :].rearrange("p a h -> p (a h)")).then_inc(g_last, 1)
                if t == 3:
                    for u in range(1, 3):
                        for h in range(IH):
                            logits(u, h)
            a_stages = (a_scores, a_outer, a_values, a_hT)
            pe.wait_ge(i_relu, 3 * IH)
            pe.wait_ge(b_ko, 1)
            pe.wait_ge(g_De, 1)
            with pe.Fori(1, MH) as h:
                pl = place(U_A, T_A, h, 8, 4)
                for t in range(4):
                    tile_x(pl, t, 2 * t)
                    a_stages[t](h - 1)

            def q_scores(i):
                j = i // 2
                pe.wait_ge(q_shift, i + 1)
                for e in range(2):
                    for u in range(2):
                        mm(M[2 * e][:, u * TP:(u + 1) * TP], q_cur[:, e, u * P:u * P + P], kTp[:, j, :])
                    mm(M[2 * e + 1][0:TS, 0:SS], q_cur[:, e, TP:T], kTs[:, j, :]).then_inc(q_sc, 1)

            def q_probsT(i):
                for e in range(2):
                    pe.wait_ge(q_pn, i * 2 + (e + 1))
                    for s in range(2):
                        for u in range(2):
                            turn(M[4 + e][:, s * TP + u * P:s * TP + u * P + P],
                                 sp_[:, e, u * TP + s * P:u * TP + s * P + P])
                        turn(M[2 * e + 1][:, s * TS:(s + 1) * TS], ss_[0:TS, e, s * P:s * P + P])
                    turn(M[2 * e + 1][0:TS, 2 * TS:3 * TS], ss_[0:TS, e, PAST:SS]).then_inc(q_pt, 1)

            def q_values(i):
                for e in range(2):
                    pe.wait_ge(q_pT, i * 2 + (e + 1))
                    b = M[4 + e]
                    for s in range(2):
                        mm(b[:, 0:TP], v_cur[:, s, :], pTp[:, e, s * TP:(s + 1) * TP], s == 0, s == 1)
                    for s in range(3):
                        n = P if s < 2 else TS
                        last = mm(b[:, TP:T], v_cur[0:n, 2 + s, :], pTs[0:n, e, s * TS:(s + 1) * TS], s == 0, s == 2)
                    last.then_inc(q_pv, 1)

            def q_rotate(pl, e):
                pe.wait_ge(bank_read[e], pl.bank_read(e))
                mm(M[2 * e][:, 0:T], K[:, C_R128:C_R128 + P], q_raw[:, e, :]).then_inc(q_rot, 1)

            pl = place(U_Q, T_Q)
            tile_x(pl, 0, 0)
            a_scores(MH - 1)
            a_outer(MH - 1)
            tile_x(pl, 1, 2)
            a_values(MH - 1)
            a_hT(MH - 1)
            for e in range(2):
                q_rotate(pl, e)
            with pe.Fori(1, AH // 2) as i:
                pl = place(U_Q, T_Q, i, 4, 2)
                tile_x(pl, 0, 0)
                q_scores(i - 1)
                tile_x(pl, 1, 2)
                q_probsT(i - 1)
                for e in range(2):
                    q_rotate(pl, e)
                q_values(i - 1)
            q_scores(AH // 2 - 1)
            q_probsT(AH // 2 - 1)
            q_values(AH // 2 - 1)

            pe.wait_ge(q_lo, AH)
            with pe.Fori(0, KT // 4) as i:
                pl = place(U_G, T_G, i, 36, 24)
                for n in range(4):
                    for b in range(3):
                        tile_x(pl, 6 * n + b, 9 * n + 2 * b)
                    for b in range(3):
                        multiply(pl, 6 * n + 3 + b, [(9 * n + 6 + b, bhi[b], blo[b], 0, UK)], T)

            pe.wait_ge(m_lo, KT + 1)
            with pe.Fori(0, KT // 2) as i:
                pl = place(U_O, T_O, i, 4, 2)
                for e in range(2):
                    multiply(pl, e, [(2 * e, mghi, mglo, 0, UK), (2 * e + 1, mghi, mglo, UK, UK)], T)
            pe.wait_ge(h_sum, KT + 1)
            mm(M[0][:, 0:T], K[:, C_ONE:C_ONE + P], hacc[:, 0:T]).then_inc(sums, 1)

            pe.wait_ge(h_lo, KT)
            for g in range(GROUPS):
                with pe.Fori(0, GT) as f:
                    pl = place(U_F + g * UF_G, T_F + g * TF_G, f, 4, 2)
                    tile_x(pl, 0, 0)
                    tile_x(pl, 1, 2)
                pe.wait_ge(f_lo, GT * g + KD[0] + 1)
                with pe.Fori(0, KT // 2) as i:
                    pl = place(U_F + g * UF_G + 4 * GT, T_F + g * TF_G + 2 * GT, i, 4, 2)
                    for e in range(2):
                        multiply(pl, e, [(2 * e, yhi, ylo, 0, KD[0]), (2 * e + 1, yhi, ylo, KD[0], KD[1])], T,
                                 parts=(f_lo, GT * (g + 1) + 1))

            for j in range(4):
                last = turn(M[1][0:2 * FT, j * P:j * P + P], ustate[:, j, :])
            last.then_inc(u_T, 1)
            turn(M[2][0:MH, 0:P], nout[:, 0, :])
            turn(M[2][0:MH, P:2 * P], nout[:, 1, :]).then_inc(n_T, 1)
            pe.wait_ge(h_sum, 2 * KT + 2)
            for u in range(3):
                last = mm(M[5][:, u:u + 1], hacc[:, u * P:u * P + P], K[:, C_ONE:C_ONE + 1])
            last.then_inc(sums, 1)
            for n in range(12):
                u, q = n // 4, n % 4
                rows = P if u < 2 else TS
                if n < 4:
                    pe.wait_ge(h_g, 4 * q + 4)
                else:
                    pe.wait_ge(y_dve if n % 2 else y_act, (n - 4) // 2 + 1)
                if n == 0:
                    pe.wait_ge(n_tok, 1)
                for k in range(4):
                    last = turn(M[n % 4][0:rows, k * P:k * P + P], hg[:, 4 * q + k, u * P:u * P + rows])
                last.then_inc(y_T, 1)

        @block.scalar
        def _(act):
            act.sem_inc(f_us, 1)
            act.sem_inc(bank_read[0], 1)
            act.sem_inc(bank_read[1], 1)

            def split(pl, *units):
                for j in units:
                    j += LEAD
                    act.wait_ge(raw_in[pl.slot(j)], pl.loads(j))
                    act.wait_ge(w_used, pl.free(j))
                    act.copy(whi[:, pl.slot(j), :, :], raw[:, pl.slot(j), :, :]).then_inc(w_hi, 1)

            def read_tile(pl, t, j, out, m=P, n=T, func=ACT.Copy, scale=1.0, bias=None):
                act.wait_ge(w_used, pl.through(j))
                kw_ = {} if bias is None else {"bias": bias}
                act.activation(out, G[t % 2][0:m, 0:n], func, scale=scale, **kw_).then_inc(bank_read[t % 2], 1)

            def copy_tokens(n0, n1, out_of):
                for n in range(n0, n1, 2):
                    act.wait_ge(xp_done, n + 1)
                    act.copy(*out_of(n)).then_inc(xp_act, 1)

            def norm_hi(lo, n, hi, sq):
                with act.Fori(0, KT) as k:
                    act.wait_ge(n_x, k + (lo * KT + 1))
                    act.copy(hi[:, k, 0:n], sq[:, k, 0:n]).then_inc(n_hi, 1)

            def root(done, n):
                act.wait_ge(variances, done)
                act.activation(nv[:, 1, 0:n] if done < 3 else fnv[:, 1, 0:n],
                               nv[:, 0, 0:n] if done < 3 else fnv[:, 0, 0:n], ACT.Sqrt).then_inc(roots, 1)

            copy_tokens(0, 8, lambda n: (memT[:, 2 * n:2 * n + 2, :], M[n % 4][:, :].rearrange("p (e m) -> p e m", e=2)))
            act.wait_ge(xp_act, 4)
            act.wait_ge(xp_dve, 4)
            act.activation(msq[:, :, :], memT[:, :, :], ACT.Square).then_inc(squares, 1)
            root(1, NMEM)
            norm_hi(0, NMEM, mhi, msq)
            pl = place(U_C, T_C)
            split(pl, -2, -1)
            copy_tokens(8, 24, lambda n: (xT[:, n - 8, :], M[n % 4][:, 0:T]))
            act.wait_ge(xp_act, 12)
            act.wait_ge(xp_dve, 12)
            act.dma_start(scratch, xT[:, :, :].rearrange("p k t -> p (k t)")).then_inc(xT_out, 16)
            act.activation(xsq[:, :, :], xT[:, :, :], ACT.Square).then_inc(squares, 1)
            root(2, T)

            def c_copies(h):
                act.wait_ge(c_xp, h + 1)
                act.copy(mvn[:, :, :], M[0][:, :].rearrange("p (m d) -> p m d", m=2)).then_inc(c_mvn, 1)
                act.copy(mkn[:, :, :], M[2][:, :].rearrange("p (m d) -> p m d", m=2)).then_inc(c_mkn, 1)

            def c_exps(h):
                act.wait_ge(c_nm, h + 1)
                for u in range(2):
                    act.activation(c_p[:, u, :], M[3][:, u * NMEM:(u + 1) * NMEM], ACT.Exp, scale=1.0 / 16,
                                   bias=c_st[:, 1, u:u + 1], accum_out=c_st[:, 2, u:u + 1])
                act.activation(c_p[0:TS, 2, :], M[4][0:TS, 0:NMEM], ACT.Exp, scale=1.0 / 16,
                               bias=c_st[0:TS, 1, 2:3], accum_out=c_st[0:TS, 2, 2:3]).then_inc(c_exp, 1)

            def c_pT0(h):
                act.wait_ge(c_pt, h + 1)
                act.copy(c_pT[:, 0, :], M[5][:, 0:T]).then_inc(c_pTa, 1)

            def c_his(h):
                for d in range(2):
                    act.wait_ge(c_pv, h * 2 + (d + 3))
                    act.copy(bhi[2][:, h * 2 + d, :], M[3 + d][:, 0:T]).then_inc(c_hi, 1)

            def c_tiles(pl, stages, shifted):
                for t in range(6):
                    split(pl, 2 * t, 2 * t + 1)
                    if t % 2 == 0:
                        if t == 0 and shifted is not None:
                            act.wait_ge(c_shift, shifted)
                        read_tile(pl, t, 2 * t + 1, (mk_n[:, 0, :], mv_n[:, 0, :], cq_n[:, 0, :])[t // 2],
                                  n=NMEM if t < 4 else T)
                    if t < len(stages):
                        stages[t]()
            norm_hi(1, T, xhi, xsq)
            act.wait_ge(xT_out, 16)
            c_tiles(pl, [], None)
            with act.Fori(1, CHD) as h:
                c_tiles(place(U_C, T_C, h, 12, 6), [lambda: c_copies(h - 1), lambda: c_exps(h - 1),
                                                    lambda: c_pT0(h - 1), lambda: c_his(h - 1)], h)

            pl = place(U_B, T_B)
            for t in range(10):
                split(pl, 2 * t, 2 * t + 1)
                if t == 2:
                    read_tile(pl, t, 5, ifT[0:16, :], 16, func=ACT.Identity, bias=bias16[0:16, :])
                elif t % 2 == 0:
                    if t >= 6:
                        act.wait_ge(b_rope, (t - 6) // 2 * 2 + 1)
                    read_tile(pl, t, 2 * t + 1, vraw[:, 0, :] if t == 0 else rin[:, 0, :])
                if t < 4:
                    (c_copies, c_exps, c_pT0, c_his)[t](CHD - 1)
                if t == 4:
                    act.wait_ge(b_vx, 1)
                    act.copy(vnp[:, :, :], M[0][:, :].rearrange("p (u c) -> p u c", u=2))
                    act.copy(vns[0:TS, :], M[1][0:TS, 0:256]).then_inc(b_v, 1)
                    act.wait_ge(b_gx, 1)
                    act.copy(igf[0:CH, :, :], M[5][0:CH, 0:16 * NCH].rearrange("p (c g) -> p c g", c=NCH)).then_inc(b_if, 1)
                if t == 6:
                    act.wait_ge(b_cx, 1)
                    act.copy(kTs[:, :, 0:PAST], M[3][:, :].rearrange("p (j s) -> p j s", j=2))
                    act.copy(kic[:, :], M[4][:, 0:PAST]).then_inc(b_cT, 1)
                if t == 7:
                    act.wait_ge(b_if, 1)
                    act.activation(g1[0:CH, :, :], igf[0:CH, :, MH:2 * MH], ACT.Abs).then_inc(act_own, 1)
                    act.wait_ge(act_own, 1)
                    act.activation(g1[0:CH, :, :], g1[0:CH, :, :], ACT.Exp, scale=-1.0).then_inc(act_own, 1)
                    act.wait_ge(act_own, 2)
                    act.activation(g1[0:CH, :, :], g1[0:CH, :, :], ACT.Ln, bias=1.0).then_inc(g_l, 1)

            def a_read(pl, t, n):
                if t == 3:
                    read_tile(pl, t, 2 * t + 1, a_nxt[:, 3, :], func=ACT.Tanh, scale=0.5)
                elif t != 1:
                    read_tile(pl, t, 2 * t + 1, a_nxt[:, t, :])

            def a_vcopies(h):
                act.wait_ge(a_s0, h + 1)
                act.copy(vn[0:CH, 0:4, :], M[2][0:CH, :].rearrange("p (c v) -> p c v", c=4))
                act.copy(vn[0:CH, 4, :], M[3][0:CH, P:2 * P])
                act.copy(Cst[:, 5, 0:P], M[3][:, 2 * P:3 * P])
                act.copy(Cst[:, 5, P:P + 1], nst[:, ds(h, 1)]).then_inc(a_vn, 1)

            def a_sdTs(h):
                act.wait_ge(a_s1, h + 1)
                act.copy(sdT[0:CH, :, :], M[0][0:CH, 0:T].rearrange("p (c s) -> p c s", c=NCH)).then_inc(a_sdT, 1)

            def a_Cout(h):
                act.wait_ge(a_s2, h + 1)
                act.copy(co[:, :, :], M[1][:, 0:2 * P].rearrange("p (g d) -> p g d", g=2)).then_inc(a_co, 1)

            def a_his(h):
                act.wait_ge(a_ga, h + 1)
                act.activation(bhi[0][:, ds(h, 1), :].rearrange("p o t -> p (o t)"), ga[:, :], ACT.Copy,
                               scale=0.5).then_inc(a_hi, 1)

            def relus(u, h0, h1):
                rows = P if u < 2 else TS
                n_ = TP if u < 2 else SS
                for h in range(h0, h1):
                    n = u * IH + h
                    act.wait_ge(i_lg, n + 1)
                    if n >= 2:
                        act.wait_ge(i_acc, n - 1)
                    act.activation(rl[0:rows, h % 2, 0:n_], (M[4] if n % 2 else M[2])[0:rows, 0:n_], ACT.Relu,
                                   scale=0.125).then_inc(i_relu, 1)

            pl = place(U_A, T_A)
            for t in range(4):
                split(pl, 2 * t, 2 * t + 1)
                a_read(pl, t, 0)
                if t == 1:
                    act.wait_ge(b_kx, 1)
                    act.copy(kout[:, 0:2, :], M[0][:, :].rearrange("p (u c) -> p u c", u=2))
                    act.copy(kout[0:TS, 2, :], M[1][0:TS, 0:256])
                    act.copy(kiout[:, 0:2, :], M[1][:, 256:384].rearrange("p (u c) -> p u c", u=2))
                    act.copy(kiout[0:TS, 2, :], M[1][0:TS, 384:448]).then_inc(b_ko, 1)
                if t == 2:
                    relus(0, 0, IH)
                    act.wait_ge(g_arg, 1)
                    for x in (inter, wexp, enm):
                        act.activation(x[0:CH, :, :], x[0:CH, :, :], ACT.Exp)
                    act.activation(dec[:, :, :], dec[:, :, :], ACT.Exp).then_inc(g_exp, 1)
                    act.wait_ge(g_Da, 1)
                    act.activation(Dm[0:CH, :, :, :], Dm[0:CH, :, :, :], ACT.Exp).then_inc(g_De, 1)
                if t == 3:
                    relus(1, 0, IH)
                    relus(2, 0, IH)
            with act.Fori(1, MH) as h:
                pl = place(U_A, T_A, h, 8, 4)
                for t in range(4):
                    split(pl, 2 * t, 2 * t + 1)
                    if t == 0:
                        act.wait_ge(a_shift, h)
                    a_read(pl, t, h)
                    (a_vcopies, a_sdTs, a_Cout, a_his)[t](h - 1)

            def q_read(pl, e):
                if e == 0:
                    read_tile(pl, 0, 1, q_raw[:, 0, :])

            def q_exps(i):
                for e in range(2):
                    act.wait_ge(q_nm, i * 2 + (e + 1))
                    for u in range(2):
                        act.activation(sp_[:, e, u * TP:(u + 1) * TP], sp_[:, e, u * TP:(u + 1) * TP], ACT.Exp,
                                       bias=q_st[:, e, 1, u:u + 1], accum_out=q_st[:, e, 2, u:u + 1])
                    act.activation(ss_[0:TS, e, :], ss_[0:TS, e, :], ACT.Exp, bias=q_st[0:TS, e, 1, 2:3],
                                   accum_out=q_st[0:TS, e, 2, 2:3]).then_inc(q_exp, 1)

            def q_pTs(i):
                for e in range(2):
                    act.wait_ge(q_pt, i * 2 + (e + 1))
                    act.copy(pTp[:, e, :], M[4 + e][:, :])
                    act.copy(pTs[:, e, 0:2 * TS], M[2 * e + 1][:, 0:2 * TS])
                    act.copy(pTs[0:TS, e, 2 * TS:3 * TS], M[2 * e + 1][0:TS, 2 * TS:3 * TS]).then_inc(q_pT, 1)

            def q_his(i):
                for e in range(2):
                    act.wait_ge(q_pv, i * 2 + (e + 1))
                    act.copy(bhi[1][:, i * 2 + e, :], M[4 + e][:, 0:T]).then_inc(q_hi, 1)

            pl = place(U_Q, T_Q)
            split(pl, 0, 1)
            act.wait_ge(a_shift, MH)
            q_read(pl, 0)
            a_vcopies(MH - 1)
            a_sdTs(MH - 1)
            split(pl, 2, 3)
            a_Cout(MH - 1)
            a_his(MH - 1)
            with act.Fori(1, AH // 2) as i:
                pl = place(U_Q, T_Q, i, 4, 2)
                split(pl, 0, 1)
                act.wait_ge(q_rope, i * 2)
                q_read(pl, 0)
                q_exps(i - 1)
                split(pl, 2, 3)
                q_pTs(i - 1)
                q_his(i - 1)
            q_exps(AH // 2 - 1)
            q_pTs(AH // 2 - 1)
            q_his(AH // 2 - 1)

            with act.Fori(0, KT // 4) as i:
                pl = place(U_G, T_G, i, 36, 24)
                for n in range(4):
                    for b in range(3):
                        split(pl, 9 * n + 2 * b, 9 * n + 2 * b + 1)
                        if b == 0:
                            act.wait_ge(m_sum, i * 4 + (n + 1))
                        read_tile(pl, 6 * n + b, 9 * n + 2 * b + 1, th[:, b, :], func=ACT.Tanh, scale=0.5)
                    for b in range(3):
                        split(pl, 9 * n + 6 + b)
                    act.wait_ge(m_sum, i * 4 + (n + 2))
                    act.activation(mghi[:, i * 4 + n, :], acc[:, :], ACT.Copy, scale=0.5).then_inc(m_hi, 1)

            def square(pl, e, k, summed):
                act.wait_ge(bank_read[e], pl.bank_read(e))
                act.wait_ge(h_sum, summed)
                act.activation(h2[:, :], hT[:, k, :], ACT.Square).then_inc(h_sq, 1)
            act.wait_ge(xT_out, 16)
            act.dma_start(hT[:, :, :].rearrange("p k t -> p (k t)"), scratch).then_inc(hT_in, 16)
            with act.Fori(0, KT // 2) as i:
                pl = place(U_O, T_O, i, 4, 2)
                for e in range(2):
                    split(pl, 2 * e, 2 * e + 1)
                    square(pl, e, i * 2 + e, i * 2 + (e + 1))
                    act.activation(xhi[:, i * 2 + e, :], hT[:, i * 2 + e, :], ACT.Identity,
                                   scale=gcols[:, 2, ds(i * 2 + e, 1)]).then_inc(h_hi, 1)
            root(3, T)

            def conv_inputs(pl, e, pair, col):
                act.copy(ext[:, e, TP + 2:TP + 4], ccols[:, 4:6, col]).then_inc(f_ext, 1)
                act.wait_ge(f_ext, pair * 2 + (e + 1))
                act.wait_ge(bank_read[e], pl.bank_read(e))
                act.activation(cbuf[:, e, 0:T + 2], ext[:, e, 2:E2], ACT.Identity, scale=ccols[:, 2, ds(col, 1)],
                               bias=ccols[:, 3, ds(col, 1)]).then_inc(f_c0, 1)
                act.copy(ustate[:, 0:2, col], ext[:, e, TP:TP + 2])
                act.copy(ustate[:, 2:4, col], ext[:, e, E2 - 2:E2]).then_inc(f_us, 1)

            def gate(f, pair):
                act.wait_ge(f_conv, pair * 2 + 1)
                act.activation(gth[:, 0:T + 2], cbuf[:, 0, 0:T + 2], ACT.Tanh, scale=0.5).then_inc(f_th, 1)
                act.wait_ge(f_y, pair + 2)
                act.activation(yhi[:, f, :], ybuf[:, :], ACT.Copy, scale=0.5).then_inc(f_hi, 1)

            def up(g, f, first):
                pl = place(U_F + g * UF_G, T_F + g * TF_G, f, 4, 2)
                pair = f + g * GT
                split(pl, 0, 1)
                if not first:
                    gate(f - 1, pair - 1)
                conv_inputs(pl, 0, pair, pair)
                split(pl, 2, 3)
                conv_inputs(pl, 1, pair, pair + FT)

            def h_tail(pl, e, k):
                square(pl, e, k, k + (KT + 2))
                act.activation(hg[:, k, :], hT[:, k, :], ACT.Identity, scale=gcols[:, 3, ds(k, 1)]).then_inc(h_g, 1)

            for g in range(GROUPS):
                up(g, 0, True)
                with act.Fori(1, GT) as f:
                    up(g, f, False)
                gate(GT - 1, g * GT + (GT - 1))
                u0, t0 = U_F + g * UF_G + 4 * GT, T_F + g * TF_G + 2 * GT
                if g < GROUPS - 1:
                    with act.Fori(0, KT // 2) as i:
                        split(place(u0, t0, i, 4, 2), 0, 1, 2, 3)
            pl = place(u0, t0)
            split(pl, 0, 1, 2, 3)
            h_tail(pl, 0, 0)
            with act.Fori(1, KT // 2 - 1) as i:
                pl = place(u0, t0, i, 4, 2)
                split(pl, 0, 1)
                h_tail(place(u0 - 4, t0 - 2, i, 4, 2), 1, i * 2 - 1)
                split(pl, 2, 3)
                h_tail(pl, 0, i * 2)
            pl = place(UNITS - 4, T_END - 2)
            split(pl, 0, 1)
            h_tail(place(UNITS - 8, T_END - 4), 1, KT - 3)
            for e in range(2):
                h_tail(pl, e, KT - 2 + e)

            root(4, 3)
            act.wait_ge(u_T, 1)
            act.copy(cvo[0:2 * FT, :, :], M[1][0:2 * FT, :].rearrange("p (j c) -> p j c", j=4)).then_inc(u_tok, 1)
            act.wait_ge(n_T, 1)
            act.copy(nrow2[0:MH, :], M[2][0:MH, 0:2 * P]).then_inc(n_tok, 1)
            act.wait_ge(f_rms, 2)
            for n in range(0, 12, 2):
                u, q = n // 4, n % 4
                rows = P if u < 2 else TS
                act.wait_ge(y_T, n + 1)
                act.activation(ytok[0:rows, u, q * 4 * P:(q + 1) * 4 * P], M[n % 4][0:rows, :], ACT.Identity,
                               scale=fnv[0:rows, 2, u:u + 1]).then_inc(y_act, 1)

        @block.vector
        def _(dve):
            own = Steps(dve, dve_own)
            dve.sem_inc(w_lo, RING)
            dve.sem_inc(c_lo, 2)
            for s_ in (m_sum, m_lo, f_y, f_lo):
                dve.sem_inc(s_, 1)
            f32 = lambda ap: ap.bitcast(F32)

            def split(pl, *units):
                for j in units:
                    j += LEAD
                    dve.wait_ge(w_hi, pl.split(j))
                    dve.tensor_tensor(wlo[:, pl.slot(j), :, :], raw[:, pl.slot(j), :, :],
                                      f32(whi[:, pl.slot(j), :, :]), ALU.subtract).then_inc(w_lo, 1)

            def read_tile(pl, t, j, out, m=P, n=T):
                dve.wait_ge(w_used, pl.through(j))
                dve.tensor_copy(out, G[t % 2][0:m, 0:n]).then_inc(bank_read[t % 2], 1)

            def lo_part(out, x, hi, done):
                dve.tensor_tensor(out, x, f32(hi), ALU.subtract).then_inc(done, 1)

            def copy_tokens(n0, n1, out_of):
                for n in range(n0 + 1, n1, 2):
                    dve.wait_ge(xp_done, n + 1)
                    dve.tensor_copy(*out_of(n)).then_inc(xp_dve, 1)

            def norm_scale(which, n, bank, v, x, sq, gain):
                rms(which, n, bank, v)
                own.settle()
                with dve.Fori(0, KT) as k:
                    dve.scalar_tensor_tensor(sq[:, k, 0:n], x[:, k, 0:n], gcols[:, gain, ds(k, 1)], v[:, 2, 0:n],
                                             ALU.mult, ALU.mult).then_inc(n_x, 1)

            def rms(which, n, bank, v):
                dve.wait_ge(sums, which + 1)
                dve.tensor_scalar(v[:, 0, 0:n], bank[:, 0:n], 1.0 / D, EPS, ALU.mult, ALU.add).then_inc(variances, 1)
                dve.wait_ge(roots, which + 1)
                own.did(dve.reciprocal(v[:, 2, 0:n], v[:, 1, 0:n]))
                own.settle()
                own.did(dve.tensor_tensor(v[:, 1, 0:n], v[:, 2, 0:n], v[:, 2, 0:n], ALU.mult))
                own.settle()
                own.did(dve.tensor_tensor(v[:, 1, 0:n], v[:, 1, 0:n], v[:, 0, 0:n], ALU.mult))
                own.settle()
                own.did(dve.tensor_scalar(v[:, 1, 0:n], v[:, 1, 0:n], -0.5, 1.5, ALU.mult, ALU.add))
                own.settle()
                own.did(dve.tensor_tensor(v[:, 2, 0:n], v[:, 2, 0:n], v[:, 1, 0:n], ALU.mult))

            def norm_lo(which, n, hi, lo, sq):
                with dve.Fori(0, KT) as k:
                    dve.wait_ge(n_hi, k + (which * KT + 1))
                    lo_part(lo[:, k, 0:n], sq[:, k, 0:n], hi[:, k, 0:n], n_lo)

            dve.wait_ge(rows_T, 1)
            dve.tensor_copy(ccols[:, 0:3, :], M[4][:, 0:264].rearrange("p (j f) -> p j f", j=3))
            dve.tensor_copy(ccols[:, 3:6, :], M[5][:, 64:328].rearrange("p (j f) -> p j f", j=3))
            dve.tensor_copy(gcols[:, :, :], M[5][:, 0:64].rearrange("p (g k) -> p g k", g=4))
            dve.tensor_copy(mst[:, :], M[5][:, 400:408])
            dve.tensor_copy(nst[:, :], M[5][:, 408:416]).then_inc(rows_out, 1)

            copy_tokens(0, 8, lambda n: (memT[:, 2 * n:2 * n + 2, :], M[n % 4][:, :].rearrange("p (e m) -> p e m", e=2)))
            dve.wait_ge(rows_out, 1)
            norm_scale(0, NMEM, M[4], nv, memT, msq, 1)
            norm_lo(0, NMEM, mhi, mlo, msq)
            pl = place(U_C, T_C)
            split(pl, -2, -1)
            copy_tokens(8, 24, lambda n: (xT[:, n - 8, :], M[n % 4][:, 0:T]))
            norm_scale(1, T, M[5], nv, xT, xsq, 0)

            def c_keys(h):
                dve.wait_ge(c_xp, h + 1)
                dve.tensor_copy(ckT[:, :, :], M[1][:, :].rearrange("p (d m) -> p d m", d=2)).then_inc(c_ckT, 1)

            def c_softmax(h):
                dve.wait_ge(c_sc, h + 1)
                dve.tensor_reduce(c_st[:, 0, 0:2], M[3][:, :].rearrange("p (u m) -> p u m", u=2), AX.X, ALU.max)
                own.did(dve.tensor_reduce(c_st[0:TS, 0, 2:3], M[4][0:TS, 0:NMEM], AX.X, ALU.max))
                own.settle()
                dve.tensor_scalar(c_st[:, 1, 0:2], c_st[:, 0, 0:2], -1.0 / 16, None, ALU.mult)
                dve.tensor_scalar(c_st[0:TS, 1, 2:3], c_st[0:TS, 0, 2:3], -1.0 / 16, None, ALU.mult).then_inc(c_nm, 1)
                dve.wait_ge(c_exp, h + 1)
                dve.reciprocal(c_st[:, 3, 0:2], c_st[:, 2, 0:2])
                own.did(dve.reciprocal(c_st[0:TS, 3, 2:3], c_st[0:TS, 2, 2:3]))
                own.settle()
                for u in range(2):
                    dve.tensor_scalar(c_p[:, u, :], c_p[:, u, :], c_st[:, 3, u:u + 1], None, ALU.mult)
                dve.tensor_scalar(c_p[0:TS, 2, :], c_p[0:TS, 2, :], c_st[0:TS, 3, 2:3], None, ALU.mult).then_inc(c_pn, 1)

            def c_pT1(h):
                dve.wait_ge(c_pt, h + 1)
                dve.tensor_copy(c_pT[:, 1, :], M[2][:, 0:T]).then_inc(c_pTd, 1)

            def c_los(h):
                for d in range(2):
                    dve.wait_ge(c_hi, h * 2 + (d + 1))
                    lo_part(blo[2][:, h * 2 + d, :], M[3 + d][:, 0:T], bhi[2][:, h * 2 + d, :], c_lo)
            c_stages = (c_keys, c_softmax, c_pT1, c_los)

            def c_tiles(pl, stages, shifted):
                for t in range(6):
                    split(pl, 2 * t, 2 * t + 1)
                    if t % 2 == 1:
                        if t == 1 and shifted is not None:
                            dve.wait_ge(c_shift, shifted)
                        read_tile(pl, t, 2 * t + 1, (mk_n[:, 1, :], mv_n[:, 1, :], cq_n[:, 1, :])[t // 2],
                                  n=NMEM if t < 4 else T)
                    if t < len(stages):
                        stages[t]()
            norm_lo(1, T, xhi, xlo, xsq)
            dve.wait_ge(xT_out, 16)
            c_tiles(pl, [], None)
            with own.loop(1, CHD, 2) as h:
                c_tiles(place(U_C, T_C, h, 12, 6), [lambda: c_keys(h - 1), lambda: c_softmax(h - 1),
                                                    lambda: c_pT1(h - 1), lambda: c_los(h - 1)], h)

            def rope(x, bank, cos, sin, tmp, out, done, *waits):
                for w in waits:
                    dve.wait_ge(*w)
                own.did(dve.tensor_tensor(tmp, bank[:, 0:T], sin, ALU.mult))
                own.did(dve.tensor_tensor(x, x, cos, ALU.mult))
                own.settle()
                for n, (dst, lo, hi) in enumerate(out):
                    last = dve.tensor_tensor(dst, tmp[:, lo:hi], x[:, lo:hi], ALU.add)
                last.then_inc(done, 1)
            cos64, sin64 = K[:, C_COS64:C_COS64 + T], K[:, C_SIN64:C_SIN64 + T]
            cos128, sin128 = K[:, C_COS128:C_COS128 + T], K[:, C_SIN128:C_SIN128 + T]
            pl = place(U_B, T_B)
            for t in range(10):
                split(pl, 2 * t, 2 * t + 1)
                if t % 2 == 1:
                    if t == 3:
                        read_tile(pl, t, 7, kiw[0:72, :], 72)
                    else:
                        if t >= 7:
                            dve.wait_ge(b_rope, t - 5)
                        read_tile(pl, t, 2 * t + 1, vraw[:, 1, :] if t == 1 else rin[:, 1, :])
                if t < 4:
                    c_stages[t](CHD - 1)
                if t == 4:
                    dve.wait_ge(b_gx, 1)
                    dve.tensor_scalar(iw[:, 0:2, :], M[2][:, 0:144].rearrange("p (u c) -> p u c", u=2)[:, :, 64:72],
                                      IH ** -0.5, None, ALU.mult)
                    dve.tensor_scalar(iw[0:TS, 2, :], M[2][0:TS, 208:216], IH ** -0.5, None, ALU.mult).then_inc(b_iw, 1)
                if t == 5:
                    dve.wait_ge(b_kix, 1)
                    own.did(dve.tensor_tensor(ki2[:, :], M[3][:, 0:T], cos64, ALU.mult))
                    own.did(dve.tensor_tensor(rtmp[:, :], M[4][:, 0:T], sin64, ALU.mult))
                    own.settle()
                    dve.tensor_tensor(ki2[:, :], ki2[:, :], rtmp[:, :], ALU.add).then_inc(b_ki, 1)
                if t >= 5:
                    n = t - 5
                    bank = M[(0, 1, 2, 5, 0)[n]]
                    if n < 4:
                        rope(rin[:, (t - 1) % 2, :], bank, cos64, sin64, rtmp[:, :], [(iqT[:, n, :], 0, T)], b_rope,
                             (b_rot, n + 1), (b_rope, n) if n else (b_ki, 1))
                    else:
                        rope(rin[:, 0, :], bank, cos128, sin128, rtmp[:, :],
                             [(kTp[:, 0, :], 0, TP), (kTs[:, 0, PAST:SS], TP, T)], b_rope, (b_rot, 5), (b_rope, 4))
                if t == 8:
                    dve.wait_ge(g_l, 1)
                    dve.scalar_tensor_tensor(g2[0:CH, :, :], igf[0:CH, :, MH:2 * MH], 0.0, g1[0:CH, :, :],
                                             ALU.min, ALU.subtract).then_inc(g_lf, 1)

            def over(ap, n):
                return ap.unsqueeze(2).broadcast_to([ap.shape[0], ap.shape[1], n])

            def a_decay(h):
                dve.wait_ge(a_s0, h + 1)
                dve.tensor_tensor(SD[0:CH, :, :], M[0][0:CH, 0:T].rearrange("p (c s) -> p c s", c=NCH),
                                  Dm[0:CH, :, h, :], ALU.mult).then_inc(a_sd, 1)
                dve.tensor_tensor(kw[0:CH, 0:4, :], M[1][0:CH, :].rearrange("p (c d) -> p c d", c=4),
                                  over(wexp[0:CH, 0:4, h], P), ALU.mult)
                dve.wait_ge(a_vn, h + 1)
                dve.tensor_scalar(kw[0:CH, 4, :], M[3][0:CH, 0:P], wexp[0:CH, 4, ds(h, 1)], None, ALU.mult)\
                   .then_inc(a_kw, 1)
                dve.wait_ge(a_sd, h + 1)
                own.did(dve.tensor_reduce(a_st[0:CH, 0, 0:NCH], SD[0:CH, :, :], AX.X, ALU.add))

            def a_recur(h):
                dve.wait_ge(a_s1, h + 1)
                dve.wait_ge(a_vn, h + 1)
                for c in range(NCH):
                    src, dst = (c, c + 1) if c < 4 else (5, 6)
                    kv = M[1][:, c * P:c * P + P] if c < 4 else M[3][:, 0:P]
                    d = dec[:, c, ds(h, 1)]
                    dve.scalar_tensor_tensor(Cst[:, dst, 0:P], Cst[:, src, 0:P], d, kv, ALU.mult, ALU.add)
                    own.did(dve.scalar_tensor_tensor(Cst[:, dst, P:P + 1], Cst[:, src, P:P + 1], d, M[5][:, c:c + 1],
                                                     ALU.mult, ALU.add))
                    own.settle()
                dve.tensor_copy(nout[:, 0, ds(h, 1)], Cst[:, 4, P:P + 1])
                dve.tensor_copy(nout[:, 1, ds(h, 1)], Cst[:, 6, P:P + 1]).then_inc(a_C, 1)

            def a_combine(h):
                dve.wait_ge(a_s2, h + 1)
                den, ih = a_st[0:CH, 1, 0:NCH], inter[0:CH, :, h]
                own.did(dve.tensor_tensor(den, M[5][0:CH, 8:8 + NCH], ih, ALU.mult))
                dve.tensor_tensor(hn[0:CH, 0:4, :], M[4][0:CH, :].rearrange("p (c v) -> p c v", c=4),
                                  over(inter[0:CH, 0:4, h], P), ALU.mult)
                own.did(dve.tensor_scalar(hn[0:CH, 4, :], M[5][0:CH, 2 * P:3 * P], inter[0:CH, 4, ds(h, 1)], None, ALU.mult))
                own.settle()
                own.did(dve.tensor_tensor(den, den, a_st[0:CH, 0, 0:NCH], ALU.add))
                dve.tensor_tensor(hn[0:CH, 0:4, :], hn[0:CH, 0:4, :], M[2][0:CH, :].rearrange("p (c v) -> p c v", c=4), ALU.add)
                own.did(dve.tensor_tensor(hn[0:CH, 4, :], hn[0:CH, 4, :], M[5][0:CH, P:2 * P], ALU.add))
                own.settle()
                own.did(dve.scalar_tensor_tensor(den, den, -1.0, den, ALU.mult, ALU.max))
                own.settle()
                own.did(dve.tensor_tensor(den, den, enm[0:CH, :, h], ALU.max))
                own.settle()
                own.did(dve.reciprocal(den, den))
                own.settle()
                dve.tensor_tensor(hn[0:CH, :, :], hn[0:CH, :, :], over(den, P), ALU.mult).then_inc(a_h, 1)

            def a_gate(h):
                dve.wait_ge(a_s3, h + 1)
                dve.scalar_tensor_tensor(ga[:, :], s_c, 1.0, M[4][:, 0:T], ALU.add, ALU.mult).then_inc(a_ga, 1)
                dve.wait_ge(a_hi, h + 1)
                dve.scalar_tensor_tensor(blo[0][:, h, :], ga[:, :], 0.5, f32(bhi[0][:, h, :]), ALU.mult, ALU.subtract)\
                   .then_inc(a_lo, 1)
            a_stages = (a_decay, a_recur, a_combine, a_gate)

            def scores_u(u):
                rows, n_ = (P, TP) if u < 2 else (TS, SS)
                own.settle()
                for h in range(IH):
                    n = u * IH + h
                    dve.wait_ge(i_relu, n + 1)
                    w = iw[0:rows, u, h:h + 1]
                    if h == 0:
                        dve.tensor_scalar(score[0:rows, 0:n_], rl[0:rows, 0, 0:n_], w, None, ALU.mult).then_inc(i_acc, 1)
                    else:
                        dve.wait_ge(i_acc, n)
                        dve.scalar_tensor_tensor(score[0:rows, 0:n_], rl[0:rows, h % 2, 0:n_], w, score[0:rows, 0:n_],
                                                 ALU.mult, ALU.add).then_inc(i_acc, 1)

            def select_u(u):
                rows, n_, k = (P, TP, TOPK_P) if u < 2 else (TS, SS, TOPK_S)
                sc = score[0:rows, 0:n_]
                dve.wait_ge(i_acc, u * IH + IH)
                if u < 2:
                    own.did(dve.tensor_tensor(sc, sc, K[0:rows, C_ADM + u * TP:C_ADM + (u + 1) * TP], ALU.add))
                    own.settle()
                for _ in range(k // 8):
                    own.did(dve.max(top8[0:rows, :], sc))
                    own.settle()
                    own.did(dve.match_replace(sc, top8[0:rows, :], sc, TAKEN))
                    own.settle()
                own.did(dve.tensor_scalar(msk[0:rows, u * TP:u * TP + n_], sc, -2e38, NEG, ALU.is_gt, ALU.mult))

            pl = place(U_A, T_A)
            for t in range(4):
                split(pl, 2 * t, 2 * t + 1)
                if t == 1:
                    dve.wait_ge(w_used, pl.through(3))
                    dve.tensor_scalar(a_nxt[:, 1, :], G[1][:, 0:T], P ** -0.5, None, ALU.mult).then_inc(bank_read[1], 1)
                if t == 0:
                    rope(rin[:, 1, :], M[1], cos128, sin128, rtmp[:, :],
                         [(kTp[:, 1, :], 0, TP), (kTs[:, 1, PAST:SS], TP, T)], b_rope, (b_rot, 6), (b_rope, 5))
                    dve.wait_ge(g_b, 1)
                    own.did(dve.tensor_copy(bcs[0:CH, :, :], M[5][0:CH, 0:NCH * MH].rearrange("p (c h) -> p c h", c=NCH)))
                    own.settle()
                    own.did(dve.tensor_tensor(acs[0:CH, :, :], igf[0:CH, :, 0:MH], bcs[0:CH, :, :], ALU.subtract))
                    own.settle()
                if t == 1:
                    eye = ident[0:CH, 0:CH].unsqueeze(1).broadcast_to([CH, MH, CH])
                    caus = K[0:CH, C_CAUS:C_CAUS + CH].unsqueeze(1).broadcast_to([CH, MH, CH])
                    for c in range(NCH):
                        if c >= 1:
                            dve.wait_ge(g_R, c)
                        dve.tensor_tensor(diag[0:CH, :, :], eye, over(acs[0:CH, c, :], CH), ALU.mult).then_inc(g_dg, 1)
                        dve.wait_ge(g_R, c + 1)
                        dve.tensor_tensor(Dm[0:CH, c, :, :],
                                          M[3 if c % 2 else 5][0:CH, :].rearrange("p (h s) -> p h s", h=MH),
                                          over(bcs[0:CH, c, :], CH), ALU.add).then_inc(g_D, 1)
                        dve.wait_ge(g_D, c + 1)
                        own.did(dve.tensor_tensor(Dm[0:CH, c, :, :], Dm[0:CH, c, :, :], caus, ALU.add))
                        own.settle()
                        own.did(dve.tensor_reduce(mxs[0:CH, c, :], Dm[0:CH, c, :, :], AX.X, ALU.max))
                if t == 2:
                    scores_u(0)
                    for c in range(NCH):
                        own.settle()
                        if c == 0:
                            own.did(dve.tensor_copy(mint[0:CH, 0, :], bcs[0:CH, 0, :]))
                        else:
                            before = mst[:, :] if c == 4 else mnew[:, c - 1, :]
                            own.did(dve.tensor_tensor(mint[0:CH, c, :], bcs[0:CH, c, :], before[0:CH, :], ALU.add))
                        own.settle()
                        dve.tensor_tensor(mb[0:CH, c, 0, :], mint[0:CH, c, :], mxs[0:CH, c, :], ALU.max)
                        dve.tensor_copy(mb[0:CH, c, 1, :], bcs[0:CH, c, :]).then_inc(g_mb, 1)
                        dve.wait_ge(g_last, c + 1)
                        dve.tensor_copy(blast[:, c, :], M[3][:, 16 * c + 8:16 * c + 16])
                        own.did(dve.tensor_copy(mnew[:, c, :], M[3][:, 16 * c:16 * c + 8]))
                        own.settle()
                        if c == 0:
                            own.did(dve.tensor_tensor(dec[:, c, :], blast[:, c, :], mnew[:, c, :], ALU.subtract))
                        else:
                            own.did(dve.tensor_tensor(dec[:, c, :], blast[:, c, :], before, ALU.add))
                            own.settle()
                            own.did(dve.tensor_tensor(dec[:, c, :], dec[:, c, :], mnew[:, c, :], ALU.subtract))
                    own.settle()
                    m_t = mb[0:CH, :, 0, :]
                    own.did(dve.tensor_tensor(inter[0:CH, :, :], mint[0:CH, :, :], m_t, ALU.subtract))
                    own.did(dve.tensor_scalar(enm[0:CH, :, :], m_t, -1.0, None, ALU.mult))
                    own.did(dve.tensor_tensor(wexp[0:CH, :, :], blast[0:CH, :, :], mnew[0:CH, :, :], ALU.subtract))
                    own.settle()
                    dve.tensor_tensor(wexp[0:CH, :, :], wexp[0:CH, :, :], acs[0:CH, :, :], ALU.add).then_inc(g_arg, 1)
                    for c in range(NCH):
                        last = dve.tensor_tensor(Dm[0:CH, c, :, :], Dm[0:CH, c, :, :], over(mb[0:CH, c, 0, :], CH),
                                                 ALU.subtract)
                    last.then_inc(g_Da, 1)
                if t == 3:
                    select_u(0)
                    scores_u(1)
                    select_u(1)
                    scores_u(2)
                    select_u(2)
            dve.wait_ge(a_shift, 1)
            own.did(dve.memset(Cst[:, 0, :], 0.0))
            own.settle()
            dve.wait_ge(g_exp, 1)
            dve.wait_ge(g_De, 1)
            with own.loop(1, MH, 13) as h:
                pl = place(U_A, T_A, h, 8, 4)
                for t in range(4):
                    split(pl, 2 * t, 2 * t + 1)
                    if t == 1:
                        dve.wait_ge(a_shift, h)
                        dve.wait_ge(w_used, pl.through(3))
                        dve.tensor_scalar(a_nxt[:, 1, :], G[1][:, 0:T], P ** -0.5, None, ALU.mult).then_inc(bank_read[1], 1)
                    a_stages[t](h - 1)

            own.settle()

            def q_softmax(i):
                for e in range(2):
                    p_, s_, st = sp_[:, e, :], ss_[0:TS, e, :], q_st[:, e, :, :]
                    dve.wait_ge(q_sc, i * 2 + (e + 1))
                    dve.scalar_tensor_tensor(p_, M[2 * e][:, :], P ** -0.5, msk[:, 0:2 * TP], ALU.mult, ALU.add)
                    own.did(dve.scalar_tensor_tensor(s_, M[2 * e + 1][0:TS, 0:SS], P ** -0.5, msk[0:TS, 2 * TP:2 * TP + SS],
                                                     ALU.mult, ALU.add))
                    own.settle()
                    dve.tensor_reduce(st[:, 0, 0:2], p_.rearrange("p (u s) -> p u s", u=2), AX.X, ALU.max)
                    own.did(dve.tensor_reduce(st[0:TS, 0, 2:3], s_, AX.X, ALU.max))
                    own.settle()
                    dve.tensor_scalar(st[:, 1, 0:2], st[:, 0, 0:2], -1.0, None, ALU.mult)
                    dve.tensor_scalar(st[0:TS, 1, 2:3], st[0:TS, 0, 2:3], -1.0, None, ALU.mult).then_inc(q_nm, 1)
                for e in range(2):
                    st = q_st[:, e, :, :]
                    dve.wait_ge(q_exp, i * 2 + (e + 1))
                    dve.reciprocal(st[:, 3, 0:2], st[:, 2, 0:2])
                    own.did(dve.reciprocal(st[0:TS, 3, 2:3], st[0:TS, 2, 2:3]))
                    own.settle()
                    for u in range(2):
                        p_ = sp_[:, e, u * TP:(u + 1) * TP]
                        dve.tensor_scalar(p_, p_, st[:, 3, u:u + 1], None, ALU.mult)
                    dve.tensor_scalar(ss_[0:TS, e, :], ss_[0:TS, e, :], st[0:TS, 3, 2:3], None, ALU.mult).then_inc(q_pn, 1)

            def q_ropes(i, first=False):
                for e in range(2):
                    before = [] if first and e == 0 else [(q_rope, i * 2 + e)]
                    rope(q_raw[:, e, :], M[2 * e], cos128, sin128, q_tmp[:, :], [(q_nxt[:, e, :], 0, T)], q_rope,
                         (q_rot, i * 2 + (e + 1)), *before)

            def q_los(i):
                for e in range(2):
                    dve.wait_ge(q_hi, i * 2 + (e + 1))
                    lo_part(blo[1][:, i * 2 + e, :], M[4 + e][:, 0:T], bhi[1][:, i * 2 + e, :], q_lo)

            pl = place(U_Q, T_Q)
            split(pl, 0, 1)
            a_decay(MH - 1)
            a_recur(MH - 1)
            split(pl, 2, 3)
            read_tile(pl, 1, 3, q_raw[:, 1, :])
            a_combine(MH - 1)
            a_gate(MH - 1)
            q_ropes(0, True)
            with own.loop(1, AH // 2, 10) as i:
                pl = place(U_Q, T_Q, i, 4, 2)
                split(pl, 0, 1)
                q_softmax(i - 1)
                split(pl, 2, 3)
                dve.wait_ge(q_rope, i * 2)
                read_tile(pl, 1, 3, q_raw[:, 1, :])
                dve.wait_ge(q_shift, i)
                q_ropes(i)
                q_los(i - 1)
            q_softmax(AH // 2 - 1)
            q_los(AH // 2 - 1)

            with own.loop(0, KT // 4, 4) as i:
                pl = place(U_G, T_G, i, 36, 24)
                for n in range(4):
                    for b in range(3):
                        split(pl, 9 * n + 2 * b, 9 * n + 2 * b + 1)
                    for b in range(3):
                        t = 6 * n + 3 + b
                        split(pl, 9 * n + 6 + b)
                        dve.wait_ge(w_used, pl.through(9 * n + 6 + b))
                        if b == 0:
                            dve.wait_ge(m_lo, i * 4 + (n + 1))
                        dve.scalar_tensor_tensor(gtmp[:, :] if b else acc[:, :], th[:, b, :], 1.0, G[t % 2][:, 0:T],
                                                 ALU.add, ALU.mult).then_inc(bank_read[t % 2], 1)
                        dve.wait_ge(bank_read[t % 2], pl.bank_read(t))
                        if b:
                            add = dve.tensor_tensor(acc[:, :], acc[:, :], gtmp[:, :], ALU.add)
                            if b == 1:
                                own.did(add)
                                own.settle()
                            else:
                                add.then_inc(m_sum, 1)
                    dve.wait_ge(m_hi, i * 4 + (n + 1))
                    dve.scalar_tensor_tensor(mglo[:, i * 4 + n, :], acc[:, :], 0.5, f32(mghi[:, i * 4 + n, :]),
                                             ALU.mult, ALU.subtract).then_inc(m_lo, 1)

            def add_h(pl, e, k):
                dve.wait_ge(w_used, pl.through(2 * e + 1))
                dve.tensor_tensor(hT[:, k, :], hT[:, k, :], G[e][:, 0:T], ALU.add).then_inc(bank_read[e], 1)

            def add_square(squared, summed):
                dve.wait_ge(h_sq, squared)
                dve.wait_ge(h_sum, summed)
                dve.tensor_tensor(hacc[:, 0:T], hacc[:, 0:T], h2[:, :], ALU.add).then_inc(h_sum, 1)

            dve.memset(hacc[:, :], 0.0).then_inc(h_sum, 1)
            dve.wait_ge(hT_in, 16)
            with dve.Fori(0, KT // 2) as i:
                pl = place(U_O, T_O, i, 4, 2)

                def parts(e):
                    k = i * 2 + e
                    add_square(i * 2 + (e + 1), i * 2 + (e + 1))
                    dve.wait_ge(h_hi, i * 2 + (e + 1))
                    dve.scalar_tensor_tensor(xlo[:, k, :], hT[:, k, :], gcols[:, 2, ds(k, 1)], f32(xhi[:, k, :]),
                                             ALU.mult, ALU.subtract).then_inc(h_lo, 1)
                split(pl, 0, 1)
                add_h(pl, 0, i * 2)
                split(pl, 2, 3)
                parts(0)
                add_h(pl, 1, i * 2 + 1)
                parts(1)
            own.did(dve.memset(ext[:, :, 0:2], 0.0))
            rms(2, T, M[0], fnv)
            own.settle()

            def taps(e, pair, col, pl):
                dve.wait_ge(w_used, pl.through(2 * e + 1))
                dve.wait_ge(f_us, pair * 2 + (e + 1))
                dve.tensor_tensor(ext[:, e, 2:2 + TP], G[e][:, 0:TP], fnv[:, 2, 0:TP], ALU.mult)
                dve.tensor_tensor(ext[:, e, TP + 4:E2], G[e][:, TP:T], fnv[:, 2, TP:T], ALU.mult).then_inc(bank_read[e], 1)
                dve.wait_ge(bank_read[e], pl.bank_read(e))
                dve.wait_ge(f_c0, pair * 2 + (e + 1))
                c = cbuf[:, e, 0:T + 2]
                own.did(dve.scalar_tensor_tensor(c, ext[:, e, 1:T + 3], ccols[:, 1, ds(col, 1)], c, ALU.mult, ALU.add))
                own.settle()
                dve.scalar_tensor_tensor(c, ext[:, e, 0:T + 2], ccols[:, 0, ds(col, 1)], c, ALU.mult, ALU.add)\
                   .then_inc(f_conv, 1)

            def gate(f, pair):
                dve.wait_ge(f_th, pair + 1)
                own.did(dve.scalar_tensor_tensor(gth[:, 0:T + 2], gth[:, 0:T + 2], 1.0, cbuf[:, 0, 0:T + 2],
                                                 ALU.add, ALU.mult))
                dve.wait_ge(f_conv, pair * 2 + 2)
                own.settle()
                dve.wait_ge(f_lo, pair + 1)
                own.did(dve.tensor_tensor(ybuf[:, 0:TP], gth[:, 0:TP], cbuf[:, 1, 0:TP], ALU.mult))
                dve.tensor_tensor(ybuf[:, TP:T], gth[:, TP + 2:T + 2], cbuf[:, 1, TP + 2:T + 2], ALU.mult).then_inc(f_y, 1)
                dve.wait_ge(f_hi, pair + 1)
                dve.scalar_tensor_tensor(ylo[:, f, :], ybuf[:, :], 0.5, f32(yhi[:, f, :]), ALU.mult, ALU.subtract)\
                   .then_inc(f_lo, 1)

            def up(g, f, first):
                pl = place(U_F + g * UF_G, T_F + g * TF_G, f, 4, 2)
                pair = f + g * GT
                split(pl, 0, 1)
                if not first:
                    gate(f - 1, pair - 1)
                taps(0, pair, pair, pl)
                split(pl, 2, 3)
                taps(1, pair, pair + FT, pl)

            for g in range(GROUPS):
                up(g, 0, True)
                with own.loop(1, GT, 4) as f:
                    up(g, f, False)
                gate(GT - 1, g * GT + (GT - 1))
                u0, t0 = U_F + g * UF_G + 4 * GT, T_F + g * TF_G + 2 * GT
                if g < GROUPS - 1:
                    with dve.Fori(0, KT // 2) as i:
                        pl = place(u0, t0, i, 4, 2)
                        for e in range(2):
                            split(pl, 2 * e, 2 * e + 1)
                            add_h(pl, e, i * 2 + e)
            dve.wait_ge(variances, 3)
            dve.memset(hacc[:, :], 0.0).then_inc(h_sum, 1)
            pl = place(u0, t0)
            split(pl, 0, 1)
            add_h(pl, 0, 0)
            split(pl, 2, 3)
            add_square(KT + 1, KT + 2)
            add_h(pl, 1, 1)
            with dve.Fori(1, KT // 2 - 1) as i:
                pl = place(u0, t0, i, 4, 2)
                split(pl, 0, 1)
                add_square(i * 2 + KT, i * 2 + (KT + 1))
                add_h(pl, 0, i * 2)
                split(pl, 2, 3)
                add_square(i * 2 + (KT + 1), i * 2 + (KT + 2))
                add_h(pl, 1, i * 2 + 1)
            pl = place(UNITS - 4, T_END - 2)
            split(pl, 0, 1)
            add_square(2 * KT - 2, 2 * KT - 1)
            for e in range(2):
                add_h(pl, e, KT - 2 + e)
                add_square(2 * KT - 1 + e, 2 * KT + e)
            rms(3, 3, M[5], fnv)
            dve.wait_ge(dve_own, own.n)
            dve.sem_inc(f_rms, 2)
            for n in range(1, 12, 2):
                u, q = n // 4, n % 4
                rows = P if u < 2 else TS
                dve.wait_ge(y_T, n + 1)
                dve.tensor_scalar(ytok[0:rows, u, q * 4 * P:(q + 1) * 4 * P], M[n % 4][0:rows, :],
                                  fnv[0:rows, 2, u:u + 1], None, ALU.mult).then_inc(y_dve, 1)

        @block.gpsimd
        def _(pool):
            def wait(s_, value):
                pool.wait_ge(s_, value)
                pool.sem_inc(pool_passed, 1)
            mk_src = a["cache_mem_k"][0, 0].rearrange("(m p) h d -> h p m d", p=P)
            mv_src = a["cache_mem_v"][0, 0].rearrange("(m p) h d -> h p m d", p=P)
            mk_dst = o["p_mem_k"][0, 0].rearrange("(m p) h d -> h p m d", p=P)
            mv_dst = o["p_mem_v"][0, 0].rearrange("(m p) h d -> h p m d", p=P)

            def c_load(h):
                pool.dma_start(ck[:, :, :], mk_src[h]).then_inc(c_cache, 16)
                pool.dma_start(cv[:, :, :], mv_src[h]).then_inc(c_cache, 16)

            def c_move(h):
                pl = place(U_C, T_C, h, 12, 6)
                wait(bank_read[0], pl.bank_read(4))
                wait(bank_read[1], pl.bank_read(5))
                pool.tensor_copy(c_cur[:, :], c_nxt[:, :]).then_inc(c_shift, 1)

            def c_store(h):
                wait(c_mvn, h + 1)
                pool.dma_start(mv_dst[h], mvn[:, :, :]).then_inc(c_out, 16)
                wait(c_mkn, h + 1)
                pool.dma_start(mk_dst[h], mkn[:, :, :]).then_inc(c_out, 16)

            pool.wait_ge(n_x, 2 * KT)
            pool.wait_ge(xT_out, 16)
            c_load(0)
            pool.dma_start(cvB[:, :, :], a["cache_dsa_v"][0, 0].rearrange("(u p) j d -> p u (j d)", p=P)).then_inc(cache_in, 16)
            c_move(0)
            with pool.Fori(1, CHD) as h:
                c_store(h - 1)
                wait(c_pv, h * 2 + 2)
                c_load(h)
                wait(c_out, h * 32)
                c_move(h)
            pool.dma_start(ckB[:, :, :], a["cache_dsa_k"][0, 0].rearrange("(u p) j d -> p u (j d)", p=P)).then_inc(cache_in, 16)
            for n in range(2):
                pool.dma_start(ckI[:, :, n, :], a["cache_dsa_kidx"][0, 0].rearrange("(u p) d -> p u d", p=P))\
                    .then_inc(cache_in, 16)
            c_store(CHD - 1)

            def store(dst_p, dst_s, src_p, src_s, done):
                pool.dma_start(dst_p.rearrange("(u p) n -> p u n", p=P), src_p).then_inc(done, 16)
                pool.dma_start(dst_s, src_s).then_inc(done, 16)

            pool.wait_ge(b_v, 1)
            store(o["p_v"][0, 0].rearrange("t j d -> t (j d)"), o["s_v"][0, 0].rearrange("t j d -> t (j d)"),
                  vnp[:, :, :], vns[0:TS, :], b_vo)
            pool.wait_ge(b_ko, 1)
            store(o["p_k"][0, 0].rearrange("t j d -> t (j d)"), o["s_k"][0, 0].rearrange("t j d -> t (j d)"),
                  kout[:, 0:2, :], kout[0:TS, 2, :], b_kio)
            store(o["p_kidx"][0, 0], o["s_kidx"][0, 0], kiout[:, 0:2, :], kiout[0:TS, 2, :], b_kio)
            pool.wait_ge(g_arg, 1)
            pool.dma_start(o["p_m"][0], mnew[0:1, 3, :]).then_inc(g_mo, 16)
            pool.dma_start(o["s_m"][0], mnew[0:1, 4, :]).then_inc(g_mo, 16)

            def a_load(h):
                pool.dma_start(cs[:, :], a["state_mlstm_C"][0, 0][h]).then_inc(a_cs, 16)

            def a_move(h):
                pl = place(U_A, T_A, h, 8, 4)
                wait(bank_read[0], pl.bank_read(2))
                wait(bank_read[1], pl.bank_read(3))
                pool.tensor_copy(a_cur[:, :, :], a_nxt[:, :, :]).then_inc(a_shift, 1)

            def a_store(h):
                wait(a_co, h + 1)
                pool.dma_start(o["p_C"][0, 0][h], co[:, 0, :]).then_inc(a_out, 16)
                pool.dma_start(o["s_C"][0, 0][h], co[:, 1, :]).then_inc(a_out, 16)
            pool.wait_ge(c_out, 32 * CHD)
            pool.wait_ge(b_kio, 64)
            a_load(0)
            a_move(0)
            with pool.Fori(1, MH) as h:
                wait(a_s0, h)
                a_load(h)
                a_store(h - 1)
                wait(a_lo, h)
                wait(a_out, h * 32)
                a_move(h)
            a_store(MH - 1)

            def q_move(i):
                j = i // 2
                wait(q_rope, i * 2 + 2)
                pool.tensor_copy(q_cur[:, :, :], q_nxt[:, :, :])
                pool.tensor_copy(v_cur[:, 0:2, :], vnp[:, :, ds(j * P, P)])
                pool.tensor_copy(v_cur[:, 2:4, :], cvB[:, :, ds(j * P, P)])
                pool.tensor_copy(v_cur[0:TS, 4, :], vns[0:TS, ds(j * P, P)]).then_inc(q_shift, 1)
            pool.wait_ge(b_vo, 32)
            pool.wait_ge(g_mo, 32)
            pool.wait_ge(a_out, 32 * MH)
            q_move(0)
            with pool.Fori(1, AH // 2) as i:
                wait(q_pv, i * 2)
                q_move(i)

            pool.wait_ge(u_tok, 1)
            for n, name in enumerate(("p_conv", "s_conv")):
                pool.dma_start(o[name][0, 0].rearrange("j (f p) -> f j p", p=P),
                               cvo[0:2 * FT, 2 * n:2 * n + 2, :]).then_inc(u_out, 16)
            pool.wait_ge(n_tok, 1)
            for n, name in enumerate(("p_n", "s_n")):
                pool.dma_start(o[name][0, 0], nrow2[0:MH, n * P:(n + 1) * P]).then_inc(a_n, 16)


INS = ["x_prompt", "x_sample", "mem_prompt", "cache_dsa_k", "cache_dsa_v", "cache_dsa_kidx", "state_mlstm_C",
       "state_mlstm_n", "state_mlstm_m", "state_ffn_conv", "cache_mem_k", "cache_mem_v", "g_mix", "w_in", "b_igate",
       "b_fgate", "w_branch", "w_out", "g_mem", "w_mem_kv", "g_ffn", "w_up", "conv_w", "conv_b", "w_down", "g_final"]
OUTS = [("y_prompt", (1, TP, D)), ("y_sample", (1, TS, D)),
        ("p_k", (1, 1, TP, 2, 128)), ("p_v", (1, 1, TP, 2, 128)), ("p_kidx", (1, 1, TP, 64)),
        ("p_C", (1, 1, MH, 128, 128)), ("p_n", (1, 1, MH, 128)), ("p_m", (1, 1, MH)),
        ("p_conv", (1, 1, 2, 2 * FF)), ("p_mem_k", (1, 1, NMEM, CHD, 256)), ("p_mem_v", (1, 1, NMEM, CHD, 256)),
        ("s_k", (1, 1, TS, 2, 128)), ("s_v", (1, 1, TS, 2, 128)), ("s_kidx", (1, 1, TS, 64)),
        ("s_C", (1, 1, MH, 128, 128)), ("s_n", (1, 1, MH, 128)), ("s_m", (1, 1, MH)),
        ("s_conv", (1, 1, 2, 2 * FF))]


def kernel(**inputs):
    import concourse.bacc as bacc
    from concourse.bass_utils import run_bass_kernel_spmd

    nc = bacc.Bacc("TRN2", target_bir_lowering=False, num_devices=1)
    arrays, a, o = {}, {}, {}
    for name in INS:
        arrays[f"in_{name}"] = np.ascontiguousarray(inputs[name])
    arrays["in_tables"] = shape_tables()
    for name in INS + ["tables"]:
        a[name] = nc.dram_tensor(f"in_{name}", arrays[f"in_{name}"].shape, F32, kind="ExternalInput").ap()
    for name, shape in OUTS:
        o[name] = nc.dram_tensor(f"out_{name}", shape, F32, kind="ExternalOutput").ap()
    layer(nc, a, o)
    r = run_bass_kernel_spmd(nc, [arrays], core_ids=[0])
    return tuple(r.results[0][f"out_{name}"] for name, _ in OUTS)
```

```python
from contextlib import ExitStack, contextmanager

import numpy as np

import concourse.bass as bass
from concourse import mybir

F32 = mybir.dt.float32
F32R = mybir.dt.float32r
ACT = mybir.ActivationFunctionType
ALU = mybir.AluOpType
AX = mybir.AxisListType
ds = bass.ds

P = 128
D = 2048
TP, TS = 256, 64
T = TP + TS
PAST = 256
SS = PAST + TS
CH = 64
NCH = T // CH
KT = D // P
MH, AH, IH, CHD = 8, 8, 8, 4
NMEM = 256
FF = 5632
FT = FF // P
GROUPS = 4
GT = FT // GROUPS
EPS = 1e-6
NEG = -1e30
TAKEN = -3e38
TOPK_P, TOPK_S = TP // 4, SS // 4

O_MQ, O_MK, O_MV, O_MO = 0, 1024, 2048, 3072
O_IF = 4096
O_AQ = O_IF + 16
O_AK = O_AQ + 1024
O_AV = O_AK + 256
O_IQ = O_AV + 256
O_IKW = O_IQ + 512
O_CQ = O_IKW + 72
O_G = O_CQ + 1024
WIN = O_G + 3 * D

RING = 4
UK = 8
LEAD = 2

U_C, T_C = 0, 0
U_B, T_B = U_C + CHD * 12, T_C + CHD * 6
U_A, T_A = U_B + 20, T_B + 10
U_Q, T_Q = U_A + MH * 8, T_A + MH * 4
U_G, T_G = U_Q + AH * 2, T_Q + AH
U_O, T_O = U_G + KT * 9, T_G + KT * 6
U_F, T_F = U_O + KT * 2, T_O + KT
UF_G, TF_G = GT * 4 + KT * 2, GT * 2 + KT
UNITS = U_F + GROUPS * UF_G
T_END = T_F + GROUPS * TF_G

C_ID, C_CAUS, C_CUM, C_LAST, C_ONE = 0, 128, 192, 256, 384
C_R128, C_R64, C_DUP, C_RDUP = 512, 640, 768, 896
C_COS128, C_SIN128, C_COS64, C_SIN64 = (1024 + n * T for n in range(4))
C_ADM = 1024 + 4 * T
CW = C_ADM + 2 * TP


def shape_tables():
    c = np.zeros((P, CW), np.float32)
    c[:, C_ID:C_ID + P] = np.eye(P)
    i = np.arange(CH)
    c[:CH, C_CAUS:C_CAUS + CH] = np.where(i[None, :] <= i[:, None], 0.0, NEG)
    c[:CH, C_CUM:C_CUM + CH] = i[:, None] <= i[None, :]
    c[CH - 1, C_LAST:C_LAST + P] = 1.0
    c[:, C_ONE:C_ONE + P] = 1.0

    def rotation(d):
        r = np.zeros((d, d), np.float32)
        half = d // 8
        for m in range(half):
            r[m + half, m] = -1.0
            r[m, m + half] = 1.0
        return r
    c[:, C_R128:C_R128 + P] = rotation(128)
    for o in (0, 64):
        c[o:o + 64, C_R64 + o:C_R64 + o + 64] = rotation(64)
    for o in (0, 64):
        c[:64, C_DUP + o:C_DUP + o + 64] = np.eye(64)
        c[:64, C_RDUP + o:C_RDUP + o + 64] = rotation(64)
    pos = np.arange(T).astype(np.float32)
    for d, oc, os in ((128, C_COS128, C_SIN128), (64, C_COS64, C_SIN64)):
        r, half = d // 4, d // 8
        inv = np.float32(500000.0) ** (-np.arange(half, dtype=np.float32) * np.float32(2.0) / np.float32(r))
        ang = pos[:, None] * inv.astype(np.float32)[None, :]
        for p in range(P):
            q = p % d
            c[p, oc:oc + T] = np.cos(ang[:, q % half]) if q < r else 1.0
            c[p, os:os + T] = np.sin(ang[:, q % half]) if q < r else 0.0
    for t in range(2):
        q = t * P + np.arange(P)
        end = (q // CH + 1) * CH
        c[:, C_ADM + t * TP:C_ADM + (t + 1) * TP] = np.where(np.arange(TP)[None, :] < end[:, None], 0.0, NEG)
    return c


class Steps:

    def __init__(self, eng, sem):
        self.eng, self.sem, self.n, self.base = eng, sem, 0, 0

    def did(self, ins):
        ins.then_inc(self.sem, 1)
        self.n += 1

    def settle(self):
        self.eng.wait_ge(self.sem, self.base + self.n)

    @contextmanager
    def loop(self, lo, hi, per):
        start = self.n
        with self.eng.Fori(lo, hi) as i:
            self.base, self.n = (i - lo) * per + start, 0
            yield i
            assert self.n == per, f"{self.n} steps in the body"
        self.base, self.n = 0, start + (hi - lo) * per


class Place:

    def __init__(self, unit, tile):
        self.lap, self.pair = unit, tile

    def slot(self, j):
        return j % RING

    def loads(self, j):
        return (self.lap + j // RING) * 16 + 16

    def free(self, j):
        return self.lap * RING + (j + 1)

    def through(self, j):
        return self.lap * RING + (j + 1 + RING)

    def split(self, j):
        return self.lap * RING + (j + 1)

    def bank_free(self, t):
        return self.pair + (t // 2 + 1)

    def bank_read(self, t):
        return self.pair + (t // 2 + 2)


def place(unit, tile, i=0, units=0, tiles=0):
    assert unit % RING == 0 and units % RING == 0 and tile % 2 == 0 and tiles % 2 == 0
    return Place(i * (units // RING) + unit // RING, i * (tiles // 2) + tile // 2)


def layer(nc, a, o):
    with ExitStack() as ctx:
        BASE = (nc.sbuf_base + 63) // 64 * 64
        END = nc.sbuf_usable_end - BASE
        R_RING = 0
        R_XN = R_RING + 3 * RING * UK * P * 4
        R_BC = R_XN + 2 * KT * T * 4
        R_BA = R_BC + 2 * 8 * T * 4
        R_BB = R_BA + 2 * 8 * T * 4
        R_K = R_BB + 2 * 8 * T * 4
        R_S = R_K + CW * 4
        R_W = R_S + 4224

        def at(name, off, shape, dt=F32):
            size = int(np.prod(shape)) * 4
            assert off + size <= END, name
            return nc.alloc_sbuf_tensor_at(name, [P] + shape, dt, offset=BASE + off)

        class Region:

            def __init__(self, off, end):
                self.off, self.end = off, end

            def __call__(self, name, shape, dt=F32):
                t = at(name, self.off, shape, dt)
                self.off += (int(np.prod(shape)) * 4 + 31) // 32 * 32
                assert self.off <= self.end, (name, self.off, self.end)
                return t

        raw = at("w_raw", R_RING, [RING, UK, P])
        whi = at("w_hi", R_RING + RING * UK * P * 4, [RING, UK, P], F32R)
        wlo = at("w_lo", R_RING + 2 * RING * UK * P * 4, [RING, UK, P], F32R)
        xhi = at("xn_hi", R_XN, [KT, T], F32R)
        xlo = at("xn_lo", R_XN + KT * T * 4, [KT, T], F32R)
        bhi = [at(f"branch_hi{n}", r, [8, T], F32R) for n, r in enumerate((R_BA, R_BB, R_BC))]
        blo = [at(f"branch_lo{n}", r + 8 * T * 4, [8, T], F32R) for n, r in enumerate((R_BA, R_BB, R_BC))]
        K = at("shape_consts", R_K, [CW])
        ident = K[:, C_ID:C_ID + P]
        small = Region(R_S, R_W)
        gcols = small("norm_gains", [4, KT])
        ccols = small("conv_cols", [6, 2 * FT])
        ustate = small("u_last", [4, 2 * FT])
        bias16 = small("if_bias", [1])
        nout = small("n_out", [2, MH])
        nst = small("n_state", [MH])
        mst = small("m_state", [MH])
        WE = END

        CN = 4 * NMEM + 2 * T
        pro = Region(R_W + 4 * (4 * 256 + CN), WE)
        xT = pro("xT", [KT, T])
        xsc = pro("x_scaled", [4, T])
        inv = pro("inverse_rms", [NMEM + T])
        tsq = pro("token_squares", [5])
        mnv, xnv = pro("mem_norm_var", [3, 2]), pro("x_norm_var", [3, 3])
        mrow = pro("m_state_row", [MH])
        mtok = at("mem_tokens", R_XN, [2, D])
        early = Region(R_XN + KT * T * 4, R_BC)
        unused = early("squares_unused", [D])
        idiag = early("inverse_rms_diag", [5, P])
        msc = early("mem_scaled", [4, NMEM])
        xtok = at("x_tokens_prompt", R_BC, [2, D])
        xtos = at("x_tokens_sample", R_BA + 2 * KT * NMEM * 4, [D])
        assert 2 * KT * NMEM * 4 + D * 4 == R_K - R_BA
        rows = Region(R_BC + 2 * D * 4, R_BA)
        grow = rows("gain_rows", [P])
        crow = rows("conv_rows", [6, P])
        nrow = rows("n_state_rows", [P])
        mhi = at("mem_hi", R_BA, [KT, NMEM], F32R)
        mlo = at("mem_lo", R_BA + KT * NMEM * 4, [KT, NMEM], F32R)

        wc = Region(R_W, WE)
        ck = wc("cache_mem_k_head", [2, 256])
        cv = wc("cache_mem_v_head", [2, 256])
        c_nxt, c_cur = wc("c_next", [CN]), wc("c_current", [CN])

        def c_parts(buf):
            return (buf[:, 0:2 * NMEM].rearrange("p (d m) -> p d m", d=2),
                    buf[:, 2 * NMEM:4 * NMEM].rearrange("p (d m) -> p d m", d=2),
                    buf[:, 4 * NMEM:CN].rearrange("p (d t) -> p d t", d=2))
        mk_n, mv_n, cq_n = c_parts(c_nxt)
        mk_c, mv_c, cq_c = c_parts(c_cur)
        mvn = wc("mem_v_tokens", [2, 256])
        mkn = wc("mem_k_tokens", [2, 256])
        ckT = wc("cache_mem_kT", [2, NMEM])
        c_p = wc("c_probs", [3, NMEM])
        c_pT = wc("c_probsT", [2, T])
        c_st = wc("c_stats", [4, 4])

        wb = Region(wc.off, WE)
        kTp = wb("kT_prompt", [2, TP])
        kTs = wb("kT_sample", [2, SS])
        vnp = wb("v_prompt", [2, 256])
        vns = wb("v_new", [256])
        cvB = wb("cache_v", [2, 256])
        iw = wb("index_weights", [3, IH])
        msk = wb("mask_bias", [2 * TP + SS])
        bcs = wb("b_cumsum", [NCH, MH])
        inter = wb("inter", [NCH, MH])
        wexp = wb("w_s", [NCH, MH])
        enm = wb("exp_neg_m", [NCH, MH])
        dec = wb("decay", [NCH, MH])
        mnew = wb("m_new", [NCH, MH])
        rb = Region(R_BB, R_K)
        Dm = rb("decay_matrix", [NCH, MH, CH])
        iqT = rb("index_qT", [4, T])
        ki2 = rb("index_kT", [T])
        kic = rb("index_kT_cache", [PAST])
        rl = rb("relu", [2, SS])
        ra = Region(R_BA, R_BB)
        vraw = ra("vT_raw", [2, T])
        kiw = ra("ikw_raw", [T])
        rin = ra("rope_in", [2, T])
        rtmp = ra("rope_tmp", [T])
        ifT = ra("if_T", [T])
        ckB = ra("cache_k", [2, 256])
        ckI = ra("cache_kidx", [2, 2, 64])
        kout = ra("k_tokens", [3, 256])
        kiout = ra("kidx_tokens", [3, 64])
        igf = ra("if_gates", [NCH, 16])
        g1 = ra("gate_tmp", [NCH, MH])
        g2 = ra("log_f", [NCH, MH])
        acs = ra("ig_minus_b", [NCH, MH])
        mxs = ra("row_max", [NCH, MH])
        mb = ra("m_and_b", [NCH, 2, MH])
        mint = ra("m_inter", [NCH, MH])
        blast = ra("b_last", [NCH, MH])
        diag = at("diag", R_W + 8 * T * 4, [NCH, MH, CH])

        wa = Region(R_W, wc.off)
        a_nxt, a_cur = wa("a_next", [4, T]), wa("a_current", [4, T])
        q_c, k_c, v_c, s_c = (a_cur[:, n, :] for n in range(4))
        kw = wa("k_weighted", [NCH, P])
        vn = wa("v_tokens", [NCH, P])
        SD = wa("scores_decayed", [NCH, CH])
        sdT = wa("scoresT", [NCH, CH])
        Cst = wa("C_states", [7, P + 1])
        hn = wa("h_tokens", [NCH, P])
        ga = wa("h_gated", [T])
        cs = wa("C_state_head", [P])
        co = wa("C_out", [2, P])
        a_st = wa("a_stats", [2, 8])
        top8 = wa("top8", [3, 8])

        wq = Region(R_W, wc.off)
        q_raw = wq("q_raw", [2, T])
        q_nxt, q_cur = wq("q_next", [2, T]), wq("q_current", [2, T])
        v_cur = wq("v_current", [5, P])
        sp_ = wq("probs_prompt", [2, 2 * TP])
        ss_ = wq("probs_sample", [2, SS])
        pTp = wq("probsT_prompt", [2, 2 * TP])
        pTs = wq("probsT_sample", [2, 3 * TS])
        q_tmp = wq("q_rope_tmp", [T])
        q_st = wq("q_stats", [2, 4, 4])

        wg = Region(R_W, WE)
        mghi = wg("merged_hi", [KT, T], F32R)
        mglo = wg("merged_lo", [KT, T], F32R)
        kg = Region(R_K + C_COS128 * 4, R_S)
        th = kg("gate_tanh", [3, T])
        acc = kg("merged_sum", [T])
        gtmp = wg("merged_tmp", [T])
        hT = at("hT", R_BC, [KT, T])
        h2 = at("h_square", R_K + C_COS128 * 4, [T])
        hacc = at("h_square_sum", R_K + (C_COS128 + T) * 4, [3 * P])

        wf = Region(R_W, WE)
        yhi = wf("y_hi", [GT, T], F32R)
        ylo = wf("y_lo", [GT, T], F32R)
        E2 = T + 4
        ext = wf("u_ext", [2, E2])
        cbuf = wf("conv", [2, E2])
        gth = wf("ffn_tanh", [E2])
        ybuf = wf("y", [T])
        fnv = wf("ffn_norm_var", [3, T])
        hg = at("h_scaled", R_BA, [KT, T])
        ytok = at("y_tokens", R_XN, [3, D])
        cvo = at("conv_out", R_XN + 3 * D * 4, [4, P])
        nrow2 = at("n_out_rows", R_XN + 3 * D * 4 + 4 * P * 4, [2 * P])

        scratch = nc.dram_tensor("xT_scratch", (P, KT * T), F32, kind="Internal").ap()

        psum = [ctx.enter_context(nc.psum_tensor(f"bank{n}", [P, 512], F32)) for n in range(8)]
        G, M = psum[0:2], psum[2:8]

        def sem(name):
            return ctx.enter_context(nc.semaphore(name))

        tables_in, mem_in, x_in, cache_in = sem("tables_in"), sem("mem_in"), sem("x_in"), sem("cache_in")
        raw_in = [sem(f"raw_in{n}") for n in range(RING)]
        w_hi, w_lo, w_used = sem("w_hi"), sem("w_lo"), sem("w_used")
        bank_read = [sem("bank_read0"), sem("bank_read1")]
        act_own, dve_own = sem("act_own"), sem("dve_own")
        sp_passed, pool_passed, dve_passed = (sem(n) for n in ("sp_passed", "pool_passed", "dve_passed"))
        rows_T, rows_out = sem("rows_transposed"), sem("rows_out")
        ident_in, rows_in = sem("identity_in"), sem("rows_in")
        xp_done, xp_act, xp_dve = sem("tokens_transposed"), sem("tokens_out_act"), sem("tokens_out_dve")
        t_ones, t_sq, t_diag, t_inv = (sem("token_" + n) for n in ("ones", "squares", "diag", "inverse_rms"))
        sums, variances, roots = sem("sums"), sem("variances"), sem("roots")
        n_x, n_hi, n_lo = sem("norm_x"), sem("norm_hi"), sem("norm_lo")
        xT_out, hT_in = sem("xT_out"), sem("hT_in")
        c_shift, c_cache, c_xp, c_mvn, c_mkn, c_ckT = (sem("c_" + n) for n in (
            "shift", "cache", "transposed", "v_tokens", "k_tokens", "cache_kT"))
        c_sc, c_nm, c_exp, c_pn, c_pt, c_pTa, c_pTd, c_pv, c_hi, c_lo, c_out = (sem("c_" + n) for n in (
            "scores", "negmax", "exp", "probs", "transposes", "pT_act", "pT_dve", "values", "hi", "lo", "out"))
        b_vx, b_gx, b_v, b_if, b_iw, b_kix, b_ki, b_rot, b_rope, b_cx, b_cT, b_kx, b_ko, b_kio, b_vo = (
            sem("b_" + n) for n in ("v_transposed", "gates_transposed", "v_tokens", "if_gates", "index_w",
                                    "ki_rotated", "ki", "rotated", "roped", "cache_transposed", "cacheT",
                                    "k_transposed", "k_tokens", "k_out", "v_out"))
        i_lg, i_relu, i_acc = (sem("i_" + n) for n in ("logits", "relu", "score"))
        g_l, g_lf, g_b, g_dg, g_R, g_D, g_mb, g_last, g_arg, g_exp, g_Da, g_De, g_mo = (
            sem("g_" + n) for n in ("ln", "log_f", "cumsum", "diag", "rows", "logD",
                                    "m_and_b", "last_rows", "arguments", "exps", "D_arg", "D_exp", "m_out"))
        a_shift, a_cs, a_s0, a_vn, a_sd, a_kw, a_s1, a_sdT, a_C, a_s2, a_h, a_co, a_s3, a_ga, a_hi, a_lo, a_out, a_n = (
            sem("a_" + n) for n in ("shift", "state_in", "scores", "v_tokens", "decayed", "k_weighted",
                                    "outer", "scoresT", "states", "values", "h_tokens", "C_ready", "hT", "gated",
                                    "hi", "lo", "C_out", "n_out"))
        q_shift, q_rot, q_rope, q_sc, q_nm, q_exp, q_pn, q_pt, q_pT, q_pv, q_hi, q_lo = (
            sem("q_" + n) for n in ("shift", "rotated", "roped", "scores", "negmax", "exp", "probs",
                                    "transposes", "pT", "values", "hi", "lo"))
        m_sum, m_hi, m_lo = (sem("m_" + n) for n in ("sum", "hi", "lo"))
        f_us, f_ext, f_c0, f_conv, f_th, f_y, f_hi, f_lo, f_rms = (
            sem("f_" + n) for n in ("state", "ext", "tap2", "conv", "tanh", "y", "hi", "lo", "rms"))
        h_sq, h_sum, h_hi, h_lo, h_g = (sem("h_" + n) for n in ("square", "square_sum", "hi", "lo", "scaled"))
        y_T, y_act, y_dve, y_out, u_T, u_tok, u_out, n_T, n_tok = (
            sem(n) for n in ("y_transposed", "y_tokens_act", "y_tokens_dve", "y_out", "u_transposed", "u_tokens", "u_out",
                             "n_transposed", "n_tokens"))

        w_in = a["w_in"][0].rearrange("(k p) n -> p k n", p=P)
        w_mem = a["w_mem_kv"][0].rearrange("(k p) n -> p k n", p=P)
        w_out = a["w_out"][0].rearrange("(k p) n -> p k n", p=P)
        w_up = a["w_up"][0].rearrange("(k p) n -> p k n", p=P)
        w_down = a["w_down"][0].rearrange("(k p) n -> p k n", p=P)
        w_br = a["w_branch"][0].rearrange("b (k p) n -> b p k n", p=P)
        KD = (UK, GT - UK)

        block = ctx.enter_context(nc.Block())

        @block.sync
        def _(sp):
            mem, xp, xs = a["mem_prompt"][0], a["x_prompt"][0], a["x_sample"][0]
            sp.dma_start(K[:, 0:C_R128], a["tables"][:, 0:C_R128]).then_inc(ident_in, 16)
            sp.dma_start(mtok[:, :, :], mem.rearrange("(t p) n -> p t n", p=P)).then_inc(mem_in, 16)
            for n, g in enumerate(("g_mix", "g_mem", "g_ffn")):
                sp.dma_start(grow[KT * n:KT * n + KT, :], a[g][0].rearrange("(k p) -> k p", p=P)).then_inc(rows_in, 16)
            sp.dma_start(grow[3 * KT:4 * KT, :], a["g_final"].rearrange("(k p) -> k p", p=P)).then_inc(rows_in, 16)
            sp.dma_start(crow[0:2 * FT, 0:3, :], a["conv_w"][0].rearrange("j (f p) -> f j p", p=P)).then_inc(rows_in, 16)
            sp.dma_start(crow[0:2 * FT, 3, :], a["conv_b"][0].rearrange("(f p) -> f p", p=P)).then_inc(rows_in, 16)
            sp.dma_start(crow[0:2 * FT, 4:6, :],
                          a["state_ffn_conv"][0, 0].rearrange("j (f p) -> f j p", p=P)).then_inc(rows_in, 16)
            sp.dma_start(nrow[0:MH, :], a["state_mlstm_n"][0, 0]).then_inc(rows_in, 16)
            sp.dma_start(mrow[0:1, :], a["state_mlstm_m"][0]).then_inc(rows_in, 16)

            def load(pl, j, src):
                n, c = src.shape[1], src.shape[2]
                sp.wait_ge(w_lo, pl.free(j))
                sp.sem_inc(sp_passed, 1)
                sp.dma_start(raw[:, pl.slot(j), 0:n, 0:c], src).then_inc(raw_in[pl.slot(j)], 16)

            def load_tile(pl, j, w, col, cols=P, ks=(UK, UK), k0=0):
                for k in ks:
                    load(pl, j, w[:, ds(k0, k), ds(col, cols)])
                    j, k0 = j + 1, k0 + k

            def head_c(pl, h, first=0, last=6):
                for n, (w, col) in list(enumerate((
                        (w_mem, h * 256), (w_mem, h * 256 + P), (w_mem, h * 256 + 1024), (w_mem, h * 256 + (1024 + P)),
                        (w_in, h * 256 + O_CQ), (w_in, h * 256 + (O_CQ + P)))))[first:last]:
                    load_tile(pl, 2 * n, w, col)
            head_c(place(U_C, T_C), 0, 0, 2)
            sp.dma_start(xtok[:, :, :], xp.rearrange("(t p) n -> p t n", p=P)).then_inc(x_in, 16)
            sp.dma_start(xtos[0:TS, :], xs).then_inc(x_in, 16)
            head_c(place(U_C, T_C), 0, 2)
            sp.dma_start(K[:, C_R128:CW], a["tables"][:, C_R128:CW]).then_inc(tables_in, 16)
            sp.dma_start(bias16[0:MH, :], a["b_igate"].rearrange("o h -> h o")).then_inc(tables_in, 16)
            sp.dma_start(bias16[MH:2 * MH, :], a["b_fgate"].rearrange("o h -> h o")).then_inc(tables_in, 16)
            with sp.Fori(1, CHD) as h:
                head_c(place(U_C, T_C, h, 12, 6), h)
            pl = place(U_B, T_B)
            for n, (col, cols) in enumerate(((O_AV, P), (O_AV + P, P), (O_IF, 16), (O_IKW, 72),
                                             (O_IQ, P), (O_IQ + P, P), (O_IQ + 2 * P, P), (O_IQ + 3 * P, P),
                                             (O_AK, P), (O_AK + P, P))):
                load_tile(pl, 2 * n, w_in, col, cols)

            def head_a(pl, h):
                for n, col in enumerate((O_MQ, O_MK, O_MV, O_MO)):
                    load_tile(pl, 2 * n, w_in, h * P + col)
            head_a(place(U_A, T_A), 0)
            with sp.Fori(1, MH) as h:
                head_a(place(U_A, T_A, h, 8, 4), h)
            with sp.Fori(0, AH // 2) as i:
                pl = place(U_Q, T_Q, i, 4, 2)
                for e in range(2):
                    load_tile(pl, 2 * e, w_in, i * (2 * P) + (O_AQ + e * P))
            with sp.Fori(0, KT // 4) as i:
                pl = place(U_G, T_G, i, 36, 24)
                for n in range(4):
                    for b in range(3):
                        load_tile(pl, 9 * n + 2 * b, w_in, i * (4 * P) + (O_G + b * D + n * P))
                    for b in range(3):
                        load(pl, 9 * n + 6 + b, w_br[b][:, :, ds(i * (4 * P) + n * P, P)])
            with sp.Fori(0, KT // 2) as i:
                pl = place(U_O, T_O, i, 4, 2)
                for e in range(2):
                    load_tile(pl, 2 * e, w_out, i * (2 * P) + e * P)
            for g in range(GROUPS):
                with sp.Fori(0, GT) as f:
                    pl = place(U_F + g * UF_G, T_F + g * TF_G, f, 4, 2)
                    load_tile(pl, 0, w_up, f * P + g * GT * P)
                    load_tile(pl, 2, w_up, f * P + (FF + g * GT * P))
                with sp.Fori(0, KT // 2) as i:
                    pl = place(U_F + g * UF_G + 4 * GT, T_F + g * TF_G + 2 * GT, i, 4, 2)
                    for e in range(2):
                        load_tile(pl, 2 * e, w_down, i * (2 * P) + e * P, ks=KD, k0=g * GT)
            y_dst = o["y_prompt"][0].rearrange("(u p) n -> u p n", p=P)
            for u in range(3):
                sp.wait_ge(y_act, 2 * u + 2)
                sp.wait_ge(y_dve, 2 * u + 2)
                sp.dma_start(y_dst[u] if u < 2 else o["y_sample"][0], ytok[0:P if u < 2 else TS, u, :]).then_inc(y_out, 16)
            sp.wait_ge(c_out, 32 * CHD)
            sp.wait_ge(b_vo, 32)
            sp.wait_ge(b_kio, 64)
            sp.wait_ge(g_mo, 32)
            sp.wait_ge(a_out, 32 * MH)
            sp.wait_ge(a_n, 32)
            sp.wait_ge(u_out, 32)
            sp.wait_ge(y_out, 48)

        @block.tensor
        def _(pe):
            pe.sem_inc(w_used, RING)
            pe.sem_inc(c_pv, 2)

            def multiply(pl, t, units, n, m=P, parts=None, each=None):
                pe.wait_ge(bank_read[t % 2], pl.bank_free(t))
                out = G[t % 2][0:m, 0:n]
                for un, (j, hi, lo, k0, nk) in enumerate(units):
                    if un and parts is not None:
                        pe.wait_ge(*parts)
                    pe.wait_ge(w_lo, pl.through(j))
                    for k in range(nk):
                        if each is not None:
                            pe.wait_ge(each[0], each[1] + k0 + k + 1)
                        h, l = whi[:, pl.slot(j), k, 0:m], wlo[:, pl.slot(j), k, 0:m]
                        pe.matmul(out, h, hi[:, k0 + k, 0:n], start=un == 0 and k == 0, stop=False)
                        pe.matmul(out, h, lo[:, k0 + k, 0:n], start=False, stop=False)
                        last = pe.matmul(out, l, hi[:, k0 + k, 0:n], start=False,
                                         stop=un == len(units) - 1 and k == nk - 1)
                    last.then_inc(w_used, 1)

            def tile_x(pl, t, j, m=P, each=None):
                multiply(pl, t, [(j, xhi, xlo, 0, UK), (j + 1, xhi, xlo, UK, UK)], T, m, each=each)

            def tile_mem(pl, t, j, each=None):
                multiply(pl, t, [(j, mhi, mlo, 0, UK), (j + 1, mhi, mlo, UK, UK)], NMEM, each=each)

            def turn(out, in_):
                return pe.transpose(out, in_, ident[0:in_.shape[0], 0:in_.shape[0]])

            def mm(out, lhsT, rhs, first=True, last=True):
                return pe.matmul(out, lhsT, rhs, start=first, stop=last)

            def mem_T(n0, n1):
                for n in range(n0, n1):
                    if n >= 4:
                        pe.wait_ge(n_x, 2 * (n - 4) + 2)
                    for e in range(2):
                        for t in range(2):
                            k = 2 * n + e
                            last = turn(M[n % 4][:, e * NMEM + t * P:e * NMEM + t * P + P], mtok[:, t, k * P:k * P + P])
                    last.then_inc(xp_done, 1)

            def x_T(k0, k1):
                for k in range(k0, k1):
                    if k < 4:
                        pe.wait_ge(n_x, 2 * (k + 4) + 2)
                    else:
                        pe.wait_ge(xp_dve if k % 2 else xp_act, (k - 4) // 2 + 1)
                    for t in range(2):
                        turn(M[k % 4][:, t * P:t * P + P], xtok[:, t, k * P:k * P + P])
                    turn(M[k % 4][:, TP:T], xtos[0:TS, k * P:k * P + P]).then_inc(xp_done, 1)

            def inverse_rows(done, bank, columns):
                pe.wait_ge(t_diag, done)
                for n, (c, rows_) in enumerate(columns):
                    last = mm(bank[:, n * P:n * P + rows_], K[0:rows_, C_ONE:C_ONE + P], idiag[0:rows_, c, 0:rows_])
                last.then_inc(t_inv, 1)
            pe.wait_ge(ident_in, 16)
            pe.wait_ge(mem_in, 16)
            mem_T(0, 4)
            pe.wait_ge(rows_in, 16 * 9)
            for j in range(3):
                turn(M[4][:, 88 * j:88 * j + 88], crow[0:88, j, :])
                turn(M[5][:, 64 + 88 * j:64 + 88 * j + 88], crow[0:88, 3 + j, :])
            turn(M[5][:, 0:64], grow[0:64, :])
            turn(M[5][:, 408:416], nrow[0:MH, :])
            mm(M[5][:, 400:408], K[0:1, C_ONE:C_ONE + P], mrow[0:1, :]).then_inc(rows_T, 1)
            pe.wait_ge(rows_out, 1)
            inverse_rows(1, M[4], ((0, P), (1, P)))
            mem_T(4, 8)
            pe.wait_ge(x_in, 32)
            x_T(0, 4)

            def c_turn(h):
                pe.wait_ge(c_shift, h + 1)
                pe.wait_ge(c_cache, h * 32 + 32)
                for m in range(2):
                    for d in range(2):
                        turn(M[0][:, m * 256 + d * P:m * 256 + d * P + P], mv_c[:, d, m * P:m * P + P])
                        turn(M[1][:, d * 256 + m * P:d * 256 + m * P + P], ck[:, m, d * P:d * P + P])
                        last = turn(M[2][:, m * 256 + d * P:m * 256 + d * P + P], mk_c[:, d, m * P:m * P + P])
                last.then_inc(c_xp, 1)

            def c_scores(h):
                pe.wait_ge(c_ckT, h + 1)
                pe.wait_ge(c_lo, h * 2 + 2)
                for t in range(2):
                    for d in range(2):
                        mm(M[3][:, t * NMEM:(t + 1) * NMEM], cq_c[:, d, t * P:t * P + P], mk_c[:, d, :], d == 0, d == 1)
                for d in range(2):
                    last = mm(M[4][0:TS, 0:NMEM], cq_c[:, d, TP:T], ckT[:, d, :], d == 0, d == 1)
                last.then_inc(c_sc, 1)

            def c_probsT(h):
                pe.wait_ge(c_pn, h + 1)
                pe.wait_ge(c_mkn, h + 1)
                for m in range(2):
                    b = M[5] if m == 0 else M[2]
                    for t in range(2):
                        turn(b[:, t * P:t * P + P], c_p[:, t, m * P:m * P + P])
                    last = turn(b[:, TP:T], c_p[0:TS, 2, m * P:m * P + P])
                last.then_inc(c_pt, 1)

            def c_values(h):
                pe.wait_ge(c_pTa, h + 1)
                pe.wait_ge(c_pTd, h + 1)
                pe.wait_ge(c_mvn, h + 1)
                for d in range(2):
                    b = M[3 + d]
                    for m in range(2):
                        mm(b[:, 0:TP], mvn[:, m, d * P:d * P + P], c_pT[:, m, 0:TP], m == 0, m == 1)
                    for m in range(2):
                        last = mm(b[:, TP:T], cv[:, m, d * P:d * P + P], c_pT[:, m, TP:T], m == 0, m == 1)
                    last.then_inc(c_pv, 1)

            def c_tiles(pl, stages):
                for t in range(6):
                    if t < 4:
                        tile_mem(pl, t, 2 * t)
                    else:
                        tile_x(pl, t, 2 * t)
                    if t < len(stages):
                        stages[t]()

            pl = place(U_C, T_C)
            tile_mem(pl, 0, 0, (n_lo, 4))
            inverse_rows(2, M[5], ((2, P), (3, P), (4, TS)))
            x_T(4, 8)
            tile_mem(pl, 1, 2)
            x_T(8, 12)
            tile_mem(pl, 2, 4)
            x_T(12, 16)
            tile_mem(pl, 3, 6)
            tile_x(pl, 4, 8, each=(n_lo, KT + 4))
            tile_x(pl, 5, 10)
            with pe.Fori(1, CHD) as h:
                c_tiles(place(U_C, T_C, h, 12, 6), [lambda: c_turn(h - 1), lambda: c_scores(h - 1),
                                                    lambda: c_probsT(h - 1), lambda: c_values(h - 1)])

            pl = place(U_B, T_B)
            pe.wait_ge(tables_in, 16 * 3)
            for t in range(10):
                tile_x(pl, t, 2 * t, (P, P, 16, 72, P, P, P, P, P, P)[t])
                if t < 4:
                    (c_turn, c_scores, c_probsT, c_values)[t](CHD - 1)
                if t == 4:
                    pe.wait_ge(bank_read[0], pl.bank_read(0))
                    pe.wait_ge(bank_read[1], pl.bank_read(1))
                    for j in range(2):
                        for u in range(2):
                            turn(M[0][:, u * 256 + j * P:u * 256 + j * P + P], vraw[:, j, u * P:u * P + P])
                        last = turn(M[1][0:TS, j * P:j * P + P], vraw[:, j, TP:T])
                    last.then_inc(b_vx, 1)
                    pe.wait_ge(bank_read[0], pl.bank_read(2))
                    for c in range(NCH):
                        turn(M[5][0:CH, c * 16:c * 16 + 16], ifT[0:16, c * CH:c * CH + CH])
                    pe.wait_ge(bank_read[1], pl.bank_read(3))
                    for u in range(3):
                        n = P if u < 2 else TS
                        last = turn(M[2][0:n, u * 72:u * 72 + 72], kiw[0:72, u * P:u * P + n])
                    last.then_inc(b_gx, 1)
                if t == 5:
                    pe.wait_ge(c_lo, 2 * CHD + 2)
                    mm(M[3][:, 0:T], K[0:64, C_DUP:C_DUP + P], kiw[0:64, :])
                    mm(M[4][:, 0:T], K[0:64, C_RDUP:C_RDUP + P], kiw[0:64, :]).then_inc(b_kix, 1)
                if t == 6:
                    pe.wait_ge(cache_in, 64)
                    pe.wait_ge(b_ki, 1)
                    for j in range(2):
                        for u in range(2):
                            turn(M[3][:, j * 256 + u * P:j * 256 + u * P + P], ckB[:, u, j * P:j * P + P])
                    for u in range(2):
                        last = turn(M[4][:, u * P:u * P + P], ckI[:, u, :, :].rearrange("p a d -> p (a d)"))
                    last.then_inc(b_cx, 1)
                if 5 <= t:
                    n = t - 5
                    pe.wait_ge(bank_read[(t - 1) % 2], pl.bank_read(t - 1))
                    if n == 0:
                        pe.wait_ge(b_v, 1)
                        pe.wait_ge(b_iw, 1)
                    if n == 4:
                        pe.wait_ge(b_rope, 1)
                    bank = M[(0, 1, 2, 5, 0)[n]]
                    mm(bank[:, 0:T], K[:, C_R64:C_R64 + P] if n < 4 else K[:, C_R128:C_R128 + P],
                       rin[:, (t - 1) % 2, :]).then_inc(b_rot, 1)

            def a_scores(h):
                pe.wait_ge(tables_in, 16 * 3)
                pe.wait_ge(a_shift, h + 1)
                pe.wait_ge(a_cs, h * 16 + 16)
                for c in range(NCH):
                    q, k, v = (x[:, c * CH:c * CH + CH] for x in (q_c, k_c, v_c))
                    mm(M[0][0:CH, c * CH:c * CH + CH], q, k)
                    turn(M[1][0:CH, c * P:c * P + P] if c < 4 else M[3][0:CH, 0:P], k)
                    turn(M[2][0:CH, c * P:c * P + P] if c < 4 else M[3][0:CH, P:2 * P], v)
                turn(M[3][:, 2 * P:3 * P], cs[:, :]).then_inc(a_s0, 1)

            def a_outer(h):
                pe.wait_ge(tables_in, 16 * 3)
                pe.wait_ge(a_sd, h + 1)
                pe.wait_ge(a_kw, h + 1)
                pe.wait_ge(a_vn, h + 1)
                for c in range(NCH):
                    turn(M[0][0:CH, c * CH:c * CH + CH], SD[0:CH, c, :])
                    mm(M[1][:, c * P:c * P + P] if c < 4 else M[3][:, 0:P], kw[0:CH, c, :], vn[0:CH, c, :])
                    last = mm(M[5][:, c:c + 1], kw[0:CH, c, :], K[0:CH, C_ONE:C_ONE + 1])
                last.then_inc(a_s1, 1)

            def a_values(h):
                pe.wait_ge(tables_in, 16 * 3)
                pe.wait_ge(a_sdT, h + 1)
                pe.wait_ge(a_C, h + 1)
                for c in range(NCH):
                    q = q_c[:, c * CH:c * CH + CH]
                    C = Cst[:, c if c < 4 else 5, :]
                    mm(M[2][0:CH, c * P:c * P + P] if c < 4 else M[5][0:CH, P:2 * P], sdT[0:CH, c, :], vn[0:CH, c, :])
                    mm(M[4][0:CH, c * P:c * P + P] if c < 4 else M[5][0:CH, 2 * P:3 * P], q, C[:, 0:P])
                    mm(M[5][0:CH, 8 + c:9 + c], q, C[:, P:P + 1])
                turn(M[1][:, 0:P], Cst[:, 4, 0:P])
                turn(M[1][:, P:2 * P], Cst[:, 6, 0:P]).then_inc(a_s2, 1)

            def a_hT(h):
                pe.wait_ge(tables_in, 16 * 3)
                pe.wait_ge(a_h, h + 1)
                for c in range(NCH):
                    last = turn(M[4][:, c * CH:c * CH + CH], hn[0:CH, c, :])
                last.then_inc(a_s3, 1)

            def logits(u, h):
                n = u * IH + h
                q = 64 * (h % 2)
                rows = P if u < 2 else TS
                if n >= 2:
                    pe.wait_ge(i_relu, n - 1)
                b = M[4] if n % 2 else M[2]
                lhs = iqT[q:q + 64, h // 2, u * P:u * P + rows]
                if u < 2:
                    last = mm(b[0:rows, 0:TP], lhs, ki2[q:q + 64, 0:TP])
                else:
                    mm(b[0:rows, 0:PAST], lhs, kic[q:q + 64, :])
                    last = mm(b[0:rows, PAST:SS], lhs, ki2[q:q + 64, TP:T])
                last.then_inc(i_lg, 1)

            def decay_rows(c):
                mm(M[(3, 5, 2, 4, 3)[c]][0:CH, :], K[0:CH, C_ONE:C_ONE + CH],
                   diag[0:CH, c, :, :].rearrange("p h s -> p (h s)")).then_inc(g_R, 1)

            pl = place(U_A, T_A)
            plb = place(U_B, T_B)
            for t in range(4):
                tile_x(pl, t, 2 * t)
                if t == 0:
                    pe.wait_ge(bank_read[1], plb.bank_read(9))
                    pe.wait_ge(b_rope, 4)
                    mm(M[1][:, 0:T], K[:, C_R128:C_R128 + P], rin[:, 1, :]).then_inc(b_rot, 1)
                    pe.wait_ge(g_lf, 1)
                    mm(M[5][0:CH, 0:NCH * MH], K[0:CH, C_CUM:C_CUM + CH],
                       g2[0:CH, :, :].rearrange("p c h -> p (c h)")).then_inc(g_b, 1)
                if t == 1:
                    pe.wait_ge(b_rope, 6)
                    for j in range(2):
                        for u in range(2):
                            turn(M[0][:, u * 256 + j * P:u * 256 + j * P + P], kTp[:, j, u * P:u * P + P])
                        turn(M[1][0:TS, j * P:j * P + P], kTs[:, j, PAST:SS])
                    for u in range(3):
                        n = P if u < 2 else TS
                        last = turn(M[1][0:n, 256 + 64 * u:320 + 64 * u], ki2[0:64, u * P:u * P + n])
                    last.then_inc(b_kx, 1)
                    pe.wait_ge(b_cT, 1)
                    pe.wait_ge(g_dg, 1)
                    for c in range(4):
                        decay_rows(c)
                if t == 2:
                    pe.wait_ge(g_D, 1)
                    decay_rows(4)
                    pe.wait_ge(g_D, 4)
                    for h in range(IH):
                        logits(0, h)
                    pe.wait_ge(g_D, 5)
                    for c in range(NCH):
                        pe.wait_ge(g_mb, c + 1)
                        mm(M[3][:, 16 * c:16 * c + 16], K[0:CH, C_LAST:C_LAST + P],
                           mb[0:CH, c, :, :].rearrange("p a h -> p (a h)")).then_inc(g_last, 1)
                if t == 3:
                    for u in range(1, 3):
                        for h in range(IH):
                            logits(u, h)
            a_stages = (a_scores, a_outer, a_values, a_hT)
            pe.wait_ge(i_relu, 3 * IH)
            pe.wait_ge(b_ko, 1)
            pe.wait_ge(g_De, 1)
            with pe.Fori(1, MH) as h:
                pl = place(U_A, T_A, h, 8, 4)
                for t in range(4):
                    tile_x(pl, t, 2 * t)
                    a_stages[t](h - 1)

            def q_scores(i):
                j = i // 2
                pe.wait_ge(q_shift, i + 1)
                for e in range(2):
                    for u in range(2):
                        mm(M[2 * e][:, u * TP:(u + 1) * TP], q_cur[:, e, u * P:u * P + P], kTp[:, j, :])
                    mm(M[2 * e + 1][0:TS, 0:SS], q_cur[:, e, TP:T], kTs[:, j, :]).then_inc(q_sc, 1)

            def q_probsT(i):
                for e in range(2):
                    pe.wait_ge(q_pn, i * 2 + (e + 1))
                    for s in range(2):
                        for u in range(2):
                            turn(M[4 + e][:, s * TP + u * P:s * TP + u * P + P],
                                 sp_[:, e, u * TP + s * P:u * TP + s * P + P])
                        turn(M[2 * e + 1][:, s * TS:(s + 1) * TS], ss_[0:TS, e, s * P:s * P + P])
                    turn(M[2 * e + 1][0:TS, 2 * TS:3 * TS], ss_[0:TS, e, PAST:SS]).then_inc(q_pt, 1)

            def q_values(i):
                for e in range(2):
                    pe.wait_ge(q_pT, i * 2 + (e + 1))
                    b = M[4 + e]
                    for s in range(2):
                        mm(b[:, 0:TP], v_cur[:, s, :], pTp[:, e, s * TP:(s + 1) * TP], s == 0, s == 1)
                    for s in range(3):
                        n = P if s < 2 else TS
                        last = mm(b[:, TP:T], v_cur[0:n, 2 + s, :], pTs[0:n, e, s * TS:(s + 1) * TS], s == 0, s == 2)
                    last.then_inc(q_pv, 1)

            def q_rotate(pl, e):
                pe.wait_ge(bank_read[e], pl.bank_read(e))
                mm(M[2 * e][:, 0:T], K[:, C_R128:C_R128 + P], q_raw[:, e, :]).then_inc(q_rot, 1)

            pl = place(U_Q, T_Q)
            tile_x(pl, 0, 0)
            a_scores(MH - 1)
            a_outer(MH - 1)
            tile_x(pl, 1, 2)
            a_values(MH - 1)
            a_hT(MH - 1)
            for e in range(2):
                q_rotate(pl, e)
            with pe.Fori(1, AH // 2) as i:
                pl = place(U_Q, T_Q, i, 4, 2)
                tile_x(pl, 0, 0)
                q_scores(i - 1)
                tile_x(pl, 1, 2)
                q_probsT(i - 1)
                for e in range(2):
                    q_rotate(pl, e)
                q_values(i - 1)
            def merge_tiles(pl, stages):
                for n in range(4):
                    for b in range(3):
                        tile_x(pl, 6 * n + b, 9 * n + 2 * b)
                        if n == 0 and stages:
                            stages[b](AH // 2 - 1)
                    for b in range(3):
                        if n == 0 and b == 1 and stages:
                            pe.wait_ge(q_lo, AH)
                        multiply(pl, 6 * n + 3 + b, [(9 * n + 6 + b, bhi[b], blo[b], 0, UK)], T)
            merge_tiles(place(U_G, T_G), (q_scores, q_probsT, q_values))
            with pe.Fori(1, KT // 4) as i:
                merge_tiles(place(U_G, T_G, i, 36, 24), ())

            pe.wait_ge(m_lo, UK + 1)
            with pe.Fori(0, KT // 2) as i:
                pl = place(U_O, T_O, i, 4, 2)
                for e in range(2):
                    multiply(pl, e, [(2 * e, mghi, mglo, 0, UK), (2 * e + 1, mghi, mglo, UK, UK)], T,
                             parts=(m_lo, KT + 1))
            pl = place(U_F, T_F)
            pe.wait_ge(h_lo, UK)
            multiply(pl, 0, [(0, xhi, xlo, 0, UK), (1, xhi, xlo, UK, UK)], T, parts=(h_lo, KT))
            pe.wait_ge(h_sum, KT + 1)
            mm(M[0][:, 0:T], K[:, C_ONE:C_ONE + P], hacc[:, 0:T]).then_inc(sums, 1)

            tile_x(pl, 1, 2)
            for g in range(GROUPS):
                with pe.Fori(g == 0, GT) as f:
                    pl = place(U_F + g * UF_G, T_F + g * TF_G, f, 4, 2)
                    tile_x(pl, 0, 0)
                    tile_x(pl, 1, 2)
                pe.wait_ge(f_lo, GT * g + KD[0] + 1)
                with pe.Fori(0, KT // 2) as i:
                    pl = place(U_F + g * UF_G + 4 * GT, T_F + g * TF_G + 2 * GT, i, 4, 2)
                    for e in range(2):
                        multiply(pl, e, [(2 * e, yhi, ylo, 0, KD[0]), (2 * e + 1, yhi, ylo, KD[0], KD[1])], T,
                                 parts=(f_lo, GT * (g + 1) + 1))

            for j in range(4):
                last = turn(M[1][0:2 * FT, j * P:j * P + P], ustate[:, j, :])
            last.then_inc(u_T, 1)
            turn(M[2][0:MH, 0:P], nout[:, 0, :])
            turn(M[2][0:MH, P:2 * P], nout[:, 1, :]).then_inc(n_T, 1)
            pe.wait_ge(h_sum, 2 * KT + 2)
            for u in range(3):
                last = mm(M[5][:, u:u + 1], hacc[:, u * P:u * P + P], K[:, C_ONE:C_ONE + 1])
            last.then_inc(sums, 1)
            for n in range(12):
                u, q = n // 4, n % 4
                rows = P if u < 2 else TS
                if n < 4:
                    pe.wait_ge(h_g, 4 * q + 4)
                else:
                    pe.wait_ge(y_dve if n % 2 else y_act, (n - 4) // 2 + 1)
                if n == 0:
                    pe.wait_ge(n_tok, 1)
                for k in range(4):
                    last = turn(M[n % 4][0:rows, k * P:k * P + P], hg[:, 4 * q + k, u * P:u * P + rows])
                last.then_inc(y_T, 1)

        @block.scalar
        def _(act):
            act.sem_inc(f_us, 1)
            act.sem_inc(bank_read[0], 1)
            act.sem_inc(bank_read[1], 1)

            def split(pl, *units):
                for j in units:
                    j += LEAD
                    act.wait_ge(raw_in[pl.slot(j)], pl.loads(j))
                    act.wait_ge(w_used, pl.free(j))
                    act.copy(whi[:, pl.slot(j), :, :], raw[:, pl.slot(j), :, :]).then_inc(w_hi, 1)

            def read_tile(pl, t, j, out, m=P, n=T, func=ACT.Copy, scale=1.0, bias=None):
                act.wait_ge(w_used, pl.through(j))
                kw_ = {} if bias is None else {"bias": bias}
                act.activation(out, G[t % 2][0:m, 0:n], func, scale=scale, **kw_).then_inc(bank_read[t % 2], 1)

            def token_squares(n, rows_, x):
                if n:
                    act.wait_ge(t_sq, n)
                act.activation(unused[0:rows_, :], x, ACT.Square, accum_out=tsq[0:rows_, n:n + 1]).then_inc(t_sq, 1)

            def root(done, n, v):
                act.wait_ge(variances, done)
                act.activation(v[:, 1, 0:n], v[:, 0, 0:n], ACT.Sqrt).then_inc(roots, 1)

            def x_group(g):
                for k in (4 * g, 4 * g + 2):
                    act.wait_ge(xp_done, k + 9)
                    act.copy(xT[:, k, :], M[k % 4][:, 0:T]).then_inc(xp_act, 1)
                for k in range(4 * g, 4 * g + 4):
                    act.wait_ge(n_x, KT + k + 1)
                    act.copy(xhi[:, k, :], xsc[:, k % 4, :]).then_inc(n_hi, 1)

            act.wait_ge(t_ones, 1)
            act.wait_ge(mem_in, 16)
            for n in range(2):
                token_squares(n, P, mtok[:, n, :])
            root(1, 2, mnv)
            pl = place(U_C, T_C)
            split(pl, -2, -1, 0, 1)
            with act.Fori(0, KT // 4) as i:
                for j in range(4):
                    act.wait_ge(n_x, i * 4 + (j + 1))
                    act.copy(mhi[:, i * 4 + j, :], msc[:, j, :]).then_inc(n_hi, 1)
            act.wait_ge(x_in, 32)
            for n in range(2, 4):
                token_squares(n, P, xtok[:, n - 2, :])
            token_squares(4, TS, xtos[0:TS, :])
            root(2, 3, xnv)
            x_group(0)

            def c_copies(h):
                act.wait_ge(c_xp, h + 1)
                act.copy(mvn[:, :, :], M[0][:, :].rearrange("p (m d) -> p m d", m=2)).then_inc(c_mvn, 1)
                act.copy(mkn[:, :, :], M[2][:, :].rearrange("p (m d) -> p m d", m=2)).then_inc(c_mkn, 1)

            def c_exps(h):
                act.wait_ge(c_nm, h + 1)
                for u in range(2):
                    act.activation(c_p[:, u, :], M[3][:, u * NMEM:(u + 1) * NMEM], ACT.Exp, scale=1.0 / 16,
                                   bias=c_st[:, 1, u:u + 1], accum_out=c_st[:, 2, u:u + 1])
                act.activation(c_p[0:TS, 2, :], M[4][0:TS, 0:NMEM], ACT.Exp, scale=1.0 / 16,
                               bias=c_st[0:TS, 1, 2:3], accum_out=c_st[0:TS, 2, 2:3]).then_inc(c_exp, 1)

            def c_pT0(h):
                act.wait_ge(c_pt, h + 1)
                act.copy(c_pT[:, 0, :], M[5][:, 0:T]).then_inc(c_pTa, 1)

            def c_his(h):
                for d in range(2):
                    act.wait_ge(c_pv, h * 2 + (d + 3))
                    act.copy(bhi[2][:, h * 2 + d, :], M[3 + d][:, 0:T]).then_inc(c_hi, 1)

            def c_tiles(pl, stages, shifted):
                for t in range(6):
                    if shifted is not None or t:
                        split(pl, 2 * t, 2 * t + 1)
                    if shifted is None and t < 3:
                        x_group(t + 1)
                    if shifted is None and t == 2:
                        act.wait_ge(xp_act, 8)
                        act.wait_ge(xp_dve, 8)
                        act.dma_start(scratch, xT[:, :, :].rearrange("p k t -> p (k t)")).then_inc(xT_out, 16)
                    if t % 2 == 0:
                        if t == 0 and shifted is not None:
                            act.wait_ge(c_shift, shifted)
                        read_tile(pl, t, 2 * t + 1, (mk_n[:, 0, :], mv_n[:, 0, :], cq_n[:, 0, :])[t // 2],
                                  n=NMEM if t < 4 else T)
                    if t < len(stages):
                        stages[t]()
            c_tiles(place(U_C, T_C), [], None)
            with act.Fori(1, CHD) as h:
                c_tiles(place(U_C, T_C, h, 12, 6), [lambda: c_copies(h - 1), lambda: c_exps(h - 1),
                                                    lambda: c_pT0(h - 1), lambda: c_his(h - 1)], h)

            act.wait_ge(tables_in, 16 * 3)
            pl = place(U_B, T_B)
            for t in range(10):
                split(pl, 2 * t, 2 * t + 1)
                if t == 2:
                    read_tile(pl, t, 5, ifT[0:16, :], 16, func=ACT.Identity, bias=bias16[0:16, :])
                elif t % 2 == 0:
                    if t >= 6:
                        act.wait_ge(b_rope, (t - 6) // 2 * 2 + 1)
                    read_tile(pl, t, 2 * t + 1, vraw[:, 0, :] if t == 0 else rin[:, 0, :])
                if t < 4:
                    (c_copies, c_exps, c_pT0, c_his)[t](CHD - 1)
                if t == 4:
                    act.wait_ge(b_vx, 1)
                    act.copy(vnp[:, :, :], M[0][:, :].rearrange("p (u c) -> p u c", u=2))
                    act.copy(vns[0:TS, :], M[1][0:TS, 0:256]).then_inc(b_v, 1)
                    act.wait_ge(b_gx, 1)
                    act.copy(igf[0:CH, :, :], M[5][0:CH, 0:16 * NCH].rearrange("p (c g) -> p c g", c=NCH)).then_inc(b_if, 1)
                if t == 6:
                    act.wait_ge(b_cx, 1)
                    act.copy(kTs[:, :, 0:PAST], M[3][:, :].rearrange("p (j s) -> p j s", j=2))
                    act.copy(kic[:, :], M[4][:, 0:PAST]).then_inc(b_cT, 1)
                if t == 7:
                    act.wait_ge(b_if, 1)
                    act.activation(g1[0:CH, :, :], igf[0:CH, :, MH:2 * MH], ACT.Abs).then_inc(act_own, 1)
                    act.wait_ge(act_own, 1)
                    act.activation(g1[0:CH, :, :], g1[0:CH, :, :], ACT.Exp, scale=-1.0).then_inc(act_own, 1)
                    act.wait_ge(act_own, 2)
                    act.activation(g1[0:CH, :, :], g1[0:CH, :, :], ACT.Ln, bias=1.0).then_inc(g_l, 1)

            def a_read(pl, t):
                if t == 3:
                    read_tile(pl, t, 2 * t + 1, a_nxt[:, 3, :], func=ACT.Tanh, scale=0.5)
                elif t != 1:
                    read_tile(pl, t, 2 * t + 1, a_nxt[:, t, :])

            def a_vcopies(h):
                act.wait_ge(a_s0, h + 1)
                act.copy(vn[0:CH, 0:4, :], M[2][0:CH, :].rearrange("p (c v) -> p c v", c=4))
                act.copy(vn[0:CH, 4, :], M[3][0:CH, P:2 * P])
                act.copy(Cst[:, 5, 0:P], M[3][:, 2 * P:3 * P])
                act.copy(Cst[:, 5, P:P + 1], nst[:, ds(h, 1)]).then_inc(a_vn, 1)

            def a_sdTs(h):
                act.wait_ge(a_s1, h + 1)
                act.copy(sdT[0:CH, :, :], M[0][0:CH, 0:T].rearrange("p (c s) -> p c s", c=NCH)).then_inc(a_sdT, 1)

            def a_Cout(h):
                act.wait_ge(a_s2, h + 1)
                act.copy(co[:, :, :], M[1][:, 0:2 * P].rearrange("p (g d) -> p g d", g=2)).then_inc(a_co, 1)

            def a_his(h):
                act.wait_ge(a_ga, h + 1)
                act.activation(bhi[0][:, ds(h, 1), :].rearrange("p o t -> p (o t)"), ga[:, :], ACT.Copy,
                               scale=0.5).then_inc(a_hi, 1)

            def relus(u, h0, h1):
                rows = P if u < 2 else TS
                n_ = TP if u < 2 else SS
                for h in range(h0, h1):
                    n = u * IH + h
                    act.wait_ge(i_lg, n + 1)
                    if n >= 2:
                        act.wait_ge(i_acc, n - 1)
                    act.activation(rl[0:rows, h % 2, 0:n_], (M[4] if n % 2 else M[2])[0:rows, 0:n_], ACT.Relu,
                                   scale=0.125).then_inc(i_relu, 1)

            pl = place(U_A, T_A)
            for t in range(4):
                split(pl, 2 * t, 2 * t + 1)
                a_read(pl, t)
                if t == 1:
                    act.wait_ge(b_kx, 1)
                    act.copy(kout[:, 0:2, :], M[0][:, :].rearrange("p (u c) -> p u c", u=2))
                    act.copy(kout[0:TS, 2, :], M[1][0:TS, 0:256])
                    act.copy(kiout[:, 0:2, :], M[1][:, 256:384].rearrange("p (u c) -> p u c", u=2))
                    act.copy(kiout[0:TS, 2, :], M[1][0:TS, 384:448]).then_inc(b_ko, 1)
                if t == 2:
                    relus(0, 0, IH)
                    act.wait_ge(g_arg, 1)
                    for x in (inter, wexp, enm):
                        act.activation(x[0:CH, :, :], x[0:CH, :, :], ACT.Exp)
                    act.activation(dec[:, :, :], dec[:, :, :], ACT.Exp).then_inc(g_exp, 1)
                    act.wait_ge(g_Da, 1)
                    act.activation(Dm[0:CH, :, :, :], Dm[0:CH, :, :, :], ACT.Exp).then_inc(g_De, 1)
                if t == 3:
                    relus(1, 0, IH)
                    relus(2, 0, IH)
            with act.Fori(1, MH) as h:
                pl = place(U_A, T_A, h, 8, 4)
                for t in range(4):
                    split(pl, 2 * t, 2 * t + 1)
                    if t == 0:
                        act.wait_ge(a_shift, h)
                    a_read(pl, t)
                    (a_vcopies, a_sdTs, a_Cout, a_his)[t](h - 1)

            def q_read(pl, e):
                if e == 0:
                    read_tile(pl, 0, 1, q_raw[:, 0, :])

            def q_exps(i):
                for e in range(2):
                    act.wait_ge(q_nm, i * 2 + (e + 1))
                    for u in range(2):
                        act.activation(sp_[:, e, u * TP:(u + 1) * TP], sp_[:, e, u * TP:(u + 1) * TP], ACT.Exp,
                                       bias=q_st[:, e, 1, u:u + 1], accum_out=q_st[:, e, 2, u:u + 1])
                    act.activation(ss_[0:TS, e, :], ss_[0:TS, e, :], ACT.Exp, bias=q_st[0:TS, e, 1, 2:3],
                                   accum_out=q_st[0:TS, e, 2, 2:3]).then_inc(q_exp, 1)

            def q_pTs(i):
                for e in range(2):
                    act.wait_ge(q_pt, i * 2 + (e + 1))
                    act.copy(pTp[:, e, :], M[4 + e][:, :])
                    act.copy(pTs[:, e, 0:2 * TS], M[2 * e + 1][:, 0:2 * TS])
                    act.copy(pTs[0:TS, e, 2 * TS:3 * TS], M[2 * e + 1][0:TS, 2 * TS:3 * TS]).then_inc(q_pT, 1)

            def q_his(i):
                for e in range(2):
                    act.wait_ge(q_pv, i * 2 + (e + 1))
                    act.copy(bhi[1][:, i * 2 + e, :], M[4 + e][:, 0:T]).then_inc(q_hi, 1)

            pl = place(U_Q, T_Q)
            split(pl, 0, 1)
            act.wait_ge(a_shift, MH)
            q_read(pl, 0)
            a_vcopies(MH - 1)
            a_sdTs(MH - 1)
            split(pl, 2, 3)
            a_Cout(MH - 1)
            a_his(MH - 1)
            with act.Fori(1, AH // 2) as i:
                pl = place(U_Q, T_Q, i, 4, 2)
                split(pl, 0, 1)
                act.wait_ge(q_rope, i * 2)
                q_read(pl, 0)
                q_exps(i - 1)
                split(pl, 2, 3)
                q_pTs(i - 1)
                q_his(i - 1)
            def merge_tiles(i, stages):
                pl = place(U_G, T_G, i, 36, 24)
                for n in range(4):
                    for b in range(3):
                        split(pl, 9 * n + 2 * b, 9 * n + 2 * b + 1)
                        if b == 0:
                            act.wait_ge(m_sum, i * 4 + (n + 1))
                        read_tile(pl, 6 * n + b, 9 * n + 2 * b + 1, th[:, b, :], func=ACT.Tanh, scale=0.5)
                        if n == 0 and stages:
                            stages[b](AH // 2 - 1)
                    for b in range(3):
                        split(pl, 9 * n + 6 + b)
                    act.wait_ge(m_sum, i * 4 + (n + 2))
                    act.activation(mghi[:, i * 4 + n, :], acc[:, :], ACT.Copy, scale=0.5).then_inc(m_hi, 1)
            act.wait_ge(q_rope, AH)
            merge_tiles(0, (q_exps, q_pTs, q_his))
            with act.Fori(1, KT // 4) as i:
                merge_tiles(i, ())

            def square(pl, e, k, summed):
                act.wait_ge(bank_read[e], pl.bank_read(e))
                act.wait_ge(h_sum, summed)
                act.activation(h2[:, :], hT[:, k, :], ACT.Square).then_inc(h_sq, 1)
            act.wait_ge(xT_out, 16)
            act.dma_start(hT[:, :, :].rearrange("p k t -> p (k t)"), scratch).then_inc(hT_in, 16)
            with act.Fori(0, KT // 2) as i:
                pl = place(U_O, T_O, i, 4, 2)
                for e in range(2):
                    split(pl, 2 * e, 2 * e + 1)
                    square(pl, e, i * 2 + e, i * 2 + (e + 1))
                    act.activation(xhi[:, i * 2 + e, :], hT[:, i * 2 + e, :], ACT.Identity,
                                   scale=gcols[:, 2, ds(i * 2 + e, 1)]).then_inc(h_hi, 1)

            def conv_inputs(pl, e, pair, col):
                act.copy(ext[:, e, TP + 2:TP + 4], ccols[:, 4:6, col]).then_inc(f_ext, 1)
                act.wait_ge(f_ext, pair * 2 + (e + 1))
                act.wait_ge(bank_read[e], pl.bank_read(e))
                act.activation(cbuf[:, e, 0:T + 2], ext[:, e, 2:E2], ACT.Identity, scale=ccols[:, 2, ds(col, 1)],
                               bias=ccols[:, 3, ds(col, 1)]).then_inc(f_c0, 1)
                act.copy(ustate[:, 0:2, col], ext[:, e, TP:TP + 2])
                act.copy(ustate[:, 2:4, col], ext[:, e, E2 - 2:E2]).then_inc(f_us, 1)

            def y_part(f, pair):
                act.wait_ge(f_y, pair + 2)
                act.activation(yhi[:, f, :], ybuf[:, :], ACT.Copy, scale=0.5).then_inc(f_hi, 1)

            def up(g, f, first):
                pl = place(U_F + g * UF_G, T_F + g * TF_G, f, 4, 2)
                pair = f + g * GT
                split(pl, 0, 1)
                if not first:
                    y_part(f - 1, pair - 1)
                elif g == 0:
                    root(3, T, fnv)
                conv_inputs(pl, 0, pair, pair)
                split(pl, 2, 3)
                act.wait_ge(f_conv, pair * 2 + 1)
                act.activation(gth[:, 0:T + 2], cbuf[:, 0, 0:T + 2], ACT.Tanh, scale=0.5).then_inc(f_th, 1)
                conv_inputs(pl, 1, pair, pair + FT)

            def h_tail(pl, e, k):
                square(pl, e, k, k + (KT + 2))
                act.activation(hg[:, k, :], hT[:, k, :], ACT.Identity, scale=gcols[:, 3, ds(k, 1)]).then_inc(h_g, 1)

            for g in range(GROUPS):
                up(g, 0, True)
                with act.Fori(1, GT) as f:
                    up(g, f, False)
                y_part(GT - 1, g * GT + (GT - 1))
                u0, t0 = U_F + g * UF_G + 4 * GT, T_F + g * TF_G + 2 * GT
                if g < GROUPS - 1:
                    with act.Fori(0, KT // 2) as i:
                        split(place(u0, t0, i, 4, 2), 0, 1, 2, 3)
            pl = place(u0, t0)
            split(pl, 0, 1, 2, 3)
            h_tail(pl, 0, 0)
            with act.Fori(1, KT // 2 - 1) as i:
                pl = place(u0, t0, i, 4, 2)
                split(pl, 0, 1)
                h_tail(place(u0 - 4, t0 - 2, i, 4, 2), 1, i * 2 - 1)
                split(pl, 2, 3)
                h_tail(pl, 0, i * 2)
            pl = place(UNITS - 4, T_END - 2)
            split(pl, 0, 1)
            h_tail(place(UNITS - 8, T_END - 4), 1, KT - 3)
            for e in range(2):
                h_tail(pl, e, KT - 2 + e)

            root(4, 3, fnv)
            act.wait_ge(u_T, 1)
            act.copy(cvo[0:2 * FT, :, :], M[1][0:2 * FT, :].rearrange("p (j c) -> p j c", j=4)).then_inc(u_tok, 1)
            act.wait_ge(n_T, 1)
            act.copy(nrow2[0:MH, :], M[2][0:MH, 0:2 * P]).then_inc(n_tok, 1)
            act.wait_ge(f_rms, 2)
            for n in range(0, 12, 2):
                u, q = n // 4, n % 4
                rows = P if u < 2 else TS
                act.wait_ge(y_T, n + 1)
                act.activation(ytok[0:rows, u, q * 4 * P:(q + 1) * 4 * P], M[n % 4][0:rows, :], ACT.Identity,
                               scale=fnv[0:rows, 2, u:u + 1]).then_inc(y_act, 1)

        @block.vector
        def _(dve):
            own = Steps(dve, dve_own)
            dve.sem_inc(w_lo, RING)
            dve.sem_inc(c_lo, 2)
            for s_ in (m_sum, m_lo, f_y, f_lo):
                dve.sem_inc(s_, 1)
            f32 = lambda ap: ap.bitcast(F32)

            def split(pl, *units):
                for j in units:
                    j += LEAD
                    dve.wait_ge(w_hi, pl.split(j))
                    dve.tensor_tensor(wlo[:, pl.slot(j), :, :], raw[:, pl.slot(j), :, :],
                                      f32(whi[:, pl.slot(j), :, :]), ALU.subtract).then_inc(w_lo, 1)

            def read_tile(pl, t, j, out, m=P, n=T):
                dve.wait_ge(w_used, pl.through(j))
                dve.tensor_copy(out, G[t % 2][0:m, 0:n]).then_inc(bank_read[t % 2], 1)

            def lo_part(out, x, hi, done):
                dve.tensor_tensor(out, x, f32(hi), ALU.subtract).then_inc(done, 1)

            def rms(which, n, total, v):
                dve.tensor_scalar(v[:, 0, 0:n], total, 1.0 / D, EPS, ALU.mult, ALU.add).then_inc(variances, 1)
                dve.wait_ge(roots, which + 1)
                own.did(dve.reciprocal(v[:, 2, 0:n], v[:, 1, 0:n]))
                own.settle()
                own.did(dve.tensor_tensor(v[:, 1, 0:n], v[:, 2, 0:n], v[:, 2, 0:n], ALU.mult))
                own.settle()
                own.did(dve.tensor_tensor(v[:, 1, 0:n], v[:, 1, 0:n], v[:, 0, 0:n], ALU.mult))
                own.settle()
                own.did(dve.tensor_scalar(v[:, 1, 0:n], v[:, 1, 0:n], -0.5, 1.5, ALU.mult, ALU.add))
                own.settle()
                own.did(dve.tensor_tensor(v[:, 2, 0:n], v[:, 2, 0:n], v[:, 1, 0:n], ALU.mult))

            def inverse(which, n, c0, v, bank, off, size):
                rms(which, n, tsq[:, c0:c0 + n], v)
                dve.wait_ge(ident_in, 16)
                own.settle()
                for c in range(n):
                    last = dve.tensor_scalar(idiag[:, c0 + c, :], ident, v[:, 2, c:c + 1], None, ALU.mult)
                last.then_inc(t_diag, 1)
                if which == 0:
                    dve.wait_ge(rows_T, 1)
                    dve.tensor_copy(ccols[:, 0:3, :], M[4][:, 0:264].rearrange("p (j f) -> p j f", j=3))
                    dve.tensor_copy(ccols[:, 3:6, :], M[5][:, 64:328].rearrange("p (j f) -> p j f", j=3))
                    dve.tensor_copy(gcols[:, :, :], M[5][:, 0:64].rearrange("p (g k) -> p g k", g=4))
                    dve.tensor_copy(mst[:, :], M[5][:, 400:408])
                    dve.tensor_copy(nst[:, :], M[5][:, 408:416]).then_inc(rows_out, 1)
                dve.wait_ge(t_inv, which + 1)
                own.did(dve.tensor_copy(inv[:, off:off + size], bank[:, 0:size]))
                own.settle()

            def x_copies(g):
                for k in (4 * g + 1, 4 * g + 3):
                    dve.wait_ge(xp_done, k + 9)
                    dve.tensor_copy(xT[:, k, :], M[k % 4][:, 0:T]).then_inc(xp_dve, 1)

            def x_scaled(g):
                for k in range(4 * g, 4 * g + 4):
                    dve.wait_ge(xp_dve if k % 2 else xp_act, k // 2 + 1)
                    dve.wait_ge(n_lo, KT + k + 1)
                    dve.scalar_tensor_tensor(xsc[:, k % 4, :], xT[:, k, :], gcols[:, 0, k:k + 1],
                                             inv[:, NMEM:NMEM + T], ALU.mult, ALU.mult).then_inc(n_x, 1)

            dve.memset(tsq[:, :], 1.0).then_inc(t_ones, 1)
            dve.sem_inc(n_lo, 4)
            dve.wait_ge(t_sq, 2)
            inverse(0, 2, 0, mnv, M[4], 0, NMEM)
            with dve.Fori(0, KT // 8) as i:
                for j in range(8):
                    dve.wait_ge(xp_done, i * 4 + (j // 2 + 1))
                    dve.wait_ge(n_lo, i * 8 + (j + 1))
                    dve.scalar_tensor_tensor(msc[:, j % 4, :], M[j // 2][:, j % 2 * NMEM:(j % 2 + 1) * NMEM],
                                             gcols[:, 1, ds(i * 8 + j, 1)], inv[:, 0:NMEM],
                                             ALU.mult, ALU.mult).then_inc(n_x, 1)
            pl = place(U_C, T_C)
            split(pl, -2, -1)
            x_copies(0)
            split(pl, 0, 1)
            dve.wait_ge(t_sq, 5)
            inverse(1, 3, 2, xnv, M[5], NMEM, T)
            x_scaled(0)

            def x_group(g):
                x_copies(g)
                x_scaled(g)

            def c_keys(h):
                dve.wait_ge(c_xp, h + 1)
                dve.tensor_copy(ckT[:, :, :], M[1][:, :].rearrange("p (d m) -> p d m", d=2)).then_inc(c_ckT, 1)

            def c_softmax(h):
                dve.wait_ge(c_sc, h + 1)
                dve.tensor_reduce(c_st[:, 0, 0:2], M[3][:, :].rearrange("p (u m) -> p u m", u=2), AX.X, ALU.max)
                own.did(dve.tensor_reduce(c_st[0:TS, 0, 2:3], M[4][0:TS, 0:NMEM], AX.X, ALU.max))
                own.settle()
                dve.tensor_scalar(c_st[:, 1, 0:2], c_st[:, 0, 0:2], -1.0 / 16, None, ALU.mult)
                dve.tensor_scalar(c_st[0:TS, 1, 2:3], c_st[0:TS, 0, 2:3], -1.0 / 16, None, ALU.mult).then_inc(c_nm, 1)
                dve.wait_ge(c_exp, h + 1)
                dve.reciprocal(c_st[:, 3, 0:2], c_st[:, 2, 0:2])
                own.did(dve.reciprocal(c_st[0:TS, 3, 2:3], c_st[0:TS, 2, 2:3]))
                own.settle()
                for u in range(2):
                    dve.tensor_scalar(c_p[:, u, :], c_p[:, u, :], c_st[:, 3, u:u + 1], None, ALU.mult)
                dve.tensor_scalar(c_p[0:TS, 2, :], c_p[0:TS, 2, :], c_st[0:TS, 3, 2:3], None, ALU.mult).then_inc(c_pn, 1)

            def c_pT1(h):
                dve.wait_ge(c_pt, h + 1)
                dve.tensor_copy(c_pT[:, 1, :], M[2][:, 0:T]).then_inc(c_pTd, 1)

            def c_los(h):
                for d in range(2):
                    dve.wait_ge(c_hi, h * 2 + (d + 1))
                    lo_part(blo[2][:, h * 2 + d, :], M[3 + d][:, 0:T], bhi[2][:, h * 2 + d, :], c_lo)
            c_stages = (c_keys, c_softmax, c_pT1, c_los)

            def c_tiles(pl, stages, shifted):
                for t in range(6):
                    if shifted is not None or t:
                        split(pl, 2 * t, 2 * t + 1)
                    if shifted is None and t < 3:
                        x_group(t + 1)
                    if t % 2 == 1:
                        if t == 1 and shifted is not None:
                            dve.wait_ge(c_shift, shifted)
                        read_tile(pl, t, 2 * t + 1, (mk_n[:, 1, :], mv_n[:, 1, :], cq_n[:, 1, :])[t // 2],
                                  n=NMEM if t < 4 else T)
                    if t < len(stages):
                        stages[t]()
            c_tiles(pl, [], None)
            with own.loop(1, CHD, 2) as h:
                c_tiles(place(U_C, T_C, h, 12, 6), [lambda: c_keys(h - 1), lambda: c_softmax(h - 1),
                                                    lambda: c_pT1(h - 1), lambda: c_los(h - 1)], h)

            dve.wait_ge(tables_in, 16 * 3)

            def rope(x, bank, cos, sin, tmp, out, done, *waits):
                for w in waits:
                    dve.wait_ge(*w)
                own.did(dve.tensor_tensor(tmp, bank[:, 0:T], sin, ALU.mult))
                own.did(dve.tensor_tensor(x, x, cos, ALU.mult))
                own.settle()
                for n, (dst, lo, hi) in enumerate(out):
                    last = dve.tensor_tensor(dst, tmp[:, lo:hi], x[:, lo:hi], ALU.add)
                last.then_inc(done, 1)
            cos64, sin64 = K[:, C_COS64:C_COS64 + T], K[:, C_SIN64:C_SIN64 + T]
            cos128, sin128 = K[:, C_COS128:C_COS128 + T], K[:, C_SIN128:C_SIN128 + T]
            pl = place(U_B, T_B)
            for t in range(10):
                split(pl, 2 * t, 2 * t + 1)
                if t % 2 == 1:
                    if t == 3:
                        read_tile(pl, t, 7, kiw[0:72, :], 72)
                    else:
                        if t >= 7:
                            dve.wait_ge(b_rope, t - 5)
                        read_tile(pl, t, 2 * t + 1, vraw[:, 1, :] if t == 1 else rin[:, 1, :])
                if t < 4:
                    c_stages[t](CHD - 1)
                if t == 4:
                    dve.wait_ge(b_gx, 1)
                    dve.tensor_scalar(iw[:, 0:2, :], M[2][:, 0:144].rearrange("p (u c) -> p u c", u=2)[:, :, 64:72],
                                      IH ** -0.5, None, ALU.mult)
                    dve.tensor_scalar(iw[0:TS, 2, :], M[2][0:TS, 208:216], IH ** -0.5, None, ALU.mult).then_inc(b_iw, 1)
                if t == 5:
                    dve.wait_ge(b_kix, 1)
                    own.did(dve.tensor_tensor(ki2[:, :], M[3][:, 0:T], cos64, ALU.mult))
                    own.did(dve.tensor_tensor(rtmp[:, :], M[4][:, 0:T], sin64, ALU.mult))
                    own.settle()
                    dve.tensor_tensor(ki2[:, :], ki2[:, :], rtmp[:, :], ALU.add).then_inc(b_ki, 1)
                if t >= 5:
                    n = t - 5
                    bank = M[(0, 1, 2, 5, 0)[n]]
                    if n < 4:
                        rope(rin[:, (t - 1) % 2, :], bank, cos64, sin64, rtmp[:, :], [(iqT[:, n, :], 0, T)], b_rope,
                             (b_rot, n + 1), (b_rope, n) if n else (b_ki, 1))
                    else:
                        rope(rin[:, 0, :], bank, cos128, sin128, rtmp[:, :],
                             [(kTp[:, 0, :], 0, TP), (kTs[:, 0, PAST:SS], TP, T)], b_rope, (b_rot, 5), (b_rope, 4))
                if t == 8:
                    dve.wait_ge(g_l, 1)
                    dve.scalar_tensor_tensor(g2[0:CH, :, :], igf[0:CH, :, MH:2 * MH], 0.0, g1[0:CH, :, :],
                                             ALU.min, ALU.subtract).then_inc(g_lf, 1)

            def over(ap, n):
                return ap.unsqueeze(2).broadcast_to([ap.shape[0], ap.shape[1], n])

            def a_decay(h):
                dve.wait_ge(a_s0, h + 1)
                dve.tensor_tensor(SD[0:CH, :, :], M[0][0:CH, 0:T].rearrange("p (c s) -> p c s", c=NCH),
                                  Dm[0:CH, :, h, :], ALU.mult).then_inc(a_sd, 1)
                dve.tensor_tensor(kw[0:CH, 0:4, :], M[1][0:CH, :].rearrange("p (c d) -> p c d", c=4),
                                  over(wexp[0:CH, 0:4, h], P), ALU.mult)
                dve.wait_ge(a_vn, h + 1)
                dve.tensor_scalar(kw[0:CH, 4, :], M[3][0:CH, 0:P], wexp[0:CH, 4, ds(h, 1)], None, ALU.mult)\
                   .then_inc(a_kw, 1)
                dve.wait_ge(a_sd, h + 1)
                own.did(dve.tensor_reduce(a_st[0:CH, 0, 0:NCH], SD[0:CH, :, :], AX.X, ALU.add))

            def a_recur(h):
                dve.wait_ge(a_s1, h + 1)
                dve.wait_ge(a_vn, h + 1)
                for c in range(NCH):
                    src, dst = (c, c + 1) if c < 4 else (5, 6)
                    kv = M[1][:, c * P:c * P + P] if c < 4 else M[3][:, 0:P]
                    d = dec[:, c, ds(h, 1)]
                    dve.scalar_tensor_tensor(Cst[:, dst, 0:P], Cst[:, src, 0:P], d, kv, ALU.mult, ALU.add)
                    own.did(dve.scalar_tensor_tensor(Cst[:, dst, P:P + 1], Cst[:, src, P:P + 1], d, M[5][:, c:c + 1],
                                                     ALU.mult, ALU.add))
                    own.settle()
                dve.tensor_copy(nout[:, 0, ds(h, 1)], Cst[:, 4, P:P + 1])
                dve.tensor_copy(nout[:, 1, ds(h, 1)], Cst[:, 6, P:P + 1]).then_inc(a_C, 1)

            def a_combine(h):
                dve.wait_ge(a_s2, h + 1)
                den, ih = a_st[0:CH, 1, 0:NCH], inter[0:CH, :, h]
                own.did(dve.tensor_tensor(den, M[5][0:CH, 8:8 + NCH], ih, ALU.mult))
                dve.tensor_tensor(hn[0:CH, 0:4, :], M[4][0:CH, :].rearrange("p (c v) -> p c v", c=4),
                                  over(inter[0:CH, 0:4, h], P), ALU.mult)
                own.did(dve.tensor_scalar(hn[0:CH, 4, :], M[5][0:CH, 2 * P:3 * P], inter[0:CH, 4, ds(h, 1)], None, ALU.mult))
                own.settle()
                own.did(dve.tensor_tensor(den, den, a_st[0:CH, 0, 0:NCH], ALU.add))
                dve.tensor_tensor(hn[0:CH, 0:4, :], hn[0:CH, 0:4, :], M[2][0:CH, :].rearrange("p (c v) -> p c v", c=4), ALU.add)
                own.did(dve.tensor_tensor(hn[0:CH, 4, :], hn[0:CH, 4, :], M[5][0:CH, P:2 * P], ALU.add))
                own.settle()
                own.did(dve.scalar_tensor_tensor(den, den, -1.0, den, ALU.mult, ALU.max))
                own.settle()
                own.did(dve.tensor_tensor(den, den, enm[0:CH, :, h], ALU.max))
                own.settle()
                own.did(dve.reciprocal(den, den))
                own.settle()
                dve.tensor_tensor(hn[0:CH, :, :], hn[0:CH, :, :], over(den, P), ALU.mult).then_inc(a_h, 1)

            def a_gate(h):
                dve.wait_ge(a_s3, h + 1)
                dve.scalar_tensor_tensor(ga[:, :], s_c, 1.0, M[4][:, 0:T], ALU.add, ALU.mult).then_inc(a_ga, 1)
                dve.wait_ge(a_hi, h + 1)
                dve.scalar_tensor_tensor(blo[0][:, h, :], ga[:, :], 0.5, f32(bhi[0][:, h, :]), ALU.mult, ALU.subtract)\
                   .then_inc(a_lo, 1)
            a_stages = (a_decay, a_recur, a_combine, a_gate)

            score = [msk[0:P, 0:TP], msk[0:P, TP:2 * TP], msk[0:TS, 2 * TP:2 * TP + SS]]

            def scores_u(u):
                rows, n_ = (P, TP) if u < 2 else (TS, SS)
                for h in range(IH):
                    n = u * IH + h
                    dve.wait_ge(i_relu, n + 1)
                    w = iw[0:rows, u, h:h + 1]
                    if h == 0:
                        dve.tensor_scalar(score[u], rl[0:rows, 0, 0:n_], w, None, ALU.mult).then_inc(i_acc, 1)
                    else:
                        dve.wait_ge(i_acc, n)
                        dve.scalar_tensor_tensor(score[u], rl[0:rows, h % 2, 0:n_], w, score[u],
                                                 ALU.mult, ALU.add).then_inc(i_acc, 1)

            def select(*us):
                for u in us:
                    own.did(dve.max(top8[0:P if u < 2 else TS, u, :], score[u]))
                own.settle()
                dve.sem_inc(dve_passed, 1)
                for u in us:
                    own.did(dve.match_replace(score[u], top8[0:P if u < 2 else TS, u, :], score[u], TAKEN))
                own.settle()

            ROUNDS = (TOPK_P // 8 - (MH - 1), TOPK_S // 8 - (MH - 1))
            pl = place(U_A, T_A)
            for t in range(4):
                split(pl, 2 * t, 2 * t + 1)
                if t == 1:
                    dve.wait_ge(w_used, pl.through(3))
                    dve.tensor_scalar(a_nxt[:, 1, :], G[1][:, 0:T], P ** -0.5, None, ALU.mult).then_inc(bank_read[1], 1)
                if t == 0:
                    rope(rin[:, 1, :], M[1], cos128, sin128, rtmp[:, :],
                         [(kTp[:, 1, :], 0, TP), (kTs[:, 1, PAST:SS], TP, T)], b_rope, (b_rot, 6), (b_rope, 5))
                    dve.wait_ge(g_b, 1)
                    own.did(dve.tensor_copy(bcs[0:CH, :, :], M[5][0:CH, 0:NCH * MH].rearrange("p (c h) -> p c h", c=NCH)))
                    own.settle()
                    own.did(dve.tensor_tensor(acs[0:CH, :, :], igf[0:CH, :, 0:MH], bcs[0:CH, :, :], ALU.subtract))
                    own.settle()
                    dve.wait_ge(c_out, 32 * CHD)
                    eye = ident[0:CH, 0:CH].unsqueeze(1).broadcast_to([CH, MH, CH])
                    for c in range(NCH):
                        last = dve.tensor_tensor(diag[0:CH, c, :, :], eye, over(acs[0:CH, c, :], CH), ALU.mult)
                    last.then_inc(g_dg, 1)
                if t in (1, 2):
                    caus = K[0:CH, C_CAUS:C_CAUS + CH].unsqueeze(1).broadcast_to([CH, MH, CH])
                    for c in range(4) if t == 1 else (4,):
                        dve.wait_ge(g_R, c + 1)
                        dve.tensor_tensor(Dm[0:CH, c, :, :],
                                          M[(3, 5, 2, 4, 3)[c]][0:CH, :].rearrange("p (h s) -> p h s", h=MH),
                                          over(bcs[0:CH, c, :], CH), ALU.add).then_inc(g_D, 1)
                        dve.wait_ge(g_D, c + 1)
                        own.did(dve.tensor_tensor(Dm[0:CH, c, :, :], Dm[0:CH, c, :, :], caus, ALU.add))
                        own.settle()
                        own.did(dve.tensor_reduce(mxs[0:CH, c, :], Dm[0:CH, c, :, :], AX.X, ALU.max))
                if t == 2:
                    scores_u(0)
                    for c in range(NCH):
                        own.settle()
                        if c == 0:
                            own.did(dve.tensor_copy(mint[0:CH, 0, :], bcs[0:CH, 0, :]))
                        else:
                            before = mst[:, :] if c == 4 else mnew[:, c - 1, :]
                            own.did(dve.tensor_tensor(mint[0:CH, c, :], bcs[0:CH, c, :], before[0:CH, :], ALU.add))
                        own.settle()
                        dve.tensor_tensor(mb[0:CH, c, 0, :], mint[0:CH, c, :], mxs[0:CH, c, :], ALU.max)
                        dve.tensor_copy(mb[0:CH, c, 1, :], bcs[0:CH, c, :]).then_inc(g_mb, 1)
                        dve.wait_ge(g_last, c + 1)
                        dve.tensor_copy(blast[:, c, :], M[3][:, 16 * c + 8:16 * c + 16])
                        own.did(dve.tensor_copy(mnew[:, c, :], M[3][:, 16 * c:16 * c + 8]))
                        own.settle()
                        if c == 0:
                            own.did(dve.tensor_tensor(dec[:, c, :], blast[:, c, :], mnew[:, c, :], ALU.subtract))
                        else:
                            own.did(dve.tensor_tensor(dec[:, c, :], blast[:, c, :], before, ALU.add))
                            own.settle()
                            own.did(dve.tensor_tensor(dec[:, c, :], dec[:, c, :], mnew[:, c, :], ALU.subtract))
                    own.settle()
                    m_t = mb[0:CH, :, 0, :]
                    own.did(dve.tensor_tensor(inter[0:CH, :, :], mint[0:CH, :, :], m_t, ALU.subtract))
                    own.did(dve.tensor_scalar(enm[0:CH, :, :], m_t, -1.0, None, ALU.mult))
                    own.did(dve.tensor_tensor(wexp[0:CH, :, :], blast[0:CH, :, :], mnew[0:CH, :, :], ALU.subtract))
                    own.settle()
                    dve.tensor_tensor(wexp[0:CH, :, :], wexp[0:CH, :, :], acs[0:CH, :, :], ALU.add).then_inc(g_arg, 1)
                    for c in range(NCH):
                        last = dve.tensor_tensor(Dm[0:CH, c, :, :], Dm[0:CH, c, :, :], over(mb[0:CH, c, 0, :], CH),
                                                 ALU.subtract)
                    last.then_inc(g_Da, 1)
                if t == 3:
                    scores_u(1)
                    scores_u(2)
                    dve.wait_ge(i_acc, 3 * IH)
                    own.did(dve.tensor_tensor(msk[:, 0:2 * TP], msk[:, 0:2 * TP], K[:, C_ADM:C_ADM + 2 * TP], ALU.add))
                    own.settle()
                    for n in range(max(ROUNDS)):
                        select(*[u for u in range(3) if n < ROUNDS[u // 2]])
            dve.wait_ge(a_shift, 1)
            own.did(dve.memset(Cst[:, 0, :], 0.0))
            own.settle()
            dve.wait_ge(g_exp, 1)
            dve.wait_ge(g_De, 1)
            with own.loop(1, MH, 19) as h:
                pl = place(U_A, T_A, h, 8, 4)
                for t in range(4):
                    split(pl, 2 * t, 2 * t + 1)
                    if t == 1:
                        dve.wait_ge(a_shift, h)
                        dve.wait_ge(w_used, pl.through(3))
                        dve.tensor_scalar(a_nxt[:, 1, :], G[1][:, 0:T], P ** -0.5, None, ALU.mult).then_inc(bank_read[1], 1)
                    a_stages[t](h - 1)
                    if t == 3:
                        select(0, 1, 2)
            for u in range(3):
                own.did(dve.tensor_scalar(score[u], score[u], -2e38, NEG, ALU.is_gt, ALU.mult))

            own.settle()

            def q_softmax(i):
                for e in range(2):
                    p_, s_, st = sp_[:, e, :], ss_[0:TS, e, :], q_st[:, e, :, :]
                    dve.wait_ge(q_sc, i * 2 + (e + 1))
                    dve.scalar_tensor_tensor(p_, M[2 * e][:, :], P ** -0.5, msk[:, 0:2 * TP], ALU.mult, ALU.add)
                    own.did(dve.scalar_tensor_tensor(s_, M[2 * e + 1][0:TS, 0:SS], P ** -0.5, msk[0:TS, 2 * TP:2 * TP + SS],
                                                     ALU.mult, ALU.add))
                    own.settle()
                    dve.tensor_reduce(st[:, 0, 0:2], p_.rearrange("p (u s) -> p u s", u=2), AX.X, ALU.max)
                    own.did(dve.tensor_reduce(st[0:TS, 0, 2:3], s_, AX.X, ALU.max))
                    own.settle()
                    dve.tensor_scalar(st[:, 1, 0:2], st[:, 0, 0:2], -1.0, None, ALU.mult)
                    dve.tensor_scalar(st[0:TS, 1, 2:3], st[0:TS, 0, 2:3], -1.0, None, ALU.mult).then_inc(q_nm, 1)
                for e in range(2):
                    st = q_st[:, e, :, :]
                    dve.wait_ge(q_exp, i * 2 + (e + 1))
                    dve.reciprocal(st[:, 3, 0:2], st[:, 2, 0:2])
                    own.did(dve.reciprocal(st[0:TS, 3, 2:3], st[0:TS, 2, 2:3]))
                    own.settle()
                    for u in range(2):
                        p_ = sp_[:, e, u * TP:(u + 1) * TP]
                        dve.tensor_scalar(p_, p_, st[:, 3, u:u + 1], None, ALU.mult)
                    dve.tensor_scalar(ss_[0:TS, e, :], ss_[0:TS, e, :], st[0:TS, 3, 2:3], None, ALU.mult).then_inc(q_pn, 1)

            def q_ropes(i, first=False):
                for e in range(2):
                    before = [] if first and e == 0 else [(q_rope, i * 2 + e)]
                    rope(q_raw[:, e, :], M[2 * e], cos128, sin128, q_tmp[:, :], [(q_nxt[:, e, :], 0, T)], q_rope,
                         (q_rot, i * 2 + (e + 1)), *before)

            def q_los(i):
                for e in range(2):
                    dve.wait_ge(q_hi, i * 2 + (e + 1))
                    lo_part(blo[1][:, i * 2 + e, :], M[4 + e][:, 0:T], bhi[1][:, i * 2 + e, :], q_lo)

            pl = place(U_Q, T_Q)
            split(pl, 0, 1)
            a_decay(MH - 1)
            a_recur(MH - 1)
            split(pl, 2, 3)
            read_tile(pl, 1, 3, q_raw[:, 1, :])
            a_combine(MH - 1)
            a_gate(MH - 1)
            q_ropes(0, True)
            with own.loop(1, AH // 2, 10) as i:
                pl = place(U_Q, T_Q, i, 4, 2)
                split(pl, 0, 1)
                q_softmax(i - 1)
                split(pl, 2, 3)
                dve.wait_ge(q_rope, i * 2)
                read_tile(pl, 1, 3, q_raw[:, 1, :])
                dve.wait_ge(q_shift, i)
                q_ropes(i)
                q_los(i - 1)
            def merge_tiles(i, stages):
                pl = place(U_G, T_G, i, 36, 24)
                for n in range(4):
                    for b in range(3):
                        split(pl, 9 * n + 2 * b, 9 * n + 2 * b + 1)
                        if n == 0 and stages and stages[b]:
                            stages[b](AH // 2 - 1)
                    for b in range(3):
                        t = 6 * n + 3 + b
                        split(pl, 9 * n + 6 + b)
                        dve.wait_ge(w_used, pl.through(9 * n + 6 + b))
                        if b == 0:
                            dve.wait_ge(m_lo, i * 4 + (n + 1))
                        dve.scalar_tensor_tensor(gtmp[:, :] if b else acc[:, :], th[:, b, :], 1.0, G[t % 2][:, 0:T],
                                                 ALU.add, ALU.mult).then_inc(bank_read[t % 2], 1)
                        dve.wait_ge(bank_read[t % 2], pl.bank_read(t))
                        if b:
                            add = dve.tensor_tensor(acc[:, :], acc[:, :], gtmp[:, :], ALU.add)
                            if b == 1:
                                own.did(add)
                                own.settle()
                            else:
                                add.then_inc(m_sum, 1)
                    dve.wait_ge(m_hi, i * 4 + (n + 1))
                    dve.scalar_tensor_tensor(mglo[:, i * 4 + n, :], acc[:, :], 0.5, f32(mghi[:, i * 4 + n, :]),
                                             ALU.mult, ALU.subtract).then_inc(m_lo, 1)
            merge_tiles(0, (q_softmax, None, q_los))
            with own.loop(1, KT // 4, 4) as i:
                merge_tiles(i, ())

            def add_h(pl, e, k):
                dve.wait_ge(w_used, pl.through(2 * e + 1))
                dve.tensor_tensor(hT[:, k, :], hT[:, k, :], G[e][:, 0:T], ALU.add).then_inc(bank_read[e], 1)

            def add_square(squared, summed):
                dve.wait_ge(h_sq, squared)
                dve.wait_ge(h_sum, summed)
                dve.tensor_tensor(hacc[:, 0:T], hacc[:, 0:T], h2[:, :], ALU.add).then_inc(h_sum, 1)

            dve.memset(hacc[:, :], 0.0).then_inc(h_sum, 1)
            with dve.Fori(0, KT // 2) as i:
                pl = place(U_O, T_O, i, 4, 2)

                def parts(e):
                    k = i * 2 + e
                    add_square(i * 2 + (e + 1), i * 2 + (e + 1))
                    dve.wait_ge(h_hi, i * 2 + (e + 1))
                    dve.scalar_tensor_tensor(xlo[:, k, :], hT[:, k, :], gcols[:, 2, ds(k, 1)], f32(xhi[:, k, :]),
                                             ALU.mult, ALU.subtract).then_inc(h_lo, 1)
                split(pl, 0, 1)
                dve.wait_ge(hT_in, 16)
                add_h(pl, 0, i * 2)
                split(pl, 2, 3)
                parts(0)
                add_h(pl, 1, i * 2 + 1)
                parts(1)
            own.did(dve.memset(ext[:, :, 0:2], 0.0))

            def taps(e, pair, col, pl):
                dve.wait_ge(w_used, pl.through(2 * e + 1))
                dve.wait_ge(f_us, pair * 2 + (e + 1))
                dve.tensor_tensor(ext[:, e, 2:2 + TP], G[e][:, 0:TP], fnv[:, 2, 0:TP], ALU.mult)
                dve.tensor_tensor(ext[:, e, TP + 4:E2], G[e][:, TP:T], fnv[:, 2, TP:T], ALU.mult).then_inc(bank_read[e], 1)
                dve.wait_ge(bank_read[e], pl.bank_read(e))
                dve.wait_ge(f_c0, pair * 2 + (e + 1))
                c = cbuf[:, e, 0:T + 2]
                own.did(dve.scalar_tensor_tensor(c, ext[:, e, 1:T + 3], ccols[:, 1, ds(col, 1)], c, ALU.mult, ALU.add))
                own.settle()
                dve.scalar_tensor_tensor(c, ext[:, e, 0:T + 2], ccols[:, 0, ds(col, 1)], c, ALU.mult, ALU.add)\
                   .then_inc(f_conv, 1)

            def silu(pair):
                dve.wait_ge(f_th, pair + 1)
                own.did(dve.scalar_tensor_tensor(gth[:, 0:T + 2], gth[:, 0:T + 2], 1.0, cbuf[:, 0, 0:T + 2],
                                                 ALU.add, ALU.mult))

            def y_part(f, pair):
                dve.wait_ge(f_conv, pair * 2 + 2)
                dve.wait_ge(f_lo, pair + 1)
                own.did(dve.tensor_tensor(ybuf[:, 0:TP], gth[:, 0:TP], cbuf[:, 1, 0:TP], ALU.mult))
                dve.tensor_tensor(ybuf[:, TP:T], gth[:, TP + 2:T + 2], cbuf[:, 1, TP + 2:T + 2], ALU.mult).then_inc(f_y, 1)
                dve.wait_ge(f_hi, pair + 1)
                dve.scalar_tensor_tensor(ylo[:, f, :], ybuf[:, :], 0.5, f32(yhi[:, f, :]), ALU.mult, ALU.subtract)\
                   .then_inc(f_lo, 1)

            def up(g, f, first):
                pl = place(U_F + g * UF_G, T_F + g * TF_G, f, 4, 2)
                pair = f + g * GT
                split(pl, 0, 1)
                if not first:
                    y_part(f - 1, pair - 1)
                elif g == 0:
                    dve.wait_ge(sums, 1)
                    rms(2, T, M[0][:, 0:T], fnv)
                    own.settle()
                taps(0, pair, pair, pl)
                split(pl, 2, 3)
                silu(pair)
                taps(1, pair, pair + FT, pl)

            for g in range(GROUPS):
                up(g, 0, True)
                with own.loop(1, GT, 4) as f:
                    up(g, f, False)
                y_part(GT - 1, g * GT + (GT - 1))
                u0, t0 = U_F + g * UF_G + 4 * GT, T_F + g * TF_G + 2 * GT
                if g < GROUPS - 1:
                    with dve.Fori(0, KT // 2) as i:
                        pl = place(u0, t0, i, 4, 2)
                        for e in range(2):
                            split(pl, 2 * e, 2 * e + 1)
                            add_h(pl, e, i * 2 + e)
            dve.wait_ge(variances, 3)
            dve.memset(hacc[:, :], 0.0).then_inc(h_sum, 1)
            pl = place(u0, t0)
            split(pl, 0, 1)
            add_h(pl, 0, 0)
            split(pl, 2, 3)
            add_square(KT + 1, KT + 2)
            add_h(pl, 1, 1)
            with dve.Fori(1, KT // 2 - 1) as i:
                pl = place(u0, t0, i, 4, 2)
                split(pl, 0, 1)
                add_square(i * 2 + KT, i * 2 + (KT + 1))
                add_h(pl, 0, i * 2)
                split(pl, 2, 3)
                add_square(i * 2 + (KT + 1), i * 2 + (KT + 2))
                add_h(pl, 1, i * 2 + 1)
            pl = place(UNITS - 4, T_END - 2)
            split(pl, 0, 1)
            add_square(2 * KT - 2, 2 * KT - 1)
            for e in range(2):
                add_h(pl, e, KT - 2 + e)
                add_square(2 * KT - 1 + e, 2 * KT + e)
            dve.wait_ge(sums, 2)
            rms(3, 3, M[5][:, 0:3], fnv)
            dve.wait_ge(dve_own, own.n)
            dve.sem_inc(f_rms, 2)
            for n in range(1, 12, 2):
                u, q = n // 4, n % 4
                rows = P if u < 2 else TS
                dve.wait_ge(y_T, n + 1)
                dve.tensor_scalar(ytok[0:rows, u, q * 4 * P:(q + 1) * 4 * P], M[n % 4][0:rows, :],
                                  fnv[0:rows, 2, u:u + 1], None, ALU.mult).then_inc(y_dve, 1)

        @block.gpsimd
        def _(pool):
            def wait(s_, value):
                pool.wait_ge(s_, value)
                pool.sem_inc(pool_passed, 1)
            mk_src = a["cache_mem_k"][0, 0].rearrange("(m p) h d -> h p m d", p=P)
            mv_src = a["cache_mem_v"][0, 0].rearrange("(m p) h d -> h p m d", p=P)
            mk_dst = o["p_mem_k"][0, 0].rearrange("(m p) h d -> h p m d", p=P)
            mv_dst = o["p_mem_v"][0, 0].rearrange("(m p) h d -> h p m d", p=P)

            def c_load(h):
                pool.dma_start(ck[:, :, :], mk_src[h]).then_inc(c_cache, 16)
                pool.dma_start(cv[:, :, :], mv_src[h]).then_inc(c_cache, 16)

            def c_move(h):
                pl = place(U_C, T_C, h, 12, 6)
                wait(bank_read[0], pl.bank_read(4))
                wait(bank_read[1], pl.bank_read(5))
                pool.tensor_copy(c_cur[:, :], c_nxt[:, :]).then_inc(c_shift, 1)

            def c_store(h):
                wait(c_mvn, h + 1)
                pool.dma_start(mv_dst[h], mvn[:, :, :]).then_inc(c_out, 16)
                wait(c_mkn, h + 1)
                pool.dma_start(mk_dst[h], mkn[:, :, :]).then_inc(c_out, 16)

            def lo_parts(which, hi, lo, x):
                with pool.Fori(0, KT // 4) as i:
                    for j in range(4):
                        wait(n_hi, i * 4 + (which * KT + j + 1))
                        pool.tensor_tensor(lo[:, i * 4 + j, :], x[:, j, :], hi[:, i * 4 + j, :].bitcast(F32),
                                           ALU.subtract).then_inc(n_lo, 1)
            c_load(0)
            lo_parts(0, mhi, mlo, msc)
            pool.wait_ge(n_lo, KT + 4)
            lo_parts(1, xhi, xlo, xsc)
            pool.wait_ge(n_lo, 2 * KT + 4)
            pool.wait_ge(xT_out, 16)
            pool.dma_start(cvB[:, :, :], a["cache_dsa_v"][0, 0].rearrange("(u p) j d -> p u (j d)", p=P)).then_inc(cache_in, 16)
            c_move(0)
            with pool.Fori(1, CHD) as h:
                c_store(h - 1)
                wait(c_pv, h * 2 + 2)
                c_load(h)
                wait(c_out, h * 32)
                c_move(h)
            pool.dma_start(ckB[:, :, :], a["cache_dsa_k"][0, 0].rearrange("(u p) j d -> p u (j d)", p=P)).then_inc(cache_in, 16)
            for n in range(2):
                pool.dma_start(ckI[:, :, n, :], a["cache_dsa_kidx"][0, 0].rearrange("(u p) d -> p u d", p=P))\
                    .then_inc(cache_in, 16)
            c_store(CHD - 1)

            def store(dst_p, dst_s, src_p, src_s, done):
                pool.dma_start(dst_p.rearrange("(u p) n -> p u n", p=P), src_p).then_inc(done, 16)
                pool.dma_start(dst_s, src_s).then_inc(done, 16)

            pool.wait_ge(b_v, 1)
            store(o["p_v"][0, 0].rearrange("t j d -> t (j d)"), o["s_v"][0, 0].rearrange("t j d -> t (j d)"),
                  vnp[:, :, :], vns[0:TS, :], b_vo)
            pool.wait_ge(b_ko, 1)
            store(o["p_k"][0, 0].rearrange("t j d -> t (j d)"), o["s_k"][0, 0].rearrange("t j d -> t (j d)"),
                  kout[:, 0:2, :], kout[0:TS, 2, :], b_kio)
            store(o["p_kidx"][0, 0], o["s_kidx"][0, 0], kiout[:, 0:2, :], kiout[0:TS, 2, :], b_kio)
            pool.wait_ge(g_arg, 1)
            pool.dma_start(o["p_m"][0], mnew[0:1, 3, :]).then_inc(g_mo, 16)
            pool.dma_start(o["s_m"][0], mnew[0:1, 4, :]).then_inc(g_mo, 16)

            def a_load(h):
                pool.dma_start(cs[:, :], a["state_mlstm_C"][0, 0][h]).then_inc(a_cs, 16)

            def a_move(h):
                pl = place(U_A, T_A, h, 8, 4)
                wait(bank_read[0], pl.bank_read(2))
                wait(bank_read[1], pl.bank_read(3))
                pool.tensor_copy(a_cur[:, :, :], a_nxt[:, :, :]).then_inc(a_shift, 1)

            def a_store(h):
                wait(a_co, h + 1)
                pool.dma_start(o["p_C"][0, 0][h], co[:, 0, :]).then_inc(a_out, 16)
                pool.dma_start(o["s_C"][0, 0][h], co[:, 1, :]).then_inc(a_out, 16)
            pool.wait_ge(c_out, 32 * CHD)
            pool.wait_ge(b_kio, 64)
            a_load(0)
            a_move(0)
            with pool.Fori(1, MH) as h:
                wait(a_s0, h)
                a_load(h)
                a_store(h - 1)
                wait(a_lo, h)
                wait(a_out, h * 32)
                a_move(h)
            a_store(MH - 1)

            def q_move(i):
                j = i // 2
                wait(q_rope, i * 2 + 2)
                pool.tensor_copy(q_cur[:, :, :], q_nxt[:, :, :])
                pool.tensor_copy(v_cur[:, 0:2, :], vnp[:, :, ds(j * P, P)])
                pool.tensor_copy(v_cur[:, 2:4, :], cvB[:, :, ds(j * P, P)])
                pool.tensor_copy(v_cur[0:TS, 4, :], vns[0:TS, ds(j * P, P)]).then_inc(q_shift, 1)
            pool.wait_ge(b_vo, 32)
            pool.wait_ge(g_mo, 32)
            pool.wait_ge(a_out, 32 * MH)
            q_move(0)
            with pool.Fori(1, AH // 2) as i:
                wait(q_pv, i * 2)
                q_move(i)

            pool.wait_ge(u_tok, 1)
            for n, name in enumerate(("p_conv", "s_conv")):
                pool.dma_start(o[name][0, 0].rearrange("j (f p) -> f j p", p=P),
                               cvo[0:2 * FT, 2 * n:2 * n + 2, :]).then_inc(u_out, 16)
            pool.wait_ge(n_tok, 1)
            for n, name in enumerate(("p_n", "s_n")):
                pool.dma_start(o[name][0, 0], nrow2[0:MH, n * P:(n + 1) * P]).then_inc(a_n, 16)


INS = ["x_prompt", "x_sample", "mem_prompt", "cache_dsa_k", "cache_dsa_v", "cache_dsa_kidx", "state_mlstm_C",
       "state_mlstm_n", "state_mlstm_m", "state_ffn_conv", "cache_mem_k", "cache_mem_v", "g_mix", "w_in", "b_igate",
       "b_fgate", "w_branch", "w_out", "g_mem", "w_mem_kv", "g_ffn", "w_up", "conv_w", "conv_b", "w_down", "g_final"]
OUTS = [("y_prompt", (1, TP, D)), ("y_sample", (1, TS, D)),
        ("p_k", (1, 1, TP, 2, 128)), ("p_v", (1, 1, TP, 2, 128)), ("p_kidx", (1, 1, TP, 64)),
        ("p_C", (1, 1, MH, 128, 128)), ("p_n", (1, 1, MH, 128)), ("p_m", (1, 1, MH)),
        ("p_conv", (1, 1, 2, 2 * FF)), ("p_mem_k", (1, 1, NMEM, CHD, 256)), ("p_mem_v", (1, 1, NMEM, CHD, 256)),
        ("s_k", (1, 1, TS, 2, 128)), ("s_v", (1, 1, TS, 2, 128)), ("s_kidx", (1, 1, TS, 64)),
        ("s_C", (1, 1, MH, 128, 128)), ("s_n", (1, 1, MH, 128)), ("s_m", (1, 1, MH)),
        ("s_conv", (1, 1, 2, 2 * FF))]


def kernel(**inputs):
    import concourse.bacc as bacc
    from concourse.bass_utils import run_bass_kernel_spmd

    nc = bacc.Bacc("TRN2", target_bir_lowering=False, num_devices=1)
    arrays, a, o = {}, {}, {}
    for name in INS:
        arrays[f"in_{name}"] = np.ascontiguousarray(inputs[name])
    arrays["in_tables"] = shape_tables()
    for name in INS + ["tables"]:
        a[name] = nc.dram_tensor(f"in_{name}", arrays[f"in_{name}"].shape, F32, kind="ExternalInput").ap()
    for name, shape in OUTS:
        o[name] = nc.dram_tensor(f"out_{name}", shape, F32, kind="ExternalOutput").ap()
    layer(nc, a, o)
    r = run_bass_kernel_spmd(nc, [arrays], core_ids=[0])
    return tuple(r.results[0][f"out_{name}"] for name, _ in OUTS)
```
